# Optimizing a Trainium2 kernel written in Bass

```python
import math
import jax, jax.numpy as jnp
from jax import lax
import numpy as np

D_MODEL = 1024
BATCH = 1
SEQ = 256
DEPTH = 2

N_MEM = 256
GLA_HEADS = 4
GLA_DK = 64
GLA_DV = 128
GLA_RANK = 16
GLA_TAU = 16.0
GLA_CHUNK = 64
NSA_HEADS = 8
NSA_GROUPS = 2
NSA_DH = 64
CMP_LEN = 32
CMP_STRIDE = 16
CMP_HIDDEN = 256
SLC_LEN = 64
N_SEL = 8
WINDOW = 512
DIFF_HEADS = 8
DIFF_DH = 64
DIFF_DV = 128
XATTN_HEADS = 4
XATTN_DH = 64
D_FF = 2816
N_EXPERTS = 8
TOP_K = 2
Q_BLOCK = 128
EPS = 1e-6
NEG = -1e30
TINY = 1e-30
FORCE_SCORE = 1e4

GLA_SIZES = [GLA_HEADS * GLA_DK, GLA_HEADS * GLA_DK, GLA_HEADS * GLA_DV, GLA_HEADS * GLA_DV, GLA_RANK]
NSA_KV = NSA_GROUPS * NSA_DH
NSA_SIZES = [NSA_HEADS * NSA_DH, NSA_KV, NSA_KV, NSA_KV, NSA_KV, NSA_KV, NSA_KV, 3 * NSA_HEADS]
P0_SIZES = GLA_SIZES + NSA_SIZES
P0 = sum(P0_SIZES)
MIX0_OUT = GLA_HEADS * GLA_DV + NSA_HEADS * NSA_DH
P1_SIZES = [DIFF_HEADS * DIFF_DH] * 4 + [DIFF_HEADS * DIFF_DV]
P1 = sum(P1_SIZES)
MIX1_OUT = DIFF_HEADS * DIFF_DV

kernel_name = 'hybrid_gla_nsa_diffattn_moe'

def _split_points(sizes):
    return np.cumsum(sizes)[:-1].tolist()

def rms_norm(x, g):
    xf = x.astype(jnp.float32)
    y = xf * lax.rsqrt(jnp.mean(xf * xf, axis=-1, keepdims=True) + EPS)
    return (y * g.astype(jnp.float32)).astype(x.dtype)

def alibi_slopes(n):
    return jnp.asarray(2.0 ** (-8.0 * np.arange(1, n + 1) / n), dtype=jnp.float32)

def masked_softmax(s, mask, axis=-1):
    s = jnp.where(mask, s, NEG)
    p = jnp.exp(s - jnp.max(s, axis=axis, keepdims=True)) * mask
    return p / jnp.maximum(jnp.sum(p, axis=axis, keepdims=True), TINY)

def swiglu(h, wg, wu, wd):
    return (jax.nn.silu(h @ wg) * (h @ wu)) @ wd

def gla_mixer(q, k, v, r, a_lr, w_alpha, b_alpha, g_norm):
    B, S, _ = q.shape
    H, C = GLA_HEADS, GLA_CHUNK
    n_chunks = S // C
    f32 = jnp.float32

    def heads(t, d):
        return t.reshape(B, S, H, d).transpose(0, 2, 1, 3).astype(f32)

    log_alpha = jax.nn.log_sigmoid(heads(a_lr @ w_alpha + b_alpha, GLA_DK)) / GLA_TAU
    qh = heads(q, GLA_DK) * (GLA_DK ** -0.5)
    kh = heads(k, GLA_DK)
    vh = heads(v, GLA_DV)

    def chunks(t):
        return jnp.moveaxis(t.reshape(B, H, n_chunks, C, t.shape[-1]), 2, 0)

    causal = jnp.tril(jnp.ones((C, C), dtype=bool))[:, :, None]

    def step(state, inp):
        qc, kc, vc, gc = inp
        b = jnp.cumsum(gc, axis=2)
        o_inter = jnp.einsum('bhtk,bhkv->bhtv', qc * jnp.exp(b), state)
        rel = b[:, :, :, None, :] - b[:, :, None, :, :]
        decay = jnp.exp(jnp.where(causal, rel, -jnp.inf))
        scores = jnp.einsum('bhtk,bhsk,bhtsk->bhts', qc, kc, decay)
        o_intra = jnp.einsum('bhts,bhsv->bhtv', scores, vc)
        b_end = b[:, :, -1:, :]
        state = jnp.exp(b_end[:, :, 0, :, None]) * state + jnp.einsum('bhsk,bhsv->bhkv', kc * jnp.exp(b_end - b), vc)
        return state, o_inter + o_intra

    state0 = jnp.zeros((B, H, GLA_DK, GLA_DV), f32)
    _, o = lax.scan(step, state0, (chunks(qh), chunks(kh), chunks(vh), chunks(log_alpha)))
    o = jnp.moveaxis(o, 0, 2).reshape(B, H, S, GLA_DV)
    o = rms_norm(o, g_norm).transpose(0, 2, 1, 3).reshape(B, S, H * GLA_DV)
    return (o * jax.nn.silu(r.astype(f32))).astype(q.dtype)

def _nsa_geometry(S):
    n_cmp = (S - CMP_LEN) // CMP_STRIDE + 1
    c_start = np.arange(n_cmp) * CMP_STRIDE
    c_end = c_start + CMP_LEN - 1
    n_slc = S // SLC_LEN
    j_start = np.arange(n_slc) * SLC_LEN
    overlap = (c_end[:, None] >= j_start[None]) & (c_start[:, None] <= j_start[None] + SLC_LEN - 1)
    return n_cmp, c_start, c_end, n_slc, overlap.astype(np.float32)

def nsa_compress(t, pos_emb, w1, w2, c_start):
    idx = c_start[:, None] + np.arange(CMP_LEN)[None, :]
    blocks = t[:, :, idx] + pos_emb
    flat = blocks.reshape(blocks.shape[0], blocks.shape[1], blocks.shape[2], CMP_LEN * NSA_DH)
    return (jax.nn.gelu(flat @ w1) @ w2).astype(jnp.float32)

def nsa_mixer(q, k_cmp, v_cmp, k_slc, v_slc, k_win, v_win, gates, pos_k, w1_k, w2_k, pos_v, w1_v, w2_v):
    B, S, _ = q.shape
    G, Hg, dh = NSA_GROUPS, NSA_HEADS // NSA_GROUPS, NSA_DH
    f32 = jnp.float32
    n_cmp, c_start, c_end, n_slc, overlap = _nsa_geometry(S)
    nqb = S // Q_BLOCK
    pos = jnp.arange(S)
    slopes = alibi_slopes(NSA_HEADS).reshape(G, Hg)
    qh = q.reshape(B, S, G, Hg, dh).transpose(0, 2, 3, 1, 4).astype(f32) * (dh ** -0.5)

    def kv(t):
        return t.reshape(B, S, G, dh).transpose(0, 2, 1, 3).astype(f32)

    def q_blocks(t):
        return jnp.moveaxis(t.reshape(B, G, Hg, nqb, Q_BLOCK, dh), 3, 0)

    def unblock(t):
        return jnp.moveaxis(t, 0, 3).reshape(B, G, Hg, S, dh)

    kc = nsa_compress(kv(k_cmp), pos_k, w1_k, w2_k, c_start)
    vc = nsa_compress(kv(v_cmp), pos_v, w1_v, w2_v, c_start)
    dist_c = pos[:, None] - jnp.asarray(c_end)[None, :]
    s_c = jnp.einsum('bghtd,bgcd->bghtc', qh, kc) - slopes[None, :, :, None, None] * dist_c
    p_c = masked_softmax(s_c, dist_c >= 0)
    o_cmp = jnp.einsum('bghtc,bgcd->bghtd', p_c, vc)

    imp = jnp.einsum('bghtc,cj->bgtj', p_c, jnp.asarray(overlap))
    blk = jnp.arange(n_slc)
    cur = pos // SLC_LEN
    forced = (blk[None, :] == cur[:, None]) | (blk[None, :] == 0)
    valid = blk[None, :] <= cur[:, None]
    score = jnp.where(forced, FORCE_SCORE, jnp.where(valid, imp, NEG))
    _, sel = lax.top_k(score, min(N_SEL, n_slc))
    ks = kv(k_slc).reshape(B, G, n_slc, SLC_LEN, dh)
    vs = kv(v_slc).reshape(B, G, n_slc, SLC_LEN, dh)
    b_ix = jnp.arange(B)[:, None, None, None]
    g_ix = jnp.arange(G)[None, :, None, None]
    sel_b = jnp.moveaxis(sel.reshape(B, G, nqb, Q_BLOCK, sel.shape[-1]), 2, 0)
    pos_b = pos.reshape(nqb, Q_BLOCK)

    def slc_block(args):
        qb, ib, tq = args
        kg = ks[b_ix, g_ix, ib]
        vg = vs[b_ix, g_ix, ib]
        key_pos = ib[..., None] * SLC_LEN + jnp.arange(SLC_LEN)
        dist = tq[None, None, :, None, None] - key_pos
        s = jnp.einsum('bghtd,bgtkld->bghtkl', qb, kg) - slopes[None, :, :, None, None, None] * dist[:, :, None]
        p = masked_softmax(s, (dist >= 0)[:, :, None], axis=(-2, -1))
        return jnp.einsum('bghtkl,bgtkld->bghtd', p, vg)

    o_slc = unblock(lax.map(slc_block, (q_blocks(qh), sel_b, pos_b)))

    kw = jnp.pad(kv(k_win), ((0, 0), (0, 0), (WINDOW, 0), (0, 0)))
    vw = jnp.pad(kv(v_win), ((0, 0), (0, 0), (WINDOW, 0), (0, 0)))
    span = WINDOW + Q_BLOCK

    def win_block(args):
        qb, start = args
        kb = lax.dynamic_slice_in_dim(kw, start, span, axis=2)
        vb = lax.dynamic_slice_in_dim(vw, start, span, axis=2)
        tq = start + jnp.arange(Q_BLOCK)
        ts = start - WINDOW + jnp.arange(span)
        dist = tq[:, None] - ts[None, :]
        mask = (dist >= 0) & (dist < WINDOW) & (ts[None, :] >= 0)
        s = jnp.einsum('bghtd,bgsd->bghts', qb, kb) - slopes[None, :, :, None, None] * dist
        p = masked_softmax(s, mask)
        return jnp.einsum('bghts,bgsd->bghtd', p, vb)

    o_win = unblock(lax.map(win_block, (q_blocks(qh), jnp.arange(nqb) * Q_BLOCK)))

    g = jax.nn.sigmoid(gates.astype(f32)).reshape(B, S, G, Hg, 3).transpose(0, 2, 3, 1, 4)
    o = g[..., 0:1] * o_cmp + g[..., 1:2] * o_slc + g[..., 2:3] * o_win
    return o.transpose(0, 3, 1, 2, 4).reshape(B, S, NSA_HEADS * dh).astype(q.dtype)

def diff_mixer(q1, q2, k1, k2, v, lq1, lk1, lq2, lk2, g_norm, lambda_init):
    B, S, _ = q1.shape
    H = DIFF_HEADS
    f32 = jnp.float32
    nqb = S // Q_BLOCK

    def heads(t, d):
        return t.reshape(B, S, H, d).transpose(0, 2, 1, 3).astype(f32)

    q = jnp.stack([heads(q1, DIFF_DH), heads(q2, DIFF_DH)], axis=2) * (DIFF_DH ** -0.5)
    k = jnp.stack([heads(k1, DIFF_DH), heads(k2, DIFF_DH)], axis=2)
    vh = heads(v, DIFF_DV)
    lam = (jnp.exp(jnp.sum(lq1.astype(f32) * lk1.astype(f32))) - jnp.exp(jnp.sum(lq2.astype(f32) * lk2.astype(f32))) + lambda_init)
    slopes = alibi_slopes(H)
    kpos = jnp.arange(S)
    qb_all = jnp.moveaxis(q.reshape(B, H, 2, nqb, Q_BLOCK, DIFF_DH), 3, 0)

    def block(args):
        qb, tq = args
        dist = tq[:, None] - kpos[None, :]
        s = jnp.einsum('bhiqd,bhisd->bhiqs', qb, k) - slopes[None, :, None, None, None] * dist
        p = masked_softmax(s, dist >= 0)
        return jnp.einsum('bhqs,bhsd->bhqd', p[:, :, 0] - lam * p[:, :, 1], vh)

    o = lax.map(block, (qb_all, kpos.reshape(nqb, Q_BLOCK)))
    o = jnp.moveaxis(o, 0, 2).reshape(B, H, S, DIFF_DV)
    o = rms_norm(o, g_norm) * (1.0 - lambda_init)
    return o.transpose(0, 2, 1, 3).reshape(B, S, H * DIFF_DV).astype(q1.dtype)

def memory_cross_attention(h, mem_n, wq, wk, wv, wo):
    B, S, _ = h.shape
    M = mem_n.shape[1]
    q = (h @ wq).reshape(B, S, XATTN_HEADS, XATTN_DH)
    k = (mem_n @ wk).reshape(B, M, XATTN_HEADS, XATTN_DH)
    v = (mem_n @ wv).reshape(B, M, XATTN_HEADS, XATTN_DH)
    s = jnp.einsum('bthd,bmhd->bhtm', q, k).astype(jnp.float32) * (XATTN_DH ** -0.5)
    p = jax.nn.softmax(s, axis=-1).astype(v.dtype)
    o = jnp.einsum('bhtm,bmhd->bthd', p, v).reshape(B, S, XATTN_HEADS * XATTN_DH)
    return o @ wo

def moe_swiglu(h, w_router, wg, wu, wd):
    B, S, D = h.shape
    t = h.reshape(B * S, D)
    logits = (t @ w_router).astype(jnp.float32)
    top_v, top_i = lax.top_k(logits, TOP_K)
    w = jax.nn.softmax(top_v, axis=-1)
    combine = jnp.sum(jax.nn.one_hot(top_i, N_EXPERTS, dtype=jnp.float32) * w[..., None], axis=1)
    y = jnp.zeros((B * S, D), jnp.float32)
    for e in range(N_EXPERTS):
        y = y + combine[:, e:e + 1] * swiglu(t, wg[e], wu[e], wd[e]).astype(jnp.float32)
    return y.reshape(B, S, D).astype(h.dtype)

def even_layer(x, mem, mix_norm, w_in, gla_w_alpha, gla_b_alpha, gla_out_norm, nsa_cmp_pos_k, nsa_cmp_w1_k, nsa_cmp_w2_k, nsa_cmp_pos_v, nsa_cmp_w1_v, nsa_cmp_w2_v, w_out, xattn_norm, xattn_mem_norm, xattn_wq, xattn_wk, xattn_wv, xattn_wo, ffn_norm, ffn_w_gate, ffn_w_up, ffn_w_down):
    h = rms_norm(x, mix_norm) @ w_in
    (g_q, g_k, g_v, g_r, g_a, n_q, n_kc, n_vc, n_ks, n_vs, n_kw, n_vw, n_g) = jnp.split(h, _split_points(P0_SIZES), axis=-1)
    o_a = gla_mixer(g_q, g_k, g_v, g_r, g_a, gla_w_alpha, gla_b_alpha, gla_out_norm)
    o_b = nsa_mixer(n_q, n_kc, n_vc, n_ks, n_vs, n_kw, n_vw, n_g, nsa_cmp_pos_k, nsa_cmp_w1_k, nsa_cmp_w2_k, nsa_cmp_pos_v, nsa_cmp_w1_v, nsa_cmp_w2_v)
    x = x + jnp.concatenate([o_a, o_b], axis=-1) @ w_out
    x = x + memory_cross_attention(rms_norm(x, xattn_norm), rms_norm(mem, xattn_mem_norm), xattn_wq, xattn_wk, xattn_wv, xattn_wo)
    x = x + swiglu(rms_norm(x, ffn_norm), ffn_w_gate, ffn_w_up, ffn_w_down)
    return x

def odd_layer(x, mem, layer_idx, mix_norm, w_in, diff_lq1, diff_lk1, diff_lq2, diff_lk2, diff_out_norm, w_out, xattn_norm, xattn_mem_norm, xattn_wq, xattn_wk, xattn_wv, xattn_wo, ffn_norm, moe_router, moe_w_gate, moe_w_up, moe_w_down):
    lambda_init = 0.8 - 0.6 * math.exp(-0.3 * layer_idx)
    h = rms_norm(x, mix_norm) @ w_in
    q1, q2, k1, k2, v = jnp.split(h, _split_points(P1_SIZES), axis=-1)
    x = x + diff_mixer(q1, q2, k1, k2, v, diff_lq1, diff_lk1, diff_lq2, diff_lk2, diff_out_norm, lambda_init) @ w_out
    x = x + memory_cross_attention(rms_norm(x, xattn_norm), rms_norm(mem, xattn_mem_norm), xattn_wq, xattn_wk, xattn_wv, xattn_wo)
    x = x + moe_swiglu(rms_norm(x, ffn_norm), moe_router, moe_w_gate, moe_w_up, moe_w_down)
    return x

def setup_inputs(seed: int = 0) -> dict:
    key = jax.random.key(seed)
    ks = iter(jax.random.split(key, 64))
    f32 = jnp.float32

    def nrm(shape, scale):
        return jax.random.normal(next(ks), shape, f32) * scale

    def gain(n):
        return 1.0 + 0.02 * jax.random.normal(next(ks), (n,), f32)

    D = D_MODEL
    XW = XATTN_HEADS * XATTN_DH
    inp = {}
    inp['x'] = nrm((BATCH, SEQ, D), 1.0)
    inp['mem'] = nrm((BATCH, N_MEM, D), 1.0)
    inp['mix_norm_0'] = gain(D)
    inp['w_in_0'] = nrm((D, P0), D ** -0.5)
    inp['gla_w_alpha_0'] = nrm((GLA_RANK, GLA_HEADS * GLA_DK), GLA_RANK ** -0.5)
    inp['gla_b_alpha_0'] = nrm((GLA_HEADS * GLA_DK,), 0.01)
    inp['gla_out_norm_0'] = gain(GLA_DV)
    inp['nsa_cmp_pos_k_0'] = nrm((CMP_LEN, NSA_DH), 0.02)
    inp['nsa_cmp_w1_k_0'] = nrm((CMP_LEN * NSA_DH, CMP_HIDDEN), (CMP_LEN * NSA_DH) ** -0.5)
    inp['nsa_cmp_w2_k_0'] = nrm((CMP_HIDDEN, NSA_DH), CMP_HIDDEN ** -0.5)
    inp['nsa_cmp_pos_v_0'] = nrm((CMP_LEN, NSA_DH), 0.02)
    inp['nsa_cmp_w1_v_0'] = nrm((CMP_LEN * NSA_DH, CMP_HIDDEN), (CMP_LEN * NSA_DH) ** -0.5)
    inp['nsa_cmp_w2_v_0'] = nrm((CMP_HIDDEN, NSA_DH), CMP_HIDDEN ** -0.5)
    inp['w_out_0'] = nrm((MIX0_OUT, D), MIX0_OUT ** -0.5)
    inp['xattn_norm_0'] = gain(D)
    inp['xattn_mem_norm_0'] = gain(D)
    inp['xattn_wq_0'] = nrm((D, XW), D ** -0.5)
    inp['xattn_wk_0'] = nrm((D, XW), D ** -0.5)
    inp['xattn_wv_0'] = nrm((D, XW), D ** -0.5)
    inp['xattn_wo_0'] = nrm((XW, D), XW ** -0.5)
    inp['ffn_norm_0'] = gain(D)
    inp['ffn_w_gate_0'] = nrm((D, D_FF), D ** -0.5)
    inp['ffn_w_up_0'] = nrm((D, D_FF), D ** -0.5)
    inp['ffn_w_down_0'] = nrm((D_FF, D), D_FF ** -0.5)
    inp['mix_norm_1'] = gain(D)
    inp['w_in_1'] = nrm((D, P1), D ** -0.5)
    inp['diff_lq1_1'] = nrm((DIFF_DH,), 0.1)
    inp['diff_lk1_1'] = nrm((DIFF_DH,), 0.1)
    inp['diff_lq2_1'] = nrm((DIFF_DH,), 0.1)
    inp['diff_lk2_1'] = nrm((DIFF_DH,), 0.1)
    inp['diff_out_norm_1'] = gain(DIFF_DV)
    inp['w_out_1'] = nrm((MIX1_OUT, D), MIX1_OUT ** -0.5)
    inp['xattn_norm_1'] = gain(D)
    inp['xattn_mem_norm_1'] = gain(D)
    inp['xattn_wq_1'] = nrm((D, XW), D ** -0.5)
    inp['xattn_wk_1'] = nrm((D, XW), D ** -0.5)
    inp['xattn_wv_1'] = nrm((D, XW), D ** -0.5)
    inp['xattn_wo_1'] = nrm((XW, D), XW ** -0.5)
    inp['ffn_norm_1'] = gain(D)
    inp['moe_router_1'] = nrm((D, N_EXPERTS), D ** -0.5)
    inp['moe_w_gate_1'] = nrm((N_EXPERTS, D, D_FF), D ** -0.5)
    inp['moe_w_up_1'] = nrm((N_EXPERTS, D, D_FF), D ** -0.5)
    inp['moe_w_down_1'] = nrm((N_EXPERTS, D_FF, D), D_FF ** -0.5)
    inp['final_norm'] = gain(D)
    return inp

def reference(x, mem, mix_norm_0, w_in_0, gla_w_alpha_0, gla_b_alpha_0, gla_out_norm_0, nsa_cmp_pos_k_0, nsa_cmp_w1_k_0, nsa_cmp_w2_k_0, nsa_cmp_pos_v_0, nsa_cmp_w1_v_0, nsa_cmp_w2_v_0, w_out_0, xattn_norm_0, xattn_mem_norm_0, xattn_wq_0, xattn_wk_0, xattn_wv_0, xattn_wo_0, ffn_norm_0, ffn_w_gate_0, ffn_w_up_0, ffn_w_down_0, mix_norm_1, w_in_1, diff_lq1_1, diff_lk1_1, diff_lq2_1, diff_lk2_1, diff_out_norm_1, w_out_1, xattn_norm_1, xattn_mem_norm_1, xattn_wq_1, xattn_wk_1, xattn_wv_1, xattn_wo_1, ffn_norm_1, moe_router_1, moe_w_gate_1, moe_w_up_1, moe_w_down_1, final_norm):
    layer_params = (
        (mix_norm_0, w_in_0, gla_w_alpha_0, gla_b_alpha_0, gla_out_norm_0, nsa_cmp_pos_k_0, nsa_cmp_w1_k_0, nsa_cmp_w2_k_0, nsa_cmp_pos_v_0, nsa_cmp_w1_v_0, nsa_cmp_w2_v_0, w_out_0, xattn_norm_0, xattn_mem_norm_0, xattn_wq_0, xattn_wk_0, xattn_wv_0, xattn_wo_0, ffn_norm_0, ffn_w_gate_0, ffn_w_up_0, ffn_w_down_0),
        (mix_norm_1, w_in_1, diff_lq1_1, diff_lk1_1, diff_lq2_1, diff_lk2_1, diff_out_norm_1, w_out_1, xattn_norm_1, xattn_mem_norm_1, xattn_wq_1, xattn_wk_1, xattn_wv_1, xattn_wo_1, ffn_norm_1, moe_router_1, moe_w_gate_1, moe_w_up_1, moe_w_down_1),
    )
    h = x
    for layer in range(DEPTH):
        p = layer_params[layer]
        if layer % 2 == 0:
            h = even_layer(h, mem, *p)
        else:
            h = odd_layer(h, mem, layer, *p)
    return rms_norm(h, final_norm)


_drawn_inputs = setup_inputs


def setup_inputs(seed=0):
    import zlib

    import numpy as np

    out = dict(_drawn_inputs(seed))
    spreads = {}
    factors = {'gla_b_alpha_0': 8.0,
     'nsa_cmp_pos_k_0': 8.0,
     'nsa_cmp_pos_v_0': 8.0,
     'xattn_norm_0': 8.0,
     'xattn_mem_norm_0': 3.729,
     'diff_out_norm_1': 5.831,
     'xattn_norm_1': 8.0,
     'xattn_mem_norm_1': 5.604,
     'final_norm': 8.031,
     'ffn_norm_1': 8.0}
    for name, (base, spread) in spreads.items():
        noise = np.random.default_rng([zlib.crc32(name.encode()), seed]).standard_normal(out[name].shape)
        drawn = base * np.exp(spread * noise) if base else spread * noise
        out[name] = __import__('jax').numpy.asarray(drawn.astype(out[name].dtype))
    for name, factor in factors.items():
        out[name] = (out[name] * factor).astype(out[name].dtype)
    return out
```

```python
import math
from contextlib import ExitStack

import concourse.bass as bass
from concourse import mybir

F32 = mybir.dt.float32
F32R = mybir.dt.float32r
I32 = mybir.dt.int32
U8 = mybir.dt.uint8
ALU = mybir.AluOpType
ACT = mybir.ActivationFunctionType
AX = mybir.AxisListType.X

P = 128
D = 1024
DC = D // P
TT = 2
EPS = 1e-6
NEG = -1e30
TINY = 1e-30
SLOPES = [2.0 ** -(h + 1) for h in range(8)]
UPTO = 6
LAMBDA_INIT = 0.8 - 0.6 * math.exp(-0.3 * 1)
FF = 2816
FU = [512] * 5 + [256]
NE = 8
CMP = 15
RING = 11
CONV = 3
W0 = dict(q=0, k=256, v=512, r=1024, a=1536, nq=1552, kc=2064, vc=2192, ks=2320, vs=2448, kw=2576, vw=2704,
          g=2832, end=2856)
CV = dict(mix0=0, xat0=8, xmem0=16, ffn0=24, mix1=32, xat1=40, xmem1=48, ffn1=56, posk=64, posv=80,
          balpha=96, glan=98, diffn=99, rows=100)

OUTS = (["ct"] + [f"memT{j}" for j in range(4)]
        + [f"{w}{l}{j}" for l in range(2) for w in ("km", "vm") for j in range(2)]
        + [f"h0_{j}" for j in range(4)]
        + ["a", "nq0", "nq1", "nq2", "nq3", "kc", "vc", "ks", "vs0", "vs1", "kw", "vw0", "vw1", "g0", "g1"]
        + ["gq0", "gq1", "gk0", "gk1", "gv0", "gv1", "gr0", "gr1", "z0", "z1"]
        + ["ck", "cv", "c2k", "c2v", "sc", "pct0", "pct1", "pct2", "pct3"]
        + [f"n{t}{hp}" for t in range(2) for hp in range(4)]
        + ["og0", "og1", "ogT0", "ogT1"]
        + [f"y{j}" for j in range(4)]
        + [f"h1_{j}" for j in range(4)] + ["xq0_0", "xq0_1"] + [f"xo0_{j}" for j in range(4)] + [f"xy0_{j}" for j in range(4)]
        + [f"h2_{j}" for j in range(4)]
        + [f"h3_{j}" for j in range(4)]
        + [f"d{w}{2 * hf + j}" for hf in range(2) for w in ("q1", "q2", "k1", "k2") for j in range(2)]
        + ["dv00", "dv10", "dv01", "dv11", "lam"]
        + [f"od{t}{hq}" for t in range(2) for hq in range(2)] + [f"odT{t}{hq}" for t in range(2) for hq in range(2)]
        + [f"dy{j}" for j in range(4)]
        + [f"h4_{j}" for j in range(4)] + ["xq1_0", "xq1_1"] + [f"xo1_{j}" for j in range(4)] + [f"xy1_{j}" for j in range(4)]
        + [f"h5_{j}" for j in range(4)] + ["lg", "rk", "gb0", "gb1"])
IDX = {n: i for i, n in enumerate(OUTS)}
assert len(IDX) == len(OUTS)

U_NSA, U_X0, U_D, U_X1 = 0, 16, 20, 36
FFN0_LOAD = 26
MOE_LOAD = 77


def ffn_order(first):
    lag = 1 if first else 2
    order = []
    for u in range(6 + lag):
        if u < 6:
            for kind in "ug":
                order += [(kind, u, h) for h in range(2 if u < 5 else 1)]
        if u >= lag:
            order += [("d", u - lag, h) for h in range(2 if u - lag < 5 else 1)]
    return order


ORDER0 = ffn_order(True)
ORDERM = ffn_order(False)
AT0 = {k: n for n, k in enumerate(ORDER0)}
ATM = {k: n for n, k in enumerate(ORDERM)}
assert len(ORDER0) == len(ORDERM) == 33 and (MOE_LOAD % RING, 33 % RING, 33 % CONV) == (0, 0, 0)


def build(nc, a, out, upto):
    ctx = ExitStack()
    with ctx:
        TOTAL = 207 * 1024 + 512
        arena_start = (nc.sbuf_base + 31) // 32 * 32
        arena = ctx.enter_context(nc.sbuf_tensor("arena", [P, TOTAL // 4], F32))
        base = arena_start

        def size(shape, dt=F32):
            n = 1 if dt == U8 else 4
            for s in shape[1:]:
                n *= s
            return (n + 31) // 32 * 32

        def region(start):
            def put(name, shape, dt=F32):
                off = put.pos
                put.pos += size(shape, dt)
                return nc.alloc_sbuf_tensor_at(name, shape, dt, offset=off)
            put.pos = start
            return put

        def sem(name):
            return ctx.enter_context(nc.semaphore(name))

        sb = region(base)
        ring = [sb(f"ring{i}", [P, 2048]) for i in range(RING)]
        conv_base = sb.pos
        hi = [sb(f"whi{i}", [P, 2048], F32R) for i in range(CONV)]
        lo = [sb(f"wlo{i}", [P, 2048], F32R) for i in range(CONV)]
        conv_end = sb.pos
        X = sb("X", [P, TT, D])
        xn_base = sb.pos
        XN = sb("XN", [P, TT, D])
        ht_base = sb.pos
        HT = sb("HT", [P, DC, 256])
        ident = sb("ident", [P, P])
        CT = sb("CT", [P, CV["rows"]])
        small = sb("small", [P, 64])
        U_strict = sb("U_strict", [P, P])
        ones = sb("ones", [P, P])
        halfneg = sb("halfneg", [P, 8])
        WR = sb("WR", [P, DC, NE])
        WA = sb("WA", [16, 256])
        ATa = sb("ATa", [16, 256])
        W2 = [sb(f"W2{w}", [P, 2, 64]) for w in "kv"]
        CM = sb("CM", [P, TT, 16])
        lrow = sb("lrow", [1, 4, 64])
        CX = sb("CX", [P, 32])
        rstd = sb("rstd", [P, 8])
        ot_base = sb.pos
        OT = sb("OT", [P, DC, 256])
        MK = sb("MK", [P, 8, P], U8)
        TP = [sb(f"TP{i}", [P, 2, 256]) for i in range(3)]
        PT = [sb(f"PT{i}", [P, 2, 2, P]) for i in range(4)]
        nb_base = sb.pos
        NB = sb("NB", [P, 8, 256])
        KM = [sb(f"KM{l}", [P, 2, 256]) for l in range(2)]
        VM = [sb(f"VM{l}", [P, 2, 256]) for l in range(2)]
        end = sb.pos
        assert end - base <= TOTAL, (end - base, TOTAL)
        l0 = region(conv_base)
        QG, KG, LA, BG, EL1 = (l0(n, [P, 2, 256]) for n in ("QG", "KG", "LA", "BG", "EL1"))
        EL = [LA, EL1]
        VG, SR = (l0(n, [P, TT, 512]) for n in ("VG", "SR"))
        NQ = l0("NQ", [P, 4, 256])
        KS, KW = (l0(n, [P, 2, 256]) for n in ("KS", "KW"))
        VS, VW = (l0(n, [P, TT, P]) for n in ("VS", "VW"))
        r1 = region(l0.pos)
        T2 = [l0(f"T2{w}", [P, 2, 256]) for w in "kv"]
        QL = [r1(f"QL{i}", [P, 2, 256]) for i in range(2)]
        l0.pos = r1.pos
        RR = [l0(f"RR{w}", [P, 16, 2, CMP]) for w in "kv"]
        KL = [r1(f"KL{i}", [P, 2, 256]) for i in range(2)]
        l0.pos = r1.pos
        r2 = region(l0.pos)
        PCT = l0("PCT", [CMP, 16, P])
        PG = [r2(f"PG{i}", [P, 4, P]) for i in range(3)]
        GH = [l0(f"GH{w}", [P, 2, 2 * CMP]) for w in "kv"]
        KC = l0("KC", [P, 2 * CMP])
        VC = l0("VC", [CMP, 2, 64])
        GT = l0("GT", [P, TT, 24])
        PCC = l0("PCC", [P, 16, 16])
        CB = l0("CB", [P, 16, 16])
        assert l0.pos <= conv_end, (l0.pos - conv_end)
        li = region(conv_base)
        IOn = li("IOn", [P, 256], I32)
        IOc = li("IOc", [P, TT, 16], I32)
        IOs, IOt, IOx, IOy = (li(n, [P, P], I32) for n in ("IOs", "IOt", "IOx", "IOy"))
        MKf = li("MKf", [P, 8, P])
        QX = region(conv_base)("QX", [P, 2, 256])
        l1 = region(conv_base)
        QD = l1("QD", [P, 2, 4, 256])
        KD = l1("KD", [P, 2, 4, 256])
        VD = l1("VD", [P, TT, D])
        OD = l1("OD", [P, TT, D])
        SQ = l1("SQ", [P, D])
        grow = l1("grow", [1, 2, D])
        assert l1.pos <= conv_end
        f0 = region(ot_base)
        AB = [f0(f"AB{i}", [P, 512]) for i in range(2)]
        ATH = [f0(f"ATH{i}", [P, 4, P], F32R) for i in range(2)]
        ATL = [f0(f"ATL{i}", [P, 4, P], F32R) for i in range(2)]
        f1 = region(f0.pos)
        HTL = f1("HTL", [P, DC, 256], F32R)
        assert f1.pos <= nb_base
        XGH = region(ht_base)("XGH", [P, TT, D], F32R)
        XGL = region(xn_base)("XGL", [P, TT, D], F32R)
        HTH = region(xn_base)("HTH", [P, DC, 256], F32R)
        HGH = f0("HGH", [P, DC, P], F32R)
        HGL = f0("HGL", [P, DC, P], F32R)
        YEH = f0("YEH", [P, D], F32R)
        YEL = f0("YEL", [P, D], F32R)
        SEL = f0("SEL", [P, TT, P])
        SELR = f0("SELR", [P, TT, P], F32R)
        SELT = f0("SELT", [P, TT, P], F32R)
        FG = f0("FG", [P, D])
        POS = f0("POS", [P, 17, TT])
        COMB = f0("COMB", [P, 17, TT])
        CBI = f0("CBI", [P, TT])
        PSI = f0("PSI", [P, TT])
        LG, O1, O2, RA, RB = (f0(n, [P, TT, NE]) for n in ("LG", "O1", "O2", "RA", "RB"))
        iota_e = f0("iota_e", [P, TT, NE])
        iota_s = f0("iota_s", [P, P])
        WS = f0("WS", [P, 1])
        flag = f0("flag", [P, 1], I32)
        IOe = f0("IOe", [P, TT, NE], I32)
        IOf = f0("IOf", [P, P], I32)
        assert f0.pos <= end

        bank = [ctx.enter_context(nc.psum_tensor(f"bank{i}", [P, 512], F32)) for i in range(8)]

        landed = [sem(f"landed{i}") for i in range(RING)]
        slot_free = [sem(f"slot_free{i}") for i in range(RING)]
        bank_full = [sem(f"bank_full{i}") for i in range(4)]
        bank_free = [sem(f"bank_free{i}") for i in range(4)]
        x_in, mem_in, sv_in, small_in, grow_in, out_done = (
            sem(n) for n in ("x_in", "mem_in", "sv_in", "small_in", "grow_in", "out_done"))
        ident_ready, pool_const, nb_ready, mk_ready, pg_zero = (sem(n) for n in ("ident_ready", "pool_const", "nb_ready", "mk_ready", "pg_zero"))
        dve_const = sem("dve_const")
        pool_chain, dve_chain, act_chain, row_order = (sem(n) for n in ("pool_chain", "dve_chain", "act_chain", "row_order"))
        ss_ready, ms_ready, rstd_ready, xn_ready = (sem(n) for n in ("ss_ready", "ms_ready", "rstd_ready", "xn_ready"))
        act_ev, dve_ev = sem("act_ev"), sem("dve_ev")
        s_full, s_used, nm_ready, exp_done, p_ready, pt_full, pt_ready, pv_done = (
            sem(n) for n in ("s_full", "s_used", "nm_ready", "exp_done", "p_ready", "pt_full", "pt_ready", "pv_done"))
        r_ready, gh_ready, pc_ready = sem("r_ready"), sem("gh_ready"), sem("pc_ready")
        z_ready, e_ready, l_ready, b_ready, d_ready, el_ready, ql_ready, kl_ready, gl_full, gl_used = (
            sem(n) for n in ("z_ready", "e_ready", "l_ready", "b_ready", "d_ready", "el_ready", "ql_ready", "kl_ready", "gl_full", "gl_used"))
        pc_t, pc_e = sem("pc_t"), sem("pc_e")
        pg_done, ogm, ogr, ogs, lams = sem("pg_done"), sem("ogm"), sem("ogr"), sem("ogs"), sem("lams")
        er_ready = sem("er_ready")
        odm, odr, ods, odq = sem("odm"), sem("odr"), sem("ods"), sem("odq")
        hi_ready, lo_ready, conv_used = sem("hi_ready"), sem("lo_ready"), sem("conv_used")
        f_full, f_e, f_a, f_t, f_th, f_tl, f_y = (sem(n) for n in ("f_full", "f_e", "f_a", "f_t", "f_th", "f_tl", "f_y"))
        hth, htl = sem("hth"), sem("htl")
        m_full, m_e, m_a, m_t, m_th, m_tl = (sem(n) for n in ("m_full", "m_e", "m_a", "m_t", "m_th", "m_tl"))
        m_y, m_ye, m_yl, sc_full, sc_add, st_full, st_done, ga_full, hgh, hgl, sel_ready = (
            sem(n) for n in ("m_y", "m_ye", "m_yl", "sc_full", "sc_add", "st_full", "st_done", "ga_full", "hgh", "hgl", "sel_ready"))
        r_e, ch_ready, flag_ready, m_init, xg_ready, fin_ready, x_ready = (
            sem(n) for n in ("r_e", "ch_ready", "flag_ready", "m_init", "xg_ready", "fin_ready", "x_ready"))

        class Chain:

            def __init__(self, eng, s):
                self.eng, self.s, self.n, self.it, self.per = eng, s, 0, None, 0

            def link(self, ins):
                self.n += 1
                ins.then_inc(self.s, 1)
                self.eng.wait_ge(self.s, self.n if self.it is None else self.it * self.per + self.n)

            def loop(self, it, per):
                self.it, self.per, self.start = it, per, self.n

            def loop_end(self):
                assert self.n - self.start == self.per, (self.n - self.start, self.per)
                self.it = None

        def wcols(w, c0, c1, r0=0, r1=D):
            return w[r0:r1, c0:c1].rearrange("(c p) n -> p c n", p=P)

        def slot(n, c, w):
            return ring[n % RING][:, 0:c * w].rearrange("p (c n) -> p c n", c=c)

        loads = []
        for l in range(2):
            loads += [(wcols(a[f"xattn_wk_{l}"], 0, 256), 8, 256), (wcols(a[f"xattn_wv_{l}"], 0, 256), 8, 256)]
        w_in0 = a["w_in_0"]
        NSA_CUT = [W0["a"], W0["nq"] + 128, W0["nq"] + 384, W0["vc"], W0["vs"], W0["vw"], W0["end"]]
        for c0, c1 in zip(NSA_CUT, NSA_CUT[1:]):
            loads.append((wcols(w_in0, c0, c1), 8, c1 - c0))
        loads += [(wcols(w_in0, 0, 256), 8, 256), (wcols(w_in0, 256, 512), 8, 256)]
        for c in ("v", "r"):
            loads += [(wcols(w_in0, W0[c], W0[c] + 512, 512 * h, 512 * h + 512), 4, 512) for h in range(2)]
        for w in "kv":
            loads += [(wcols(a[f"nsa_cmp_w1_{w}_0"], 0, 256, 1024 * h, 1024 * h + 1024), 8, 256) for h in range(2)]
        loads += [(wcols(a["w_out_0"], 0, D, 256 * j, 256 * j + 256), 2, D) for j in range(4)]
        loads += [(wcols(a["xattn_wq_0"], 0, 256), 8, 256), (wcols(a["xattn_wo_0"], 0, D, 0, 256), 2, D)]
        assert len(loads) == FFN0_LOAD

        def ffn_load(kind, u, h, wg, wu, wd):
            c0, n = 512 * u, FU[u]
            if kind == "d":
                return wd[c0 + 256 * h:c0 + 256 * h + 256, :], 2, D
            w = wg if kind == "g" else wu
            if n == 512:
                return w[512 * h:512 * h + 512, c0:c0 + n], 4, 512
            return w[:, c0:c0 + n], 8, 256

        for k in ORDER0:
            src, c, w = ffn_load(*k, a["ffn_w_gate_0"], a["ffn_w_up_0"], a["ffn_w_down_0"])
            loads.append((src.rearrange("(c p) n -> p c n", p=P), c, w))
        DIFF_LOAD = len(loads)
        for hf in range(2):
            for w in range(4):
                loads.append((wcols(a["w_in_1"], 512 * w + 256 * hf, 512 * w + 256 * hf + 256), 8, 256))
        for half in range(2):
            for h in range(2):
                loads.append((wcols(a["w_in_1"], 2048 + 512 * half, 2560 + 512 * half, 512 * h, 512 * h + 512), 4, 512))
        loads += [(wcols(a["w_out_1"], 0, D, 256 * j, 256 * j + 256), 2, D) for j in range(4)]
        loads += [(wcols(a["xattn_wq_1"], 0, 256), 8, 256), (wcols(a["xattn_wo_1"], 0, D, 0, 256), 2, D)]
        assert len(loads) == MOE_LOAD

        def wait_landed(eng, n):
            eng.wait_ge(landed[n % RING], 16 * (n // RING + 1))

        def wait_full(eng, name):
            o = IDX[name]
            eng.wait_ge(bank_full[o % 4], o // 4 + 1)
            return bank[o % 4]

        def freed(ins, name):
            ins.then_inc(bank_free[IDX[name] % 4], 1)

        X_dram = a["x"].rearrange("b (t p) d -> p (b t) d", p=P)
        M_dram = a["mem"].rearrange("b (t p) d -> p (b t) d", p=P)
        O_dram = out.rearrange("b (t p) d -> p (b t) d", p=P)
        STOP = upto
        sv = TP[0][0:CV["rows"], 0, 0:P]
        block = ctx.enter_context(nc.Block())

        LAST = {0: "km01", 1: "vm01", 2: "km11", 3: "vm11", 4: "nq0", 5: "nq2", 6: "kc", 7: "ks", 8: "kw", 9: "g1",
                10: "gq1", 11: "gk1", 12: "gv1", 13: "gv1", 14: "gr1", 15: "gr1", 16: "ck", 17: "ck", 18: "cv", 19: "cv",
                20: "y3", 21: "y3", 22: "y3", 23: "y3", 24: "xq0_1", 25: "xy0_3"}
        for hf in range(2):
            for w, name in enumerate(("q1", "q2", "k1", "k2")):
                LAST[DIFF_LOAD + 4 * hf + w] = f"d{name}{2 * hf + 1}"
        for j in range(4):
            LAST[DIFF_LOAD + 8 + j] = ("dv10", "dv11")[j // 2]
            LAST[DIFF_LOAD + 12 + j] = "dy3"
        LAST[DIFF_LOAD + 16], LAST[DIFF_LOAD + 17] = "xq1_1", "xy1_3"

        def attn_pv_group(u):
            if u < U_X0:
                return f"n{u // 8}{u // 2 % 4}", u % 2 == 1
            if u < U_D:
                return f"xo0_{u - U_X0}", True
            if u < U_X1:
                return f"od{(u - U_D) // 8}{(u - U_D) // 4 % 2}", (u - U_D) % 4 == 3
            return f"xo1_{u - U_X1}", True

        PV_COUNT = [sum(not attn_pv_group(k)[1] for k in range(u + 1)) for u in range(40)]

        def wait_pv(eng, u):
            name, last = attn_pv_group(u)
            if last:
                wait_full(eng, name)
            else:
                eng.wait_ge(pv_done, PV_COUNT[u])

        def from_psum(u):
            return U_X0 <= u < U_D or u >= U_X1

        S_USED = [sum(not from_psum(k) for k in range(u + 1)) for u in range(40)]

        def width(u):
            if u < U_X0:
                return (P, 256)[u // 8]
            if U_D <= u < U_X1:
                return (P, 256)[(u - U_D) // 8]
            return 256

        @block.sync
        def _(sp):
            sp.dma_start(XN[:, :, :], M_dram).then_inc(mem_in, 16)
            sp.dma_start(X[:, :, :], X_dram).then_inc(x_in, 16)
            for n, (src, c, w) in enumerate(loads):
                if n >= RING:
                    m = n - RING
                    if m in LAST:
                        wait_full(sp, LAST[m])
                    else:
                        sp.wait_ge(lo_ready, m - FFN0_LOAD + 1)
                sp.dma_start(slot(n, c, w), src).then_inc(landed[n % RING], 16)
                if STOP <= 3 and n == (23, 25, 58, 74)[STOP]:
                    break

            def expert_loads(i, past):
                for k, key in enumerate(ORDERM):
                    if k < RING:
                        wait_full(sp, LAST[MOE_LOAD - RING + k])
                    sp.wait_ge(lo_ready, 33 * i + (33 * past + 23 + k))
                    kind, u, h = key
                    c0, n = 512 * u, FU[u]
                    r0 = 0
                    if kind == "d":
                        src, r0, rn, c0, n, c = a["moe_w_down_1"], c0 + 256 * h, 256, 0, D, 2
                    elif n == 512:
                        src, r0, rn, c = (a["moe_w_gate_1"] if kind == "g" else a["moe_w_up_1"]), 512 * h, 512, 4
                    else:
                        src, rn, c = (a["moe_w_gate_1"] if kind == "g" else a["moe_w_up_1"]), D, 8
                    sp.dma_start(slot(k, c, n), src[i, r0:r0 + rn, c0:c0 + n].rearrange("(c p) n -> p c n", p=P))\
                      .then_inc(landed[k % RING], 16)

            if STOP > 5:
                with sp.Fori(0, NE) as i:
                    expert_loads(i, 0)
                sp.wait_ge(flag_ready, 1)
                again = sp.value_load(flag[0:1, 0:1], min_val=0, max_val=1)
                with sp.If(again > 0):
                    with sp.Fori(0, NE) as i:
                        expert_loads(i, NE)
            sp.wait_ge(fin_ready, 1)
            sp.dma_start(O_dram, XN[:, :, :]).then_inc(out_done, 16)
            sp.wait_ge(out_done, 16)

        @block.tensor
        def _(pe):
            mm, tr = nc.tensor.matmul, nc.tensor.transpose
            rows = Chain(pe, row_order)

            def open_out(name):
                o = IDX[name]
                if o >= 4:
                    pe.wait_ge(bank_free[o % 4], o // 4)
                return bank[o % 4]

            def full(ins, name):
                ins.then_inc(bank_full[IDX[name] % 4], 1)

            def wait_out(name):
                o = IDX[name]
                pe.wait_ge(bank_free[o % 4], o // 4 + 1)

            def norm_transposes(k):
                pe.wait_ge(xn_ready, 2 * (k + 1))
                for j in range(4):
                    name = f"memT{j}" if k == 0 else f"h{k - 1}_{j}"
                    b = open_out(name)
                    for c in range(2):
                        for t in range(TT):
                            r = tr(b[:, 256 * c + P * t:256 * c + P * t + P], XN[:, t, P * (2 * j + c):P * (2 * j + c) + P], ident[:, :])
                    full(r, name)

            def project_T(name, n, c0, src, m=P):
                b = open_out(name)
                width_ = loads[n][2]
                w = slot(n, DC, width_)
                for c in range(DC):
                    r = mm(b[0:m, 0:256], w[:, c, c0:c0 + m], src[:, c, :], start=c == 0, stop=c == DC - 1)
                full(r, name)

            def project(name, n, c0, c1, t, src):
                b = open_out(name)
                w = slot(n, DC, loads[n][2])
                for c in range(DC):
                    r = mm(b[:, 0:c1 - c0], src[:, c, P * t:P * t + P], w[:, c, c0:c1], start=c == 0, stop=c == DC - 1)
                full(r, name)

            def project_wide(names, n):
                bs = [open_out(x) for x in names]
                for h in range(2):
                    wait_landed(pe, n + h)
                    w = slot(n + h, 4, 512)
                    for t in range(TT):
                        for c in range(4):
                            r = mm(bs[t][:, :], HT[:, 4 * h + c, P * t:P * t + P], w[:, c, :], start=h + c == 0, stop=h + c == 4)
                        if h == 1:
                            full(r, names[t])

            def project_out(names, n, chunks):
                bs = [open_out(x) for x in names]
                for j in range(chunks // 2):
                    wait_landed(pe, n + j)
                    w = slot(n + j, 2, D)
                    for t in range(TT):
                        for nh in range(2):
                            for c in range(2):
                                r = mm(bs[2 * t + nh][:, :], OT[:, 2 * j + c, P * t:P * t + P], w[:, c, 512 * nh:512 * nh + 512],
                                       start=j + c == 0, stop=2 * j + c == chunks - 1)
                            if j == chunks // 2 - 1:
                                full(r, names[2 * t + nh])

            def scores(u, pairs):
                if u >= 2 and from_psum(u - 2):
                    pe.wait_ge(exp_done, u - 1)
                elif u >= 2:
                    pe.wait_ge(s_used, S_USED[u - 2])
                b = bank[4 + u % 2]
                w = width(u)
                for k, (q, kk) in enumerate(pairs):
                    r = mm(b[:, w * k:w * k + w], q, kk, start=True, stop=True)
                    if k == 0 and u not in range(U_D, U_X1):
                        rows.link(r)
                r.then_inc(s_full, 1)

            def prob_transposes(u, halves):
                pe.wait_ge(p_ready, u + 1)
                if u >= 2:
                    pe.wait_ge(pt_ready, u - 1)
                b = bank[6 + u % 2]
                for hh in range(halves):
                    for kb in range(width(u) // P):
                        r = tr(b[:, 256 * hh + P * kb:256 * hh + P * kb + P], TP[u % 3][:, hh, P * kb:P * kb + P], ident[:, :])
                r.then_inc(pt_full, 1)

            def values_T(u, name, V, cols, first, last, extra=None):
                pe.wait_ge(pt_ready, u + 1)
                b = open_out(name) if first else bank[IDX[name] % 4]
                kbs = width(u) // P
                for hh in range(2):
                    for kb in range(kbs):
                        r = mm(b[64 * hh:64 * hh + 64, 0:P], V[:, kb, cols[hh]:cols[hh] + 64], PT[u % 4][:, hh, kb, :],
                               start=first and kb == 0, stop=last and extra is None and kb == kbs - 1)
                    if extra is not None:
                        r = mm(b[64 * hh:64 * hh + 64, 0:P], *extra[hh], start=False, stop=True)
                if last:
                    full(r, name)
                else:
                    r.then_inc(pv_done, 1)

            def cross_attention(l, n0, base_u):
                wait_out(f"h{(1, 4)[l]}_3")
                wait_landed(pe, n0)
                for j in range(2):
                    project_T(f"xq{l}_{j}", n0, P * j, HT)
                for s in range(6):
                    if s < 4:
                        u = base_u + s
                        t, hp = s // 2, s % 2
                        if s < 2:
                            wait_out(f"xq{l}_{hp}")
                        scores(u, [(QX[64 * hh:64 * hh + 64, hp, P * t:P * t + P], KM[l][64 * hh:64 * hh + 64, hp, :]) for hh in range(2)])
                    if 1 <= s < 5:
                        prob_transposes(base_u + s - 1, 2)
                    if s >= 2:
                        k = s - 2
                        hp = k % 2
                        values_T(base_u + k, f"xo{l}_{k}", VM[l], [P * hp, P * hp + 64], True, True)
                wait_out(f"xo{l}_3")
                wait_out(f"xo{l}_2")
                project_out([f"xy{l}_{j}" for j in range(4)], n0 + 1, 2)

            pe.wait_ge(ident_ready, 2)
            pe.wait_ge(sv_in, 16 * 13)
            b = open_out("ct")
            full(tr(b[:, 0:CV["rows"]], sv, ident[0:CV["rows"], 0:CV["rows"]]), "ct")
            norm_transposes(0)
            wait_out("memT3")
            for l, src in enumerate((HT, OT)):
                wait_landed(pe, 2 * l)
                for j in range(2):
                    project_T(f"km{l}{j}", 2 * l, P * j, src)
                wait_landed(pe, 2 * l + 1)
                for t in range(TT):
                    project(f"vm{l}{t}", 2 * l + 1, 0, 256, t, src)
            norm_transposes(1)
            wait_out("h0_3")
            wait_landed(pe, 4)
            project_T("a", 4, 0, HT, m=16)
            project_T("nq0", 4, 16, HT)
            wait_landed(pe, 5)
            project_T("nq1", 5, 0, HT)
            project_T("nq2", 5, P, HT)
            wait_landed(pe, 6)
            project_T("nq3", 6, 0, HT)
            project_T("kc", 6, P, HT)
            wait_landed(pe, 7)
            project_T("vc", 7, 0, HT)
            project_T("ks", 7, P, HT)
            wait_landed(pe, 8)
            for t in range(TT):
                project(f"vs{t}", 8, 0, P, t, HT)
            project_T("kw", 8, P, HT)
            wait_landed(pe, 9)
            for t in range(TT):
                project(f"vw{t}", 9, 0, P, t, HT)
            for t in range(TT):
                project(f"g{t}", 9, P, P + 24, t, HT)
            for k, w in enumerate(("gq", "gk")):
                wait_landed(pe, 10 + k)
                for j in range(2):
                    project_T(f"{w}{j}", 10 + k, P * j, HT)
            project_wide(["gv0", "gv1"], 12)
            project_wide(["gr0", "gr1"], 14)
            pe.wait_ge(small_in, 16 * 8)
            for j in range(2):
                b = open_out(f"z{j}")
                full(mm(b[:, 0:256], WA[:, P * j:P * j + P], ATa[:, :], start=True, stop=True), f"z{j}")
            for k, name in enumerate(("ck", "cv")):
                b = open_out(name)
                pe.wait_ge(r_ready, k + 1)
                for h in range(2):
                    wait_landed(pe, 16 + 2 * k + h)
                for jh in range(2):
                    for m in range(16):
                        w = slot(16 + 2 * k + m // 8, 8, 256)
                        r = mm(b[:, 32 * jh:32 * jh + 30], w[:, m % 8, P * jh:P * jh + P], RR[k][:, m, :, :], start=m == 0, stop=m == 15)
                full(r, name)
            b = open_out("c2k")
            wait_out("ck")
            for half in range(2):
                for jh in range(2):
                    r = mm(b[64 * half:64 * half + 64, 0:30], W2[0][:, jh, :], GH[0][:, jh, :], start=jh == 0, stop=jh == 1)
            full(r, "c2k")
            b = open_out("c2v")
            wait_out("cv")
            for g in range(2):
                for jh in range(2):
                    r = mm(b[0:CMP, 64 * g:64 * g + 64], GH[1][:, jh, CMP * g:CMP * g + CMP], W2[1][:, jh, :], start=jh == 0, stop=jh == 1)
            full(r, "c2v")
            b = open_out("sc")
            wait_out("c2k")
            for par in range(2):
                if par == 1:
                    rows.link(r)
                for t, h in [(t, h) for t in range(TT) for h in range(par, 8, 2)]:
                    p0 = 64 * (h % 2)
                    c0 = 16 * (8 * t + h)
                    r = mm(b[:, c0:c0 + CMP], NQ[p0:p0 + 64, h // 2, P * t:P * t + P], KC[p0:p0 + 64, CMP * (h // 4):CMP * (h // 4) + CMP],
                           start=True, stop=True)
            full(r, "sc")
            pe.wait_ge(pc_ready, 1)
            for j in range(4):
                b = open_out(f"pct{j}")
                for k in range(4):
                    r = tr(b[0:CMP, P * k:P * k + P], PCC[:, 4 * j + k, 0:CMP], ident[:, :])
                full(r, f"pct{j}")

            def nsa_unit(u):
                return u // 8, u // 2 % 4, u % 2

            for s in range(18):
                if s < 16:
                    t, hp, br = nsa_unit(s)
                    K = (KS, KW)[br]
                    scores(s, [(NQ[64 * hh:64 * hh + 64, hp, P * t:P * t + P], K[64 * hh:64 * hh + 64, hp // 2, 0:width(s)]) for hh in range(2)])
                if 1 <= s < 17:
                    prob_transposes(s - 1, 2)
                if s >= 2:
                    t, hp, br = nsa_unit(s - 2)
                    g = hp // 2
                    if s == 2:
                        wait_out("pct3")
                    extra = [(VC[:, g, :], PCT[:, 8 * t + 2 * hp + hh, :]) for hh in range(2)] if br else None
                    values_T(s - 2, f"n{t}{hp}", (VS, VW)[br], [64 * g, 64 * g], br == 0, br == 1, extra)

            def gla_scores(k, lev, kt, qt, q, kk):
                if k >= 4:
                    pe.wait_ge(gl_used, k - 3)
                b = bank[4 + k % 4]
                for h in (0, 2, 1, 3):
                    p0 = 64 * (h % 2)
                    if h == 1:
                        rows.link(r)
                    r = mm(b[:, P * h:P * h + P], kk[p0:p0 + 64, h // 2, P * kt:P * kt + P], q[p0:p0 + 64, h // 2, P * qt:P * qt + P],
                           start=True, stop=True)
                r.then_inc(gl_full, 1)

            pe.wait_ge(pt_ready, 16)
            k = 0
            for t in range(TT):
                gla_scores(k, 0, t, t, QG, KG)
                k += 1
            for m in range(8):
                pe.wait_ge(ql_ready, m + 1)
                pe.wait_ge(kl_ready, m + 1)
                for t in range(TT if m < 7 else 1):
                    gla_scores(k, m, t, t if m < 7 else 1, QL[m % 2], KL[m % 2])
                    k += 1
            for t in range(TT):
                b = open_out(f"og{t}")
                if t == 0:
                    pe.wait_ge(pg_done, 3)
                for h in range(4):
                    r = mm(b[:, P * h:P * h + P], PG[t][:, h, :], VG[:, t, P * h:P * h + P], start=True, stop=t == 0)
                    if t == 1:
                        r = mm(b[:, P * h:P * h + P], PG[2][:, h, :], VG[:, 0, P * h:P * h + P], start=False, stop=True)
                full(r, f"og{t}")
            for t in range(TT):
                b = open_out(f"ogT{t}")
                pe.wait_ge(ogs, t + 1)
                for h in range(4):
                    r = tr(b[:, P * h:P * h + P], VG[:, t, P * h:P * h + P], ident[:, :])
                full(r, f"ogT{t}")
            wait_out("ogT0")
            wait_out("ogT1")
            project_out([f"y{j}" for j in range(4)], 20, 8)
            if STOP == 0:
                return
            norm_transposes(2)
            cross_attention(0, 24, U_X0)
            if STOP == 1:
                return
            norm_transposes(3)
            pe.wait_ge(hth, 1)
            pe.wait_ge(htl, 1)

            def split_products(c, pairs, last):
                pe.wait_ge(lo_ready, c + 1)
                for b, ah, al, wsel, start, stop in pairs:
                    wh, wl = wsel(hi[c % CONV]), wsel(lo[c % CONV])
                    mm(b, ah, wh, start=start, stop=False)
                    mm(b, ah, wl, start=False, stop=False)
                    r = mm(b, al, wh, start=False, stop=stop)
                r.then_inc(conv_used, 1)

            def view(chunks, w, c, c0, c1):
                return lambda x: x[:, 0:chunks * w].rearrange("p (c n) -> p c n", c=chunks)[:, c, c0:c1]

            for u in range(7):
                if u < 6:
                    n = FU[u]
                    parts = 2 if n == 512 else 1
                    for kind, off in (("u", 1), ("g", 0)):
                        if u >= 1:
                            if kind == "u":
                                pe.wait_ge(f_a, 2 * u)
                            else:
                                pe.wait_ge(f_tl, 2 * u)
                        for h in range(parts):
                            ch = DC // parts
                            split_products(AT0[(kind, u, h)],
                                           [(bank[2 * t + off][:, 0:n], HTH[:, ch * h + c, P * t:P * t + P], HTL[:, ch * h + c, P * t:P * t + P],
                                             view(ch, n, c, 0, n), h + c == 0, h == parts - 1 and c == ch - 1)
                                            for t in range(TT) for c in range(ch)], False)
                if u >= 1:
                    v = u - 1
                    jn = FU[v] // P
                    if u == 1:
                        pass
                    pe.wait_ge(f_tl, 2 * v + 2)
                    for h in range(jn // 2):
                        split_products(AT0[("d", v, h)],
                                       [(bank[4 + 2 * t + nh][:, :], ATH[t][:, 2 * h + c, :], ATL[t][:, 2 * h + c, :],
                                         view(2, D, c, 512 * nh, 512 * nh + 512), v + h + c == 0, v == 5 and c == 1)
                                        for t in range(TT) for nh in range(2) for c in range(2)], False)
                if u < 6:
                    for t in range(TT):
                        pe.wait_ge(f_a, 2 * u + t + 1)
                        for j in range(FU[u] // P):
                            r = tr(bank[2 * t][:, P * j:P * j + P], AB[t][:, P * j:P * j + P], ident[:, :])
                        r.then_inc(f_t, 1)
            if STOP == 2:
                return

            norm_transposes(4)
            wait_out("h3_3")
            for hf in range(2):
                for w, name in enumerate(("q1", "q2", "k1", "k2")):
                    wait_landed(pe, DIFF_LOAD + 4 * hf + w)
                    for j in range(2):
                        project_T(f"d{name}{2 * hf + j}", DIFF_LOAD + 4 * hf + w, P * j, HT)
            for half in range(2):
                project_wide([f"dv{t}{half}" for t in range(TT)], DIFF_LOAD + 8 + 2 * half)
            b = open_out("lam")
            pe.wait_ge(lams, 1)
            full(mm(b[:, 0:1], ones[0:1, :], small[0:1, 50:51], start=True, stop=True), "lam")
            for s in range(18):
                if s < 16:
                    t, h = s // 8, s % 8
                    p0 = 64 * (h % 2)
                    scores(U_D + s, [(QD[p0:p0 + 64, i, h // 2, P * t:P * t + P], KD[p0:p0 + 64, i, h // 2, 0:width(U_D + s)]) for i in range(2)])
                if 1 <= s < 17:
                    prob_transposes(U_D + s - 1, 1)
                if s >= 2:
                    u = U_D + s - 2
                    t, h = (s - 2) // 8, (s - 2) % 8
                    name, last = attn_pv_group(u)
                    pe.wait_ge(pt_ready, u + 1)
                    b = open_out(name) if h % 4 == 0 else bank[IDX[name] % 4]
                    for kb in range(t + 1):
                        r = mm(b[:, P * (h % 4):P * (h % 4) + P], PT[u % 4][:, 0, kb, :], VD[:, kb, P * h:P * h + P], start=kb == 0, stop=kb == t)
                    if last:
                        full(r, name)
                    else:
                        r.then_inc(pv_done, 1)
            for t in range(TT):
                pe.wait_ge(ods, t + 1)
                for hq in range(2):
                    b = open_out(f"odT{t}{hq}")
                    for k in range(4):
                        h = 4 * hq + k
                        r = tr(b[:, P * k:P * k + P], OD[:, t, P * h:P * h + P], ident[:, :])
                    full(r, f"odT{t}{hq}")
            wait_out("odT10")
            wait_out("odT11")
            project_out([f"dy{j}" for j in range(4)], DIFF_LOAD + 12, 8)
            if STOP == 3:
                return
            norm_transposes(5)
            cross_attention(1, DIFF_LOAD + 16, U_X1)
            if STOP == 4:
                return

            norm_transposes(6)
            wait_out("h5_3")
            b = open_out("lg")
            for t in range(TT):
                for c in range(DC):
                    r = mm(b[:, NE * t:NE * t + NE], HT[:, c, P * t:P * t + P], WR[:, c, :], start=c == 0, stop=c == DC - 1)
            full(r, "lg")
            b = open_out("rk")
            pe.wait_ge(ch_ready, 1)
            CH = RA
            for t in range(TT):
                if t == 1:
                    mm(b[:, NE:2 * NE], ones[:, :], CH[:, 0, :], start=True, stop=False)
                r = mm(b[:, NE * t:NE * t + NE], U_strict[:, :], CH[:, t, :], start=t == 0, stop=True)
            for t in range(TT):
                r = mm(b[:, 2 * NE:3 * NE], ones[:, :], CH[:, t, :], start=t == 0, stop=t == 1)
            full(r, "rk")
            pe.wait_ge(grow_in, 32)
            for nh in range(2):
                b = open_out(f"gb{nh}")
                full(mm(b[:, :], ones[0:1, :], grow[0:1, 0, 512 * nh:512 * nh + 512], start=True, stop=True), f"gb{nh}")
            for nh in range(2):
                r = mm(bank[4 + nh][:, :], ones[0:1, :], grow[0:1, 1, 512 * nh:512 * nh + 512], start=True, stop=True)
            r.then_inc(m_y, 1)
            if STOP == 5:
                return

            def gather():
                for half in range(2):
                    b = bank[6 + half]
                    for c in range(4):
                        for t in range(TT):
                            cs = slice(P * (4 * half + c), P * (4 * half + c) + P)
                            mm(b[:, P * c:P * c + P], XGH[:, t, cs], SELR[:, t, :], start=t == 0, stop=False)
                            r = mm(b[:, P * c:P * c + P], XGL[:, t, cs], SELR[:, t, :], start=False, stop=t == 1)
                r.then_inc(ga_full, 1)

            def expert(i, past):
                it = i + past if past else i

                def unit_up(u):
                    n = FU[u]
                    parts = 2 if n == 512 else 1
                    ch = DC // parts
                    pe.wait_ge(m_a, it * 6 + (u + 1))
                    if u == 0:
                        pe.wait_ge(hgl, it + 1)
                    for off, kind in ((1, "u"), (0, "g")):
                        if kind == "g":
                            pe.wait_ge(m_tl, it * 6 + (u + 1))
                        for h in range(parts):
                            products(ATM[(kind, u, h)],
                                     [(bank[2 * (u % 2) + off][:, 0:n], HGH[:, ch * h + c, :], HGL[:, ch * h + c, :],
                                       view(ch, n, c, 0, n), h + c == 0, h == parts - 1 and c == ch - 1) for c in range(ch)])

                def products(k, pairs):
                    pe.wait_ge(lo_ready, it * 33 + (34 + k))
                    for b, ah, al, wsel, start, stop in pairs:
                        wh, wl = wsel(hi[k % CONV]), wsel(lo[k % CONV])
                        mm(b, ah, wh, start=start, stop=False)
                        mm(b, ah, wl, start=False, stop=False)
                        r = mm(b, al, wh, start=False, stop=stop)
                    r.then_inc(conv_used, 1)

                def unit_transposes(u):
                    pe.wait_ge(m_a, it * 6 + (u + 3))
                    for j in range(FU[u] // P):
                        r = tr(bank[2 * (u % 2)][:, P * j:P * j + P], AB[u % 2][:, P * j:P * j + P], ident[:, :])
                    r.then_inc(m_t, 1)

                def unit_down(u):
                    pe.wait_ge(m_tl, it * 6 + (u + 3))
                    if u == 0:
                        pe.wait_ge(m_yl, it + 1)
                    jn = FU[u] // P
                    for h in range(jn // 2):
                        products(ATM[("d", u, h)],
                                 [(bank[4 + nh][:, :], ATH[u % 2][:, 2 * h + c, :], ATL[u % 2][:, 2 * h + c, :],
                                   view(2, D, c, 512 * nh, 512 * nh + 512), u + h + c == 0, u == 5 and c == 1)
                                  for nh in range(2) for c in range(2)])

                for u in range(8):
                    if u < 6:
                        unit_up(u)
                    if u == 0:
                        scatter(it)
                    if u == 1:
                        pe.wait_ge(sc_add, it * 4 + 4)
                        for t in range(TT):
                            tr(bank[6][:, P * t:P * t + P], SEL[:, t, :], ident[:, :])
                        for t in range(TT):
                            r = mm(bank[6][:, 256:257], SEL[:, t, :], CBI[:, t:t + 1], start=t == 0, stop=t == 1)
                        r.then_inc(st_full, 1)
                    if u == 6:
                        pe.wait_ge(sel_ready, it + 2)
                        pe.wait_ge(st_done, it + 1)
                        gather()
                    if 1 <= u < 7:
                        unit_transposes(u - 1)
                    if u >= 2:
                        unit_down(u - 2)

            def scatter(it):
                pe.wait_ge(m_yl, it + 1)
                pe.wait_ge(hgl, it + 1)
                for k in range(4):
                    if k >= 2:
                        pe.wait_ge(sc_add, it * 4 + (k - 1))
                    cs = slice(512 * (k % 2), 512 * (k % 2) + 512)
                    mm(bank[6 + k % 2][:, :], SELT[:, k // 2, :], YEH[:, cs], start=True, stop=False)
                    r = mm(bank[6 + k % 2][:, :], SELT[:, k // 2, :], YEL[:, cs], start=False, stop=True)
                    r.then_inc(sc_full, 1)

            pe.wait_ge(xg_ready, 1)
            pe.wait_ge(sel_ready, 1)
            gather()
            with pe.Fori(0, NE) as i:
                expert(i, 0)
            pe.wait_ge(flag_ready, 1)
            again = pe.value_load(flag[0:1, 0:1], min_val=0, max_val=1)
            with pe.If(again > 0):
                with pe.Fori(0, NE) as i:
                    expert(i, NE)
            scatter(again * NE + NE)

        def step_slots(order, lag, s):
            up = [k for k, x in enumerate(order) if x[0] != "d" and x[1] == s]
            down = [k for k, x in enumerate(order) if x[0] == "d" and x[1] == s - lag]
            return up, down

        def nm(u, n=2):
            return small[:, 32 + 2 * (u % 3):32 + 2 * (u % 3) + n]

        def ls(u, n=2):
            return small[:, 38 + 2 * (u % 3):38 + 2 * (u % 3) + n]

        @block.scalar
        def _(act):
            af = nc.scalar.activation
            chain = Chain(act, act_chain)

            gains = (("mix0", "mix_norm_0"), ("xat0", "xattn_norm_0"), ("xmem0", "xattn_mem_norm_0"), ("ffn0", "ffn_norm_0"),
                     ("mix1", "mix_norm_1"), ("xat1", "xattn_norm_1"), ("xmem1", "xattn_mem_norm_1"), ("ffn1", "ffn_norm_1"),
                     ("balpha", "gla_b_alpha_0"), ("glan", "gla_out_norm_0"), ("diffn", "diff_out_norm_1"))
            for key, name in gains:
                src = a[name].rearrange("(r n) -> r n", n=P)
                act.dma_start(TP[0][CV[key]:CV[key] + src.shape[0], 0, 0:P], src).then_inc(sv_in, 16)
            for k, w in enumerate("kv"):
                act.dma_start(TP[0][CV["pos" + w]:CV["pos" + w] + 16, 0, 0:P],
                              a[f"nsa_cmp_pos_{w}_0"].rearrange("(m l) d -> m (l d)", l=2)).then_inc(sv_in, 16)
            act.dma_start(WA[:, :], a["gla_w_alpha_0"]).then_inc(small_in, 16)
            for k, w in enumerate("kv"):
                act.dma_start(W2[k][:, :, :], a[f"nsa_cmp_w2_{w}_0"].rearrange("(c p) n -> p c n", p=P)).then_inc(small_in, 16)
            act.dma_start(WR[:, :, :], a["moe_router_1"].rearrange("(c p) n -> p c n", p=P)).then_inc(small_in, 16)
            for k, w in enumerate(("lq1", "lk1", "lq2", "lk2")):
                act.dma_start(lrow[:, k, :], a[f"diff_{w}_1"].rearrange("(a n) -> a n", a=1)).then_inc(small_in, 16)

            def squares(n, src, junk):
                for t in range(TT):
                    af(junk(t), src[:, t, :], ACT.Square, accum_out=small[:, 2 * n + t:2 * n + t + 1]).then_inc(ss_ready, 1)

            def xsquares(n):
                act.wait_ge(x_ready, n - 1)
                squares(n, X, lambda t: XN[:, t, :])

            def out_norm(k):
                g = CV[("mix0", "xat0", "ffn0", "mix1", "xat1", "ffn1")[k]]
                for j in range(4):
                    b = wait_full(act, f"h{k}_{j}")
                    for c in range(2):
                        r = af(HT[:, 2 * j + c, :], b[:, 256 * c:256 * c + 256], ACT.Copy, scale=CT[:, g + 2 * j + c:g + 2 * j + c + 1])
                    freed(r, f"h{k}_{j}")

            def take(name, dst, src, func=ACT.Copy, scale=1.0, bias=None):
                b = wait_full(act, name)
                kw = {} if bias is None else {"bias": bias}
                freed(af(dst, src(b), func, scale=scale, **kw), name)

            def exps(u, from_psum, widths=None):
                act.wait_ge(nm_ready, u + 1)
                w = width(u)
                for k in range(2):
                    src = bank[4 + u % 2][:, w * k:w * k + w] if from_psum else TP[u % 3][:, k, 0:w]
                    if k == 0 and from_psum and u >= 3:
                        act.wait_ge(pt_full, u - 2)
                    r = af(TP[u % 3][:, k, 0:w], src, ACT.Exp, bias=nm(u)[:, k:k + 1], accum_out=ls(u)[:, k:k + 1])
                r.then_inc(exp_done, 1)

            def copy_pt(u, halves):
                act.wait_ge(pt_full, u + 1)
                if u >= 4:
                    wait_pv(act, u - 4)
                b = bank[6 + u % 2]
                w = width(u)
                if halves == 1:
                    r = af(PT[u % 4][:, 0, :, :].rearrange("p a b -> p (a b)")[:, 0:w], b[:, 0:w], ACT.Copy)
                else:
                    v = b[:, :].rearrange("p (h n) -> p h n", h=2)[:, :, 0:w]
                    r = af(PT[u % 4][:, :, :, :].rearrange("p h a b -> p h (a b)")[:, :, 0:w], v, ACT.Copy)
                r.then_inc(pt_ready, 1)

            def cross_attention(l, base_u, k):
                out_norm(k)
                for j in range(2):
                    take(f"xq{l}_{j}", QX[:, j, :], lambda b: b[:, 0:256], scale=0.125)
                for s in range(6):
                    if s < 4:
                        exps(base_u + s, True)
                    if 1 <= s < 5:
                        copy_pt(base_u + s - 1, 2)
                    if s >= 2:
                        q = s - 2
                        take(f"xo{l}_{q}", OT[:, q % 2, P * (q // 2):P * (q // 2) + P], lambda b: b[:, 0:P])

            act.wait_ge(mem_in, 16)
            squares(0, XN, lambda t: OT[:, 4 * t:4 * t + 4, :].rearrange("p a b -> p (a b)"))
            act.wait_ge(x_in, 16)
            squares(1, X, lambda t: HT[:, 4 * t:4 * t + 4, :].rearrange("p a b -> p (a b)"))
            take("ct", CT[:, :], lambda b: b[:, 0:CV["rows"]])
            act.wait_ge(bank_free[0], 1)
            for j in range(4):
                b = wait_full(act, f"memT{j}")
                for l, dst in enumerate((HT, OT)):
                    for c in range(2):
                        g = CV[f"xmem{l}"] + 2 * j + c
                        r = af(dst[:, 2 * j + c, :], b[:, 256 * c:256 * c + 256], ACT.Copy, scale=CT[:, g:g + 1])
                freed(r, f"memT{j}")
            for l in range(2):
                for j in range(2):
                    take(f"km{l}{j}", KM[l][:, j, :], lambda b: b[:, 0:256])
                for t in range(2):
                    take(f"vm{l}{t}", VM[l][:, t, :], lambda b: b[:, 0:256])
            out_norm(0)
            take("a", ATa[:, :], lambda b: b[0:16, 0:256])

            def both_halves(name, dst, shift):
                b = wait_full(act, name)
                for half in range(2):
                    for g in range(2):
                        s = shift * half
                        r = af(dst[64 * half:64 * half + 64, g, 0:256 - s], b[64 * g:64 * g + 64, s:256], ACT.Copy)
                freed(r, name)

            for j in range(4):
                take(f"nq{j}", NQ[:, j, :], lambda b: b[:, 0:256], scale=0.125)
            both_halves("kc", T2[0], 1)
            both_halves("vc", T2[1], 1)
            both_halves("ks", KS, 0)
            for t in range(TT):
                take(f"vs{t}", VS[:, t, :], lambda b: b[:, 0:P])
            both_halves("kw", KW, 0)
            for t in range(TT):
                take(f"vw{t}", VW[:, t, :], lambda b: b[:, 0:P])
            for t in range(TT):
                take(f"g{t}", GT[:, t, :], lambda b: b[:, 0:24], func=ACT.Sigmoid)
            for j in range(2):
                take(f"gq{j}", QG[:, j, :], lambda b: b[:, 0:256], scale=0.125)
            for j in range(2):
                take(f"gk{j}", KG[:, j, :], lambda b: b[:, 0:256])
            for t in range(TT):
                take(f"gv{t}", VG[:, t, :], lambda b: b[:, :])
            for t in range(TT):
                take(f"gr{t}", SR[:, t, :], lambda b: b[:, :], func=ACT.Silu)
            for j in range(2):
                take(f"z{j}", LA[:, j, :], lambda b: b[:, 0:256], func=ACT.Identity, bias=CT[:, CV["balpha"] + j:CV["balpha"] + j + 1])
            for k, name in enumerate(("ck", "cv")):
                take(name, GH[k][:, :, :], lambda b: b[:, 0:64].rearrange("p (j n) -> p j n", j=2)[:, :, 0:30], func=ACT.Gelu_apprx_tanh)
            take("c2k", KC[:, :], lambda b: b[:, 0:30])
            take("c2v", VC[:, :, :], lambda b: b[0:CMP, 0:P].rearrange("p (g d) -> p g d", g=2))
            act.wait_ge(pc_t, 1)
            af(PCC[:, :, 0:CMP], PCC[:, :, 0:CMP], ACT.Exp).then_inc(pc_e, 1)
            for j in range(4):
                take(f"pct{j}", PCT[:, 4 * j:4 * j + 4, :], lambda b: b[0:CMP, :].rearrange("p (a b) -> p a b", a=4))
            for s in range(18):
                if s < 16:
                    exps(s, False)
                if 1 <= s < 17:
                    copy_pt(s - 1, 2)
                if s >= 2 and s % 2 == 1:
                    k = (s - 3) // 2
                    take(f"n{k // 4}{k % 4}", OT[:, 4 + k % 4, P * (k // 4):P * (k // 4) + P], lambda b: b[:, 0:P])
            act.wait_ge(z_ready, 1)
            chain.link(af(EL1[:, :, :], EL1[:, :, :], ACT.Exp, scale=-1.0))
            af(EL1[:, :, :], EL1[:, :, :], ACT.Ln, bias=1.0).then_inc(l_ready, 1)
            for m in range(8):
                act.wait_ge(d_ready, m + 1)
                af(EL[m % 2][:, :, :], EL[m % 2][:, :, :], ACT.Exp, scale=-1.0).then_inc(el_ready, 1)
            for t in range(TT):
                take(f"ogT{t}", OT[:, 0:4, P * t:P * t + P], lambda b: b[:, :].rearrange("p (a b) -> p a b", a=4),
                     scale=CT[:, CV["glan"]:CV["glan"] + 1])
            if STOP == 0:
                return
            xsquares(2)
            cross_attention(0, U_X0, 1)
            if STOP == 1:
                return
            xsquares(3)
            out_norm(2)
            act.wait_ge(bank_free[IDX["h2_3"] % 4], IDX["h2_3"] // 4 + 1)
            af(HTH[:, :, :], HT[:, :, :], ACT.Copy).then_inc(hth, 1)

            def split_hi(c):
                n = FFN0_LOAD + c
                wait_landed(act, n)
                if c >= CONV:
                    act.wait_ge(conv_used, c - CONV + 1)
                w = loads[n][1] * loads[n][2]
                af(hi[c % CONV][:, 0:w], ring[n % RING][:, 0:w], ACT.Copy).then_inc(hi_ready, 1)

            def act0(u):
                act.wait_ge(conv_used, step_slots(ORDER0, 1, u)[0][-1] + 1)
                for t in range(TT):
                    af(AB[t][:, 0:FU[u]], bank[2 * t][:, 0:FU[u]], ACT.Silu).then_inc(f_e, 1)

            def ath0(u):
                for t in range(TT):
                    act.wait_ge(f_t, 2 * u + t + 1)
                    j = FU[u] // P
                    af(ATH[t][:, 0:j, :].rearrange("p a b -> p (a b)"), bank[2 * t][:, 0:FU[u]], ACT.Copy).then_inc(f_th, 1)

            for u in range(7):
                up, down = step_slots(ORDER0, 1, u)
                if u == 6:
                    for c in down:
                        split_hi(c)
                    continue
                for c in (up if u == 0 else up[len(up) // 2:]) + down:
                    split_hi(c)
                act0(u)
                if u < 5:
                    nxt = step_slots(ORDER0, 1, u + 1)[0]
                    for c in nxt[:len(nxt) // 2]:
                        split_hi(c)
                ath0(u)
            if STOP == 2:
                return

            act.wait_ge(conv_used, 33)
            if STOP > 4:
                act.dma_start(grow[:, 0, :], a["ffn_norm_1"].rearrange("(a n) -> a n", a=1)).then_inc(grow_in, 16)
                act.dma_start(grow[:, 1, :], a["final_norm"].rearrange("(a n) -> a n", a=1)).then_inc(grow_in, 16)
            xsquares(4)
            out_norm(3)
            for hf in range(2):
                for w, (name, dst) in enumerate((("q1", QD), ("q2", QD), ("k1", KD), ("k2", KD))):
                    for j in range(2):
                        take(f"d{name}{2 * hf + j}", dst[:, w % 2, 2 * hf + j, :], lambda b: b[:, 0:256], scale=0.125 if w < 2 else 1.0)
            for half in range(2):
                for t in range(TT):
                    take(f"dv{t}{half}", VD[:, t, 512 * half:512 * half + 512], lambda b: b[:, :])
            act.wait_ge(er_ready, 1)
            af(small[0:1, 52:54], small[0:1, 48:50], ACT.Exp).then_inc(r_e, 1)
            take("lam", small[:, 51:52], lambda b: b[:, 0:1])
            for s in range(19):
                if s < 16:
                    exps(U_D + s, False)
                if 1 <= s < 17:
                    copy_pt(U_D + s - 1, 1)
                if s >= 6 and (s - 6) % 4 == 0:
                    k = (s - 6) // 4
                    take(f"od{k // 2}{k % 2}", OD[:, k // 2, 512 * (k % 2):512 * (k % 2) + 512], lambda b: b[:, :])
            for t in range(TT):
                for hq in range(2):
                    take(f"odT{t}{hq}", OT[:, 4 * hq:4 * hq + 4, P * t:P * t + P], lambda b: b[:, :].rearrange("p (a b) -> p a b", a=4),
                         scale=CT[:, CV["diffn"]:CV["diffn"] + 1])
            if STOP == 3:
                return
            xsquares(5)
            cross_attention(1, U_X1, 4)
            if STOP == 4:
                return
            xsquares(6)
            out_norm(5)
            act.wait_ge(e_ready, 1)
            af(small[:, 56:58], small[:, 54:56], ACT.Exp).then_inc(r_e, 1)
            act.wait_ge(m_y, 1)
            act.wait_ge(m_init, 1)
            for nh in range(2):
                r = af(FG[:, 512 * nh:512 * nh + 512], bank[4 + nh][:, :], ACT.Copy)
            r.then_inc(m_ye, 1)
            if STOP == 5:
                return

            def result_hi(it):
                act.wait_ge(conv_used, it * 33 + 33)
                for nh in range(2):
                    r = af(YEH[:, 512 * nh:512 * nh + 512], bank[4 + nh][:, :], ACT.Copy, scale=WS[:, :])
                r.then_inc(m_ye, 1)

            def gather_hi(past):
                act.wait_ge(ga_full, past + 1)
                for half in range(2):
                    r = af(HGH[:, 4 * half:4 * half + 4, :].rearrange("p a b -> p (a b)"), bank[6 + half][:, :], ACT.Copy)
                r.then_inc(hgh, 1)

            def expert(i, past):
                it = i + past if past else i

                def split_hi_m(k):
                    act.wait_ge(landed[k % RING], it * 48 + 16 * (MOE_LOAD // RING + k // RING + 1))
                    act.wait_ge(conv_used, it * 33 + (33 + k - CONV + 1))
                    kind, u, h = ORDERM[k]
                    af(hi[k % CONV][:, :], ring[k % RING][:, :], ACT.Copy).then_inc(hi_ready, 1)

                for s in range(8):
                    up, down = step_slots(ORDERM, 2, s)
                    for k in up[:2]:
                        split_hi_m(k)
                    if s >= 2:
                        u = s - 2
                        act.wait_ge(m_t, it * 6 + (u + 1))
                        af(ATH[u % 2][:, 0:FU[u] // P, :].rearrange("p a b -> p (a b)"), bank[2 * (u % 2)][:, 0:FU[u]], ACT.Copy).then_inc(m_th, 1)
                    for k in up[2:3]:
                        split_hi_m(k)
                    if s == 0:
                        result_hi(it)
                    if 1 <= s < 7:
                        u = s - 1
                        last_up = step_slots(ORDERM, 2, u)[0][-1]
                        act.wait_ge(conv_used, it * 33 + (33 + last_up + 1))
                        af(AB[u % 2][:, 0:FU[u]], bank[2 * (u % 2)][:, 0:FU[u]], ACT.Silu).then_inc(m_e, 1)
                    for k in up[3:] + down:
                        split_hi_m(k)
                    if s == 2:
                        act.wait_ge(st_full, it + 1)
                        af(SELT[:, :, :].rearrange("p a b -> p (a b)"), bank[6][:, 0:256], ACT.Copy)
                        af(WS[:, :], bank[6][:, 256:257], ACT.Copy).then_inc(st_done, 1)
                    if s == 6:
                        gather_hi(it + 1)

            act.wait_ge(xg_ready, 1)
            gather_hi(0)
            with act.Fori(0, NE) as i:
                expert(i, 0)
            act.wait_ge(flag_ready, 1)
            again = act.value_load(flag[0:1, 0:1], min_val=0, max_val=1)
            with act.If(again > 0):
                with act.Fori(0, NE) as i:
                    expert(i, NE)
            result_hi(again * NE + NE)
            act.wait_ge(x_ready, 6)
            act.wait_ge(xn_ready, 14)
            squares(7, X, lambda t: XN[:, t, :])

        @block.vector
        def _(dve):
            v = nc.vector
            chain = Chain(dve, dve_chain)
            link = chain.link
            tt, ts = v.tensor_tensor, v.tensor_scalar

            def bc(ap, n):
                return ap.unsqueeze(2).broadcast_to([ap.shape[0], ap.shape[1], n])

            def normalise(n, src):
                dve.wait_ge(ss_ready, 2 * n + 2)
                ts(small[:, 16 + 2 * n:18 + 2 * n], small[:, 2 * n:2 * n + 2], 1.0 / D, EPS, ALU.mult, ALU.add).then_inc(ms_ready, 1)
                dve.wait_ge(rstd_ready, n + 1)
                for t in range(TT):
                    ts(XN[:, t, :], src[:, t, :], rstd[:, t:t + 1], None, ALU.mult).then_inc(xn_ready, 1)

            dve.wait_ge(pool_const, 1)
            link(v.tensor_copy(NB[:, 7, :], IOn[:, :]))
            for h in range(7):
                r = ts(NB[:, h, :], NB[:, 7, :], SLOPES[h], None, ALU.mult)
            link(r)
            link(ts(NB[:, 7, :], NB[:, 7, :], SLOPES[7], None, ALU.mult))
            link(v.tensor_copy(CB[:, 7, :], IOc[:, 0, :]))
            link(v.tensor_copy(CB[:, 15, :], IOc[:, 1, :]))
            for t in range(TT):
                for h in range(7):
                    r = ts(CB[:, 8 * t + h, :], CB[:, 8 * t + 7, :], SLOPES[h], None, ALU.mult)
            link(r)
            for t in range(TT):
                r = ts(CB[:, 8 * t + 7, :], CB[:, 8 * t + 7, :], SLOPES[7], None, ALU.mult)
            link(r)
            link(v.memset(CM[:, :, :], 1.0))
            link(tt(out=IOx[:, :], in0=IOs[:, :], in1=IOt[:, :], op=ALU.bitwise_xor))
            for m in range(8):
                if m == 0:
                    ts(MKf[:, 0, :], IOx[:, :], 0, None, ALU.is_equal)
                else:
                    link(ts(IOy[:, :], IOx[:, :], m - 1, None, ALU.logical_shift_right))
                    link(ts(MKf[:, m, :], IOy[:, :], 1, None, ALU.is_equal))
            r = v.memset(halfneg[:, :], -0.5)
            r.then_inc(dve_const, 1)
            dve.wait_ge(mk_ready, 1)
            link(v.tensor_copy(MK[:, :, :], MKf[:, :, :]))

            dve.wait_ge(mem_in, 16)
            normalise(0, XN)
            dve.wait_ge(small_in, 16 * 8)
            dve.wait_ge(bank_free[0], 1)
            link(ts(CT[:, CV["diffn"]:CV["diffn"] + 1], CT[:, CV["diffn"]:CV["diffn"] + 1], 1.0 - LAMBDA_INIT, None, ALU.mult))
            link(tt(out=lrow[:, 0::2, :], in0=lrow[:, 0::2, :], in1=lrow[:, 1::2, :], op=ALU.mult))
            v.tensor_reduce(small[0:1, 48:50], lrow[:, 0::2, :], AX, ALU.add).then_inc(er_ready, 1)

            wait_full(dve, "memT3")
            normalise(1, X)
            for k, name in enumerate(("kc", "vc")):
                o = IDX[name]
                dve.wait_ge(bank_free[o % 4], o // 4 + 1)
                for g in range(2):
                    for mh in range(2):
                        src = T2[k][:, g, 16 * mh:16 * mh + 240].rearrange("p (c m) -> p m c", m=16)[:, 0::2, :]
                        pos = CT[:, CV["pos" + "kv"[k]] + 8 * mh:CV["pos" + "kv"[k]] + 8 * mh + 8]
                        r = tt(out=RR[k][:, 8 * mh:8 * mh + 8, g, :], in0=src, in1=bc(pos, CMP), op=ALU.add)
                r.then_inc(r_ready, 1)
            b = wait_full(dve, "sc")
            dve.wait_ge(nb_ready, 1)
            bs = b[:, 0:256].rearrange("p (h c) -> p h c", c=16)[:, :, 0:CMP]
            PC = PCC[:, :, 0:CMP]
            r = tt(out=PC, in0=bs, in1=CB[:, :, 0:CMP], op=ALU.add)
            freed(r, "sc")
            dve.wait_ge(bank_free[IDX["sc"] % 4], IDX["sc"] // 4 + 1)
            PM, PS = CX[:, 0:16], CX[:, 16:32]
            link(v.tensor_reduce(PM, PC, AX, ALU.max))
            tt(out=PC, in0=PC, in1=bc(PM, CMP), op=ALU.subtract).then_inc(pc_t, 1)
            dve.wait_ge(pc_e, 1)
            for t in range(TT):
                link(tt(out=PCC[:, 8 * t:8 * t + 8, 0:CMP], in0=PCC[:, 8 * t:8 * t + 8, 0:CMP],
                        in1=CM[:, t:t + 1, 0:CMP].broadcast_to([P, 8, CMP]), op=ALU.mult))
            link(v.tensor_reduce(PS, PC, AX, ALU.add))
            link(ts(PS, PS, TINY, None, ALU.max))
            link(v.reciprocal(PS, PS))
            o = IDX["g1"]
            dve.wait_ge(bank_free[o % 4], o // 4 + 1)
            link(tt(out=PS, in0=PS, in1=GT[:, :, :].rearrange("p t (h b) -> p (t h) b", b=3)[:, :, 0], op=ALU.mult))
            tt(out=PC, in0=PC, in1=bc(PS, CMP), op=ALU.mult).then_inc(pc_ready, 1)

            def add_bias(u, h0, step):
                dve.wait_ge(s_full, u + 1)
                if u >= 3:
                    dve.wait_ge(pt_full, u - 2)
                w = width(u)
                T = TP[u % 3][:, :, 0:w]
                bias = NB[:, h0:h0 + 2, 256 - w:256] if step else NB[:, h0:h0 + 1, 256 - w:256].broadcast_to([P, 2, w])
                tt(out=T, in0=bank[4 + u % 2][:, 0:2 * w].rearrange("p (h w) -> p h w", h=2), in1=bias, op=ALU.add).then_inc(s_used, 1)
                dve.wait_ge(s_used, S_USED[u])
                v.tensor_reduce(nm(u), T, AX, ALU.max, negate=True).then_inc(nm_ready, 1)

            def scale_probs(u, gate):
                dve.wait_ge(exp_done, u + 1)
                w = width(u)
                link(v.reciprocal(ls(u), ls(u)))
                if gate is not None:
                    link(tt(out=ls(u), in0=ls(u), in1=gate, op=ALU.mult))
                for k in range(2):
                    r = ts(TP[u % 3][:, k, 0:w], TP[u % 3][:, k, 0:w], ls(u)[:, k:k + 1], None, ALU.mult)
                r.then_inc(p_ready, 1)

            for s in range(17):
                if s < 16:
                    add_bias(s, 2 * (s // 2 % 4), True)
                if s >= 1:
                    t, hp, br = (s - 1) // 8, (s - 1) // 2 % 4, (s - 1) % 2
                    gate = GT[:, t, :].rearrange("p (h b) -> p h b", b=3)[:, 2 * hp:2 * hp + 2, 1 + br]
                    scale_probs(s - 1, gate)
            dve.wait_ge(bank_free[IDX["z1"] % 4], IDX["z1"] // 4 + 1)
            v.scalar_tensor_tensor(EL1[:, :, :], LA[:, :, :], -1.0, LA[:, :, :], ALU.mult, ALU.max).then_inc(z_ready, 1)
            dve.wait_ge(l_ready, 1)
            link(v.scalar_tensor_tensor(LA[:, :, :], LA[:, :, :], 0.0, EL1[:, :, :], ALU.min, ALU.subtract))
            link(ts(LA[:, :, :], LA[:, :, :], 1.0 / 16.0, None, ALU.mult))
            link(v.memset(EL1[:, :, :], 1.0))
            for j in range(2):
                r = v.tensor_tensor_scan(BG[:, j, :], EL1[:, j, :], LA[:, j, :], 0.0, ALU.mult, ALU.add)
            link(r)
            wait_full(dve, "n13")
            for t in range(3):
                r = v.memset(PG[t][:, :, :], 0.0)
            link(r)

            def take_scores(k, lev, dst):
                dve.wait_ge(gl_full, k + 1)
                if k >= 2:
                    dve.wait_ge(gl_used, k - 1)
                src = bank[4 + k % 4][:, :].rearrange("p (h n) -> p h n", h=4)
                if lev is None:
                    v.tensor_copy(dst[:, :, :], src).then_inc(gl_used, 1)
                else:
                    v.copy_predicated(dst[:, :, :], MK[:, lev:lev + 1, :].broadcast_to([P, 4, P]), src).then_inc(gl_used, 1)

            k = 0
            for m in range(10):
                if m < 8:
                    L = 1 << m
                    if m >= 2:
                        dve.wait_ge(kl_ready, m - 1)
                        dve.wait_ge(ql_ready, m - 1)
                    bv = BG[:, :, :].rearrange("p a (n l) -> p (a n) l", l=2 * L)
                    ev = EL[m % 2][:, :, :].rearrange("p a (n l) -> p (a n) l", l=2 * L)
                    ref = bv[:, :, L - 1:L].broadcast_to([P, 256 // L, 2 * L])
                    link(tt(out=ev, in0=bv, in1=ref, op=ALU.subtract))
                    v.scalar_tensor_tensor(EL[m % 2][:, :, :], EL[m % 2][:, :, :], -1.0, EL[m % 2][:, :, :], ALU.mult, ALU.max).then_inc(d_ready, 1)
                if m == 0:
                    for t in range(TT):
                        take_scores(k, 0, PG[t])
                        k += 1
                if m >= 2:
                    for t in range(TT if m < 9 else 1):
                        take_scores(k, m - 1 if m < 9 else None, PG[t] if m < 9 else PG[2])
                        k += 1
                if m < 8:
                    if m >= 2:
                        dve.wait_ge(gl_full, 2 * m)
                    dve.wait_ge(el_ready, m + 1)
                    tt(out=QL[m % 2][:, :, :], in0=QG[:, :, :], in1=EL[m % 2][:, :, :], op=ALU.mult).then_inc(ql_ready, 1)
            v.memset(small[:, 58:59], 0.0).then_inc(pg_done, 3)
            wait_full(dve, "og1")
            G2 = NQ[:, 0:2, :].rearrange("p a b -> p (a b)")
            for t in range(TT):
                b = wait_full(dve, f"og{t}")
                freed(v.tensor_copy(VG[:, t, :], b[:, :]), f"og{t}")
                o = IDX[f"og{t}"]
                dve.wait_ge(bank_free[o % 4], o // 4 + 1)
                link(tt(out=G2, in0=VG[:, t, :], in1=VG[:, t, :], op=ALU.mult))
                G3 = G2.rearrange("p (h n) -> p h n", h=4)
                link(v.tensor_reduce(CX[:, 0:4], G3, AX, ALU.add))
                ts(CX[:, 0:4], CX[:, 0:4], 1.0 / P, EPS, ALU.mult, ALU.add).then_inc(ogm, 1)
                dve.wait_ge(ogr, t + 1)
                V3 = VG[:, t, :].rearrange("p (h n) -> p h n", h=4)
                link(tt(out=V3, in0=V3, in1=bc(CX[:, 4:8], P), op=ALU.mult))
                tt(out=VG[:, t, :], in0=VG[:, t, :], in1=SR[:, t, :], op=ALU.mult).then_inc(ogs, 1)

            def add_residual(names):
                for j in range(4):
                    b = wait_full(dve, names[j])
                    r = tt(out=X[:, j // 2, 512 * (j % 2):512 * (j % 2) + 512], in0=X[:, j // 2, 512 * (j % 2):512 * (j % 2) + 512],
                           in1=b[:, :], op=ALU.add)
                    freed(r, names[j])
                v.memset(small[:, 59:60], 0.0).then_inc(x_ready, 1)

            def finish():
                dve.wait_ge(x_ready, min(STOP + 1, 5))
                v.tensor_copy(XN[:, :, :], X[:, :, :]).then_inc(fin_ready, 1)

            add_residual([f"y{j}" for j in range(4)])
            if STOP == 0:
                return finish()

            def cross_attention(l, base_u):
                for s in range(5):
                    if s < 4:
                        u = base_u + s
                        dve.wait_ge(s_full, u + 1)
                        v.tensor_reduce(nm(u), bank[4 + u % 2][:, :].rearrange("p (h w) -> p h w", h=2), AX, ALU.max,
                                        negate=True).then_inc(nm_ready, 1)
                    if s >= 1:
                        scale_probs(base_u + s - 1, None)
                add_residual([f"xy{l}_{j}" for j in range(4)])

            normalise(2, X)
            cross_attention(0, U_X0)
            if STOP == 1:
                return finish()
            normalise(3, X)
            dve.wait_ge(hth, 1)
            tt(out=HTL[:, :, :], in0=HT[:, :, :], in1=HTH[:, :, :].bitcast(F32), op=ALU.subtract).then_inc(htl, 1)

            def split_lo(c):
                n = FFN0_LOAD + c
                dve.wait_ge(hi_ready, c + 1)
                w = loads[n][1] * loads[n][2]
                tt(out=lo[c % CONV][:, 0:w], in0=ring[n % RING][:, 0:w], in1=hi[c % CONV][:, 0:w].bitcast(F32), op=ALU.subtract).then_inc(lo_ready, 1)

            def act0(u):
                for t in range(TT):
                    dve.wait_ge(f_e, 2 * u + t + 1)
                    tt(out=AB[t][:, 0:FU[u]], in0=AB[t][:, 0:FU[u]], in1=bank[2 * t + 1][:, 0:FU[u]], op=ALU.mult).then_inc(f_a, 1)

            def atl0(u):
                for t in range(TT):
                    dve.wait_ge(f_th, 2 * u + t + 1)
                    j = FU[u] // P
                    tt(out=ATL[t][:, 0:j, :].rearrange("p a b -> p (a b)"), in0=bank[2 * t][:, 0:FU[u]],
                       in1=ATH[t][:, 0:j, :].rearrange("p a b -> p (a b)").bitcast(F32), op=ALU.subtract).then_inc(f_tl, 1)

            for u in range(7):
                up, down = step_slots(ORDER0, 1, u)
                if u == 6:
                    for c in down:
                        split_lo(c)
                    continue
                for c in (up if u == 0 else up[len(up) // 2:]) + down:
                    split_lo(c)
                act0(u)
                if u < 5:
                    nxt = step_slots(ORDER0, 1, u + 1)[0]
                    for c in nxt[:len(nxt) // 2]:
                        split_lo(c)
                atl0(u)
            dve.wait_ge(conv_used, 33)
            for j in range(4):
                tt(out=X[:, j // 2, 512 * (j % 2):512 * (j % 2) + 512], in0=X[:, j // 2, 512 * (j % 2):512 * (j % 2) + 512],
                   in1=bank[4 + j][:, :], op=ALU.add)
            v.memset(small[:, 59:60], 0.0).then_inc(x_ready, 1)
            if STOP == 2:
                return finish()

            normalise(4, X)
            dve.wait_ge(r_e, 1)
            link(ts(small[0:1, 50:51], small[0:1, 53:54], -LAMBDA_INIT, None, ALU.add))
            tt(out=small[0:1, 50:51], in0=small[0:1, 50:51], in1=small[0:1, 52:53], op=ALU.subtract).then_inc(lams, 1)
            dve.wait_ge(bank_free[IDX["lam"] % 4], IDX["lam"] // 4 + 1)
            for s in range(17):
                if s < 16:
                    add_bias(U_D + s, s % 8, False)
                if s >= 1:
                    u = U_D + s - 1
                    dve.wait_ge(exp_done, u + 1)
                    w = width(u)
                    link(v.reciprocal(ls(u), ls(u)))
                    link(tt(out=ls(u)[:, 1:2], in0=ls(u)[:, 1:2], in1=small[:, 51:52], op=ALU.mult))
                    A0, A1 = TP[u % 3][:, 0, 0:w], TP[u % 3][:, 1, 0:w]
                    link(ts(A0, A0, ls(u)[:, 0:1], None, ALU.mult))
                    v.scalar_tensor_tensor(A0, A1, ls(u)[:, 1:2], A0, ALU.mult, ALU.add).then_inc(p_ready, 1)
            for t in range(TT):
                for hq in range(2):
                    o = IDX[f"od{t}{hq}"]
                    dve.wait_ge(bank_free[o % 4], o // 4 + 1)
                link(tt(out=SQ[:, :], in0=OD[:, t, :], in1=OD[:, t, :], op=ALU.mult))
                link(v.tensor_reduce(CX[:, 0:8], SQ[:, :].rearrange("p (h n) -> p h n", h=8), AX, ALU.add))
                ts(CX[:, 0:8], CX[:, 0:8], 1.0 / P, EPS, ALU.mult, ALU.add).then_inc(odm, 1)
                dve.wait_ge(odr, t + 1)
                V3 = OD[:, t, :].rearrange("p (h n) -> p h n", h=8)
                tt(out=V3, in0=V3, in1=bc(CX[:, 8:16], P), op=ALU.mult).then_inc(ods, 1)
            add_residual([f"dy{j}" for j in range(4)])
            if STOP == 3:
                return finish()
            normalise(5, X)
            cross_attention(1, U_X1)
            if STOP == 4:
                return finish()

            normalise(6, X)
            b = wait_full(dve, "lg")
            dve.wait_ge(pt_ready, 40)
            link(v.memset(SELT[:, :, :].bitcast(F32), 0.0))
            v.memset(WS[:, :], 0.0).then_inc(m_init, 1)
            dve.wait_ge(pool_const, 2)
            link(v.tensor_copy(iota_e[:, :, :], IOe[:, :, :]))
            link(v.tensor_copy(iota_s[:, :], IOf[:, :]))
            freed(v.tensor_copy(LG[:, :, :], b[:, 0:2 * NE].rearrange("p (t e) -> p t e", t=TT)), "lg")
            dve.wait_ge(bank_free[IDX["lg"] % 4], IDX["lg"] // 4 + 1)
            M1, M2, MI = CX[:, 0:2], CX[:, 2:4], CX[:, 4:6]
            for mx, oh in ((M1, O1), (M2, O2)):
                link(v.tensor_reduce(mx, LG[:, :, :], AX, ALU.max))
                link(tt(out=RA[:, :, :], in0=LG[:, :, :], in1=bc(mx, NE), op=ALU.is_equal))
                link(v.scalar_tensor_tensor(RB[:, :, :], RA[:, :, :], -64.0, iota_e[:, :, :], ALU.mult, ALU.add))
                link(v.tensor_reduce(MI, RB[:, :, :], AX, ALU.min))
                link(tt(out=oh[:, :, :], in0=RB[:, :, :], in1=bc(MI, NE), op=ALU.is_equal))
                if mx is M1:
                    link(v.scalar_tensor_tensor(LG[:, :, :], O1[:, :, :], -3e38, LG[:, :, :], ALU.mult, ALU.add))
            link(tt(out=RA[:, :, :], in0=O1[:, :, :], in1=O2[:, :, :], op=ALU.add))
            tt(out=small[:, 54:56], in0=M2, in1=M1, op=ALU.subtract).then_inc(e_ready, 1)
            v.memset(small[:, 58:59], 0.0).then_inc(ch_ready, 1)
            dve.wait_ge(r_e, 2)
            W1, W2_ = CX[:, 6:8], CX[:, 8:10]
            link(ts(W1, small[:, 56:58], 1.0, None, ALU.add))
            link(v.reciprocal(W1, W1))
            link(tt(out=W2_, in0=W1, in1=small[:, 56:58], op=ALU.mult))
            link(tt(out=O1[:, :, :], in0=O1[:, :, :], in1=bc(W1, NE), op=ALU.mult))
            link(tt(out=O2[:, :, :], in0=O2[:, :, :], in1=bc(W2_, NE), op=ALU.mult))
            for p in range(2):
                tt(out=COMB[:, NE * p:NE * p + NE, :].rearrange("p e t -> p t e"), in0=O1[:, :, :], in1=O2[:, :, :], op=ALU.add)
            link(v.memset(COMB[:, 16, :], 0.0))
            b = wait_full(dve, "rk")
            rank = b[:, 0:2 * NE].rearrange("p (t e) -> p t e", t=TT)
            for p in range(2):
                link(v.scalar_tensor_tensor(RB[:, :, :], rank, 1.0 - P * p, RA[:, :, :], ALU.add, ALU.mult))
                link(ts(POS[:, NE * p:NE * p + NE, :].rearrange("p e t -> p t e"), RB[:, :, :], -1.0, None, ALU.add))
            link(v.memset(POS[:, 16, :], -1.0))
            freed(v.tensor_reduce(CX[:, 10:11], b[:, 2 * NE:3 * NE], AX, ALU.max), "rk")
            dve.wait_ge(bank_free[IDX["rk"] % 4], IDX["rk"] // 4 + 1)
            ts(flag[:, :], CX[:, 10:11], float(P), None, ALU.is_gt).then_inc(flag_ready, 1)
            wait_full(dve, "rk")
            for nh in range(2):
                b = wait_full(dve, f"gb{nh}")
                cs = slice(512 * nh, 512 * nh + 512)
                for t in range(TT):
                    link(tt(out=XGH[:, t, cs], in0=XN[:, t, cs], in1=b[:, :], op=ALU.mult))
                    link(tt(out=XN[:, t, cs], in0=XN[:, t, cs], in1=b[:, :], op=ALU.mult))
                    r = tt(out=XGL[:, t, cs], in0=XN[:, t, cs], in1=XGH[:, t, cs].bitcast(F32), op=ALU.subtract)
                freed(r, f"gb{nh}")
            v.memset(small[:, 58:59], 0.0).then_inc(xg_ready, 1)
            if STOP == 5:
                dve.wait_ge(m_ye, 1)
                return finish()
            link(v.memset(small[:, 59:60], 0.0))
            v.memset(small[:, 59:60], 0.0).then_inc(m_tl, 2)
            v.memset(small[:, 60:61], 0.0).then_inc(m_a, 2)

            def select(i):
                v.tensor_copy(PSI[:, :], POS[:, i, :])
                link(v.tensor_copy(CBI[:, :], COMB[:, i, :]))
                for t in range(TT):
                    ts(SEL[:, t, :], iota_s[:, :], PSI[:, t:t + 1], None, ALU.is_equal)
                    r = ts(SELR[:, t, :], iota_s[:, :], PSI[:, t:t + 1], None, ALU.is_equal)
                r.then_inc(sel_ready, 1)

            def gather_lo(past):
                dve.wait_ge(hgh, past + 1)
                for half in range(2):
                    r = tt(out=HGL[:, 4 * half:4 * half + 4, :].rearrange("p a b -> p (a b)"), in0=bank[6 + half][:, :],
                           in1=HGH[:, 4 * half:4 * half + 4, :].rearrange("p a b -> p (a b)").bitcast(F32), op=ALU.subtract)
                r.then_inc(hgl, 1)

            def result_lo(it):
                dve.wait_ge(m_ye, it + 2)
                for nh in range(2):
                    r = v.scalar_tensor_tensor(YEL[:, 512 * nh:512 * nh + 512], bank[4 + nh][:, :], WS[:, :],
                                               YEH[:, 512 * nh:512 * nh + 512].bitcast(F32), ALU.mult, ALU.subtract)
                r.then_inc(m_yl, 1)

            def scatter_add(it):
                for k in range(4):
                    dve.wait_ge(sc_full, it * 4 + (k + 1))
                    xs = X[:, k // 2, 512 * (k % 2):512 * (k % 2) + 512]
                    tt(out=xs, in0=xs, in1=bank[6 + k % 2][:, :], op=ALU.add).then_inc(sc_add, 1)

            def expert(i, past):
                it = i + past if past else i

                def split_lo_m(k):
                    dve.wait_ge(hi_ready, it * 33 + (33 + k + 1))
                    tt(out=lo[k % CONV][:, :], in0=ring[k % RING][:, :], in1=hi[k % CONV][:, :].bitcast(F32),
                       op=ALU.subtract).then_inc(lo_ready, 1)

                for s in range(8):
                    up, down = step_slots(ORDERM, 2, s)
                    for k in up[:2]:
                        split_lo_m(k)
                    if s == 1:
                        scatter_add(it)
                    if s >= 2:
                        u = s - 2
                        dve.wait_ge(m_th, it * 6 + (u + 1))
                        j = FU[u] // P
                        tt(out=ATL[u % 2][:, 0:j, :].rearrange("p a b -> p (a b)"), in0=bank[2 * (u % 2)][:, 0:FU[u]],
                           in1=ATH[u % 2][:, 0:j, :].rearrange("p a b -> p (a b)").bitcast(F32), op=ALU.subtract).then_inc(m_tl, 1)
                    for k in up[2:3]:
                        split_lo_m(k)
                    if s == 0:
                        result_lo(it)
                    if 1 <= s < 7:
                        u = s - 1
                        dve.wait_ge(m_e, it * 6 + (u + 1))
                        tt(out=AB[u % 2][:, 0:FU[u]], in0=AB[u % 2][:, 0:FU[u]], in1=bank[2 * (u % 2) + 1][:, 0:FU[u]], op=ALU.mult).then_inc(m_a, 1)
                    for k in up[3:] + down:
                        split_lo_m(k)
                    if s == 4:
                        dve.wait_ge(st_full, it + 1)
                        select(it + 1)
                    if s == 6:
                        gather_lo(it + 1)

            select(0)
            gather_lo(0)
            start = chain.n
            with dve.Fori(0, NE) as i:
                chain.loop(i, 1)
                expert(i, 0)
                chain.loop_end()
            dve.wait_ge(flag_ready, 1)
            again = dve.value_load(flag[0:1, 0:1], min_val=0, max_val=1)
            with dve.If(again > 0):
                chain.n = start
                with dve.Fori(0, NE) as i:
                    chain.loop(i + NE, 1)
                    expert(i, NE)
                    chain.loop_end()
            result_lo(again * NE + NE)
            scatter_add(again * NE + NE)
            v.memset(small[:, 59:60], 0.0).then_inc(x_ready, 1)
            dve.wait_ge(ss_ready, 16)
            normalise(7, X)
            dve.wait_ge(xn_ready, 16)
            for t in range(TT):
                r = tt(out=XN[:, t, :], in0=XN[:, t, :], in1=FG[:, :], op=ALU.mult)
            r.then_inc(fin_ready, 1)

        @block.gpsimd
        def _(pool):
            g = nc.gpsimd
            g.memset(ident[:, :], 0.0).then_inc(ident_ready, 1)
            g.memset(ones[:, :], 1.0).then_inc(pool_chain, 1)
            pool.wait_ge(ident_ready, 1)
            g.affine_select(out=ident[:, :], in_=ident[:, :], compare_op=ALU.not_equal, fill=1.0, base=0, pattern=[[-1, P]],
                            channel_multiplier=1).then_inc(ident_ready, 1)
            g.iota(IOn[:, :], [[1, 256]], base=-P, channel_multiplier=-1)
            g.iota(IOc[:, :, :], [[-P, 2], [16, 16]], base=31, channel_multiplier=-1)
            g.iota(IOs[:, :], [[0, P]], base=0, channel_multiplier=1)
            g.iota(IOt[:, :], [[1, P]], base=0, channel_multiplier=0).then_inc(pool_const, 1)
            pool.wait_ge(pool_chain, 1)
            g.affine_select(out=U_strict[:, :], in_=ones[:, :], compare_op=ALU.is_gt, fill=0.0, base=0, pattern=[[1, P]],
                            channel_multiplier=-1)
            pool.wait_ge(dve_const, 1)
            g.affine_select(out=MKf[:, :, :], in_=MKf[:, :, :], compare_op=ALU.is_ge, fill=0.0, base=0, pattern=[[0, 8], [1, P]],
                            channel_multiplier=-1).then_inc(mk_ready, 1)
            g.affine_select(out=NB[:, :, :], in_=NB[:, :, :], compare_op=ALU.is_ge, fill=NEG, base=P, pattern=[[0, 8], [-1, 256]],
                            channel_multiplier=1)
            g.affine_select(out=CB[:, :, :], in_=CB[:, :, :], compare_op=ALU.is_ge, fill=NEG, base=-31,
                            pattern=[[P, 2], [0, 8], [-16, 16]], channel_multiplier=1)
            g.affine_select(out=CM[:, :, :], in_=CM[:, :, :], compare_op=ALU.is_ge, fill=0.0, base=-31,
                            pattern=[[P, 2], [-16, 16]], channel_multiplier=1).then_inc(nb_ready, 1)

            def root(n):
                pool.wait_ge(ms_ready, n + 1)
                g.tensor_tensor(out=rstd[:, 0:2], in0=small[:, 16 + 2 * n:18 + 2 * n], in1=halfneg[:, 0:2], op=ALU.pow).then_inc(rstd_ready, 1)

            root(0)
            root(1)
            for m in range(8):
                pool.wait_ge(el_ready, m + 1)
                if m >= 2:
                    pool.wait_ge(gl_full, 2 * m)
                g.tensor_tensor(out=KL[m % 2][:, :, :], in0=KG[:, :, :], in1=EL[m % 2][:, :, :], op=ALU.mult).then_inc(kl_ready, 1)
            for t in range(TT):
                pool.wait_ge(ogm, t + 1)
                g.tensor_tensor(out=CX[:, 4:8], in0=CX[:, 0:4], in1=halfneg[:, 0:4], op=ALU.pow).then_inc(ogr, 1)
            if STOP >= 1:
                root(2)
            if STOP >= 2:
                root(3)
            if STOP >= 3:
                root(4)
                for t in range(TT):
                    pool.wait_ge(odm, t + 1)
                    g.tensor_tensor(out=CX[:, 8:16], in0=CX[:, 0:8], in1=halfneg[:, 0:8], op=ALU.pow).then_inc(odr, 1)
            if STOP >= 4:
                root(5)
            if STOP >= 5:
                root(6)
                g.iota(IOe[:, :, :], [[0, TT], [1, NE]], base=0, channel_multiplier=0)
                g.iota(IOf[:, :], [[1, P]], base=0, channel_multiplier=0).then_inc(pool_const, 1)
            if STOP >= 6:
                root(7)


_INS = ["x", "mem", "mix_norm_0", "w_in_0", "gla_w_alpha_0", "gla_b_alpha_0", "gla_out_norm_0", "nsa_cmp_pos_k_0",
        "nsa_cmp_w1_k_0", "nsa_cmp_w2_k_0", "nsa_cmp_pos_v_0", "nsa_cmp_w1_v_0", "nsa_cmp_w2_v_0", "w_out_0",
        "xattn_norm_0", "xattn_mem_norm_0", "xattn_wq_0", "xattn_wk_0", "xattn_wv_0", "xattn_wo_0", "ffn_norm_0",
        "ffn_w_gate_0", "ffn_w_up_0", "ffn_w_down_0", "mix_norm_1", "w_in_1", "diff_lq1_1", "diff_lk1_1", "diff_lq2_1",
        "diff_lk2_1", "diff_out_norm_1", "w_out_1", "xattn_norm_1", "xattn_mem_norm_1", "xattn_wq_1", "xattn_wk_1",
        "xattn_wv_1", "xattn_wo_1", "ffn_norm_1", "moe_router_1", "moe_w_gate_1", "moe_w_up_1", "moe_w_down_1",
        "final_norm"]


def kernel(**inputs):
    import numpy as np
    import concourse.bacc as bacc
    from concourse.bass_utils import run_bass_kernel_spmd as run

    nc = bacc.Bacc("TRN2", target_bir_lowering=False, num_devices=1)
    arrays, aps = {}, {}
    for name in _INS:
        arr = np.ascontiguousarray(inputs[name])
        arrays[f"in_{name}"] = arr
        aps[name] = nc.dram_tensor(f"in_{name}", arr.shape, mybir.dt.from_np(arr.dtype), kind="ExternalInput").ap()
    out = nc.dram_tensor("out", (1, 256, D), F32, kind="ExternalOutput").ap()
    build(nc, aps, out, UPTO)
    return run(nc, [arrays], core_ids=[0]).results[0]["out"]
```

```python
import math
from contextlib import ExitStack

import concourse.bass as bass
from concourse import mybir

F32 = mybir.dt.float32
F32R = mybir.dt.float32r
I32 = mybir.dt.int32
U8 = mybir.dt.uint8
ALU = mybir.AluOpType
ACT = mybir.ActivationFunctionType
AX = mybir.AxisListType.X

P = 128
D = 1024
DC = D // P
TT = 2
EPS = 1e-6
NEG = -1e30
TINY = 1e-30
SLOPES = [2.0 ** -(h + 1) for h in range(8)]
UPTO = 6
LAMBDA_INIT = 0.8 - 0.6 * math.exp(-0.3 * 1)
FF = 2816
FU = [512] * 5 + [256]
NE = 8
CMP = 15
RING = 11
CONV = 3
W0 = dict(q=0, k=256, v=512, r=1024, a=1536, nq=1552, kc=2064, vc=2192, ks=2320, vs=2448, kw=2576, vw=2704,
          g=2832, end=2856)
CV = dict(mix0=0, xat0=8, xmem0=16, ffn0=24, mix1=32, xat1=40, xmem1=48, ffn1=56, posk=64, posv=80,
          balpha=96, glan=98, diffn=99, rows=100)

OUTS = (["ct"] + [f"memT{j}" for j in range(4)]
        + [f"{w}{l}{j}" for l in range(2) for w in ("km", "vm") for j in range(2)]
        + [f"h0_{j}" for j in range(4)]
        + ["a", "nq0", "nq1", "nq2", "nq3", "kc", "vc", "ks", "vs0", "vs1", "kw", "vw0", "vw1", "g0", "g1"]
        + ["gq0", "gq1", "gk0", "gk1", "gv0", "gv1", "gr0", "gr1", "z0", "z1"]
        + ["ck", "cv", "ckT", "cvT", "c2k", "c2v", "sc", "pct0", "pct1", "pct2", "pct3"]
        + [f"n{t}{hp}" for t in range(2) for hp in range(4)]
        + ["og0", "og1", "ogT0", "ogT1"]
        + [f"y{j}" for j in range(4)]
        + [f"h1_{j}" for j in range(4)] + ["xq0_0", "xq0_1"] + [f"xo0_{j}" for j in range(4)] + [f"xy0_{j}" for j in range(4)]
        + [f"h2_{j}" for j in range(4)]
        + [f"h3_{j}" for j in range(4)]
        + [f"d{w}{2 * hf + j}" for hf in range(2) for w in ("q1", "q2", "k1", "k2") for j in range(2)]
        + ["dv00", "dv10", "dv01", "dv11", "lam"]
        + ["od00", "od01", "odT00", "od10", "odT01", "od11", "odT10", "odT11"]
        + [f"dy{j}" for j in range(4)]
        + [f"h4_{j}" for j in range(4)] + ["xq1_0", "xq1_1"] + [f"xo1_{j}" for j in range(4)] + [f"xy1_{j}" for j in range(4)]
        + [f"h5_{j}" for j in range(4)] + ["lg", "rk", "gb0", "gb1"])
IDX = {n: i for i, n in enumerate(OUTS)}
assert len(IDX) == len(OUTS)

U_NSA, U_X0, U_D, U_X1 = 0, 16, 20, 36
FFN0_LOAD = 26
MOE_LOAD = 77


def ffn_order(first):
    lag = 1 if first else 2
    order = []
    for u in range(6 + lag):
        if u < 6:
            for kind in "ug":
                order += [(kind, u, h) for h in range(2 if u < 5 else 1)]
        if u >= lag:
            order += [("d", u - lag, h) for h in range(2 if u - lag < 5 else 1)]
    return order


ORDER0 = ffn_order(True)
ORDERM = ffn_order(False)
AT0 = {k: n for n, k in enumerate(ORDER0)}
ATM = {k: n for n, k in enumerate(ORDERM)}
assert len(ORDER0) == len(ORDERM) == 33 and (MOE_LOAD % RING, 33 % RING, 33 % CONV) == (0, 0, 0)


def build(nc, a, out, upto):
    ctx = ExitStack()
    with ctx:
        TOTAL = 207 * 1024 + 512
        arena_start = (nc.sbuf_base + 31) // 32 * 32
        arena = ctx.enter_context(nc.sbuf_tensor("arena", [P, TOTAL // 4], F32))
        base = arena_start

        def size(shape, dt=F32):
            n = 1 if dt == U8 else 4
            for s in shape[1:]:
                n *= s
            return (n + 31) // 32 * 32

        def region(start):
            def put(name, shape, dt=F32):
                off = put.pos
                put.pos += size(shape, dt)
                return nc.alloc_sbuf_tensor_at(name, shape, dt, offset=off)
            put.pos = start
            return put

        def sem(name):
            return ctx.enter_context(nc.semaphore(name))

        sb = region(base)
        ring = [sb(f"ring{i}", [P, 2048]) for i in range(RING)]
        conv_base = sb.pos
        hi = [sb(f"whi{i}", [P, 2048], F32R) for i in range(CONV)]
        lo = [sb(f"wlo{i}", [P, 2048], F32R) for i in range(CONV)]
        conv_end = sb.pos
        X = sb("X", [P, TT, D])
        xn_base = sb.pos
        XN = sb("XN", [P, TT, D])
        ht_base = sb.pos
        HT = sb("HT", [P, DC, 256])
        ident = sb("ident", [P, P])
        CT = sb("CT", [P, CV["rows"]])
        small = sb("small", [P, 64])
        U_strict = sb("U_strict", [P, P])
        ones = sb("ones", [P, P])
        halfneg = sb("halfneg", [P, 8])
        WR = sb("WR", [P, DC, NE])
        WA = sb("WA", [16, 256])
        ATa = sb("ATa", [16, 256])
        W2 = [sb(f"W2{w}", [P, 2, 64]) for w in "kv"]
        CM = sb("CM", [P, TT, 16])
        CX = sb("CX", [P, 32])
        rstd = sb("rstd", [P, 8])
        ot_base = sb.pos
        OT = sb("OT", [P, DC, 256])
        MK = sb("MK", [P, 8, P], U8)
        TP = [sb(f"TP{i}", [P, 2, 256]) for i in range(4)]
        PT = [sb(f"PT{i}", [P, 2, 2, P]) for i in range(4)]
        nb_base = sb.pos
        NB = sb("NB", [P, 8, 256])
        KM = [sb(f"KM{l}", [P, 2, 256]) for l in range(2)]
        VM = [sb(f"VM{l}", [P, 2, 256]) for l in range(2)]
        end = sb.pos
        assert end - base <= TOTAL, (end - base, TOTAL)
        lrow = PT[0][0:1, :, :, :].rearrange("p h a b -> p (h a b)")[:, 0:256].rearrange("p (w d) -> p w d", w=4)
        l0 = region(conv_base)
        QG, KG, LA, BG, EL1 = (l0(n, [P, 2, 256]) for n in ("QG", "KG", "LA", "BG", "EL1"))
        EL = [LA, EL1]
        VG, SR = (l0(n, [P, TT, 512]) for n in ("VG", "SR"))
        NQ = l0("NQ", [P, 4, 256])
        KS, KW = (l0(n, [P, 2, 256]) for n in ("KS", "KW"))
        VS, VW = (l0(n, [P, TT, P]) for n in ("VS", "VW"))
        r1 = region(l0.pos)
        T2 = [l0(f"T2{w}", [P, 2, 256]) for w in "kv"]
        QL = [r1(f"QL{i}", [P, 2, 256]) for i in range(2)]
        l0.pos = r1.pos
        RR = [l0(f"RR{w}", [P, 16, 2, CMP]) for w in "kv"]
        KL = [r1(f"KL{i}", [P, 2, 256]) for i in range(2)]
        l0.pos = r1.pos
        r2 = region(l0.pos)
        PCT = l0("PCT", [CMP, 16, P])
        PG = [r2(f"PG{i}", [P, 4, P]) for i in range(3)]
        GH = [l0(f"GH{w}", [P, 2, 2 * CMP]) for w in "kv"]
        KC = l0("KC", [P, 2 * CMP])
        VC = l0("VC", [CMP, 2, 64])
        GT = l0("GT", [P, TT, 24])
        PCC = l0("PCC", [P, 16, 16])
        CB = l0("CB", [P, 16, 16])
        assert l0.pos <= conv_end, (l0.pos - conv_end)
        li = region(conv_base)
        IOn = li("IOn", [P, 256], I32)
        IOc = li("IOc", [P, TT, 16], I32)
        IOs, IOt, IOx, IOy = (li(n, [P, P], I32) for n in ("IOs", "IOt", "IOx", "IOy"))
        MKf = li("MKf", [P, 8, P])
        QX = region(conv_base)("QX", [P, 2, 256])
        l1 = region(conv_base)
        QD = l1("QD", [P, 2, 4, 256])
        KD = l1("KD", [P, 2, 4, 256])
        VD = l1("VD", [P, TT, D])
        OD = l1("OD", [P, TT, D])
        SQ = l1("SQ", [P, D])
        grow = l1("grow", [1, 2, D])
        assert l1.pos <= conv_end
        f0 = region(ot_base)
        AB = [f0(f"AB{i}", [P, 512]) for i in range(2)]
        ATH = [f0(f"ATH{i}", [P, 4, P], F32R) for i in range(2)]
        ATL = [f0(f"ATL{i}", [P, 4, P], F32R) for i in range(2)]
        f1 = region(f0.pos)
        HTL = f1("HTL", [P, DC, 256], F32R)
        assert f1.pos <= nb_base
        XGH = region(ht_base)("XGH", [P, TT, D], F32R)
        XGL = region(xn_base)("XGL", [P, TT, D], F32R)
        HTH = region(xn_base)("HTH", [P, DC, 256], F32R)
        HGH = f0("HGH", [P, DC, P], F32R)
        HGL = f0("HGL", [P, DC, P], F32R)
        YEH = f0("YEH", [P, D], F32R)
        YEL = f0("YEL", [P, D], F32R)
        SEL = f0("SEL", [P, TT, P])
        SELR = f0("SELR", [P, TT, P], F32R)
        SELT = f0("SELT", [P, TT, P], F32R)
        FG = f0("FG", [P, D])
        POS = f0("POS", [P, 17, TT])
        COMB = f0("COMB", [P, 17, TT])
        CBI = f0("CBI", [P, TT])
        PSI = f0("PSI", [P, TT])
        LG, O1, O2, RA, RB = (f0(n, [P, TT, NE]) for n in ("LG", "O1", "O2", "RA", "RB"))
        iota_e = f0("iota_e", [P, TT, NE])
        iota_s = f0("iota_s", [P, P])
        WS = f0("WS", [P, 1])
        flag = f0("flag", [P, 1], I32)
        IOe = f0("IOe", [P, TT, NE], I32)
        IOf = f0("IOf", [P, P], I32)
        assert f0.pos <= end

        bank = [ctx.enter_context(nc.psum_tensor(f"bank{i}", [P, 512], F32)) for i in range(8)]

        landed = [sem(f"landed{i}") for i in range(RING)]
        slot_free = [sem(f"slot_free{i}") for i in range(RING)]
        bank_full = [sem(f"bank_full{i}") for i in range(4)]
        bank_free = [sem(f"bank_free{i}") for i in range(4)]
        x_in, mem_in, sv_in, small_in, grow_in, out_done = (
            sem(n) for n in ("x_in", "mem_in", "sv_in", "small_in", "grow_in", "out_done"))
        ident_ready, pool_const, nb_ready, mk_ready, pg_zero = (sem(n) for n in ("ident_ready", "pool_const", "nb_ready", "mk_ready", "pg_zero"))
        dve_const = sem("dve_const")
        pool_chain, dve_chain, act_chain, row_order = (sem(n) for n in ("pool_chain", "dve_chain", "act_chain", "row_order"))
        ss_ready, ms_ready, rstd_ready, xn_ready = (sem(n) for n in ("ss_ready", "ms_ready", "rstd_ready", "xn_ready"))
        act_ev, dve_ev = sem("act_ev"), sem("dve_ev")
        s_full, s_used, nm_ready, exp_done, p_ready, pt_full, pt_ready, pv_done = (
            sem(n) for n in ("s_full", "s_used", "nm_ready", "exp_done", "p_ready", "pt_full", "pt_ready", "pv_done"))
        r_ready, gh_ready, pc_ready = sem("r_ready"), sem("gh_ready"), sem("pc_ready")
        z_ready, e_ready, l_ready, b_ready, d_ready, el_ready, ql_ready, kl_ready, gl_full, gl_used = (
            sem(n) for n in ("z_ready", "e_ready", "l_ready", "b_ready", "d_ready", "el_ready", "ql_ready", "kl_ready", "gl_full", "gl_used"))
        pc_t, pc_e = sem("pc_t"), sem("pc_e")
        pg_done, ogm, ogr, ogs, lams = sem("pg_done"), sem("ogm"), sem("ogr"), sem("ogs"), sem("lams")
        er_ready, osq = sem("er_ready"), sem("osq")
        odm, odr, ods, odq = sem("odm"), sem("odr"), sem("ods"), sem("odq")
        hi_ready, lo_ready, conv_used = sem("hi_ready"), sem("lo_ready"), sem("conv_used")
        f_full, f_e, f_a, f_t, f_th, f_tl, f_y = (sem(n) for n in ("f_full", "f_e", "f_a", "f_t", "f_th", "f_tl", "f_y"))
        hth = sem("hth")
        m_full, m_e, m_a, m_t, m_th, m_tl = (sem(n) for n in ("m_full", "m_e", "m_a", "m_t", "m_th", "m_tl"))
        m_y, m_ye, m_yl, sc_full, sc_add, st_full, st_done, ga_full, hgh, hgl, sel_ready = (
            sem(n) for n in ("m_y", "m_ye", "m_yl", "sc_full", "sc_add", "st_full", "st_done", "ga_full", "hgh", "hgl", "sel_ready"))
        r_e, ch_ready, flag_ready, m_init, xg_ready, fin_ready, x_ready = (
            sem(n) for n in ("r_e", "ch_ready", "flag_ready", "m_init", "xg_ready", "fin_ready", "x_ready"))

        class Chain:

            def __init__(self, eng, s):
                self.eng, self.s, self.n, self.it, self.per = eng, s, 0, None, 0

            def link(self, ins):
                self.n += 1
                ins.then_inc(self.s, 1)
                self.eng.wait_ge(self.s, self.n if self.it is None else self.it * self.per + self.n)

            def loop(self, it, per):
                self.it, self.per, self.start = it, per, self.n

            def loop_end(self):
                assert self.n - self.start == self.per, (self.n - self.start, self.per)
                self.it = None

        def wcols(w, c0, c1, r0=0, r1=D):
            return w[r0:r1, c0:c1].rearrange("(c p) n -> p c n", p=P)

        def slot(n, c, w):
            return ring[n % RING][:, 0:c * w].rearrange("p (c n) -> p c n", c=c)

        loads = []
        for l in range(2):
            loads += [(wcols(a[f"xattn_wk_{l}"], 0, 256), 8, 256), (wcols(a[f"xattn_wv_{l}"], 0, 256), 8, 256)]
        w_in0 = a["w_in_0"]
        NSA_CUT = [W0["a"], W0["nq"] + 128, W0["nq"] + 384, W0["vc"], W0["vs"], W0["vw"], W0["end"]]
        for c0, c1 in zip(NSA_CUT, NSA_CUT[1:]):
            loads.append((wcols(w_in0, c0, c1), 8, c1 - c0))
        loads += [(wcols(w_in0, 0, 256), 8, 256), (wcols(w_in0, 256, 512), 8, 256)]
        for c in ("v", "r"):
            loads += [(wcols(w_in0, W0[c], W0[c] + 512, 512 * h, 512 * h + 512), 4, 512) for h in range(2)]
        for w in "kv":
            loads += [(wcols(a[f"nsa_cmp_w1_{w}_0"], 0, 256, 1024 * h, 1024 * h + 1024), 8, 256) for h in range(2)]
        loads += [(wcols(a["w_out_0"], 0, D, 256 * j, 256 * j + 256), 2, D) for j in range(4)]
        loads += [(wcols(a["xattn_wq_0"], 0, 256), 8, 256), (wcols(a["xattn_wo_0"], 0, D, 0, 256), 2, D)]
        assert len(loads) == FFN0_LOAD

        def ffn_load(kind, u, h, wg, wu, wd):
            c0, n = 512 * u, FU[u]
            if kind == "d":
                return wd[c0 + 256 * h:c0 + 256 * h + 256, :], 2, D
            w = wg if kind == "g" else wu
            if n == 512:
                return w[512 * h:512 * h + 512, c0:c0 + n], 4, 512
            return w[:, c0:c0 + n], 8, 256

        for k in ORDER0:
            src, c, w = ffn_load(*k, a["ffn_w_gate_0"], a["ffn_w_up_0"], a["ffn_w_down_0"])
            loads.append((src.rearrange("(c p) n -> p c n", p=P), c, w))
        DIFF_LOAD = len(loads)
        for hf in range(2):
            for w in range(4):
                loads.append((wcols(a["w_in_1"], 512 * w + 256 * hf, 512 * w + 256 * hf + 256), 8, 256))
        for half in range(2):
            for h in range(2):
                loads.append((wcols(a["w_in_1"], 2048 + 512 * half, 2560 + 512 * half, 512 * h, 512 * h + 512), 4, 512))
        loads += [(wcols(a["w_out_1"], 0, D, 256 * j, 256 * j + 256), 2, D) for j in range(4)]
        loads += [(wcols(a["xattn_wq_1"], 0, 256), 8, 256), (wcols(a["xattn_wo_1"], 0, D, 0, 256), 2, D)]
        assert len(loads) == MOE_LOAD

        def wait_landed(eng, n):
            eng.wait_ge(landed[n % RING], 16 * (n // RING + 1))

        def wait_full(eng, name):
            o = IDX[name]
            eng.wait_ge(bank_full[o % 4], o // 4 + 1)
            return bank[o % 4]

        def freed(ins, name):
            ins.then_inc(bank_free[IDX[name] % 4], 1)

        X_dram = a["x"].rearrange("b (t p) d -> p (b t) d", p=P)
        M_dram = a["mem"].rearrange("b (t p) d -> p (b t) d", p=P)
        O_dram = out.rearrange("b (t p) d -> p (b t) d", p=P)
        STOP = upto
        sv = TP[0][0:CV["rows"], 0, 0:P]
        block = ctx.enter_context(nc.Block())

        LAST = {0: "km01", 1: "vm01", 2: "km11", 3: "vm11", 4: "nq0", 5: "nq2", 6: "kc", 7: "ks", 8: "kw", 9: "g1",
                10: "gq1", 11: "gk1", 12: "gv1", 13: "gv1", 14: "gr1", 15: "gr1", 16: "ck", 17: "ck", 18: "cv", 19: "cv",
                20: "y3", 21: "y3", 22: "y3", 23: "y3", 24: "xq0_1", 25: "xy0_3"}
        for hf in range(2):
            for w, name in enumerate(("q1", "q2", "k1", "k2")):
                LAST[DIFF_LOAD + 4 * hf + w] = f"d{name}{2 * hf + 1}"
        for j in range(4):
            LAST[DIFF_LOAD + 8 + j] = ("dv10", "dv11")[j // 2]
            LAST[DIFF_LOAD + 12 + j] = "dy3"
        LAST[DIFF_LOAD + 16], LAST[DIFF_LOAD + 17] = "xq1_1", "xy1_3"

        def attn_pv_group(u):
            if u < U_X0:
                return f"n{u // 8}{u // 2 % 4}", u % 2 == 1
            if u < U_D:
                return f"xo0_{u - U_X0}", True
            if u < U_X1:
                return f"od{(u - U_D) // 8}{(u - U_D) // 4 % 2}", (u - U_D) % 4 == 3
            return f"xo1_{u - U_X1}", True

        PV_COUNT = [sum(not attn_pv_group(k)[1] for k in range(u + 1)) for u in range(40)]

        def wait_pv(eng, u):
            name, last = attn_pv_group(u)
            if last:
                wait_full(eng, name)
            else:
                eng.wait_ge(pv_done, PV_COUNT[u])

        def from_psum(u):
            return U_X0 <= u < U_D or u >= U_X1

        S_USED = [sum(not from_psum(k) for k in range(u + 1)) for u in range(40)]

        def width(u):
            if u < U_X0:
                return (P, 256)[u // 8]
            if U_D <= u < U_X1:
                return (P, 256)[(u - U_D) // 8]
            return 256

        @block.sync
        def _(sp):
            sp.dma_start(XN[:, :, :], M_dram).then_inc(mem_in, 16)
            for n, (src, c, w) in enumerate(loads):
                if n == 1:
                    sp.wait_ge(sv_in, 16 * 13)
                if n == 2:
                    sp.dma_start(X[:, :, :], X_dram).then_inc(x_in, 16)
                if n >= RING:
                    m = n - RING
                    if m in LAST:
                        wait_full(sp, LAST[m])
                    else:
                        sp.wait_ge(lo_ready, m - FFN0_LOAD + 1)
                sp.dma_start(slot(n, c, w), src).then_inc(landed[n % RING], 16)
                if STOP <= 3 and n == (23, 25, 58, 74)[STOP]:
                    break

            def expert_loads(i, past):
                for k, key in enumerate(ORDERM):
                    if k < RING:
                        wait_full(sp, LAST[MOE_LOAD - RING + k])
                    sp.wait_ge(lo_ready, 33 * i + (33 * past + 23 + k))
                    kind, u, h = key
                    c0, n = 512 * u, FU[u]
                    r0 = 0
                    if kind == "d":
                        src, r0, rn, c0, n, c = a["moe_w_down_1"], c0 + 256 * h, 256, 0, D, 2
                    elif n == 512:
                        src, r0, rn, c = (a["moe_w_gate_1"] if kind == "g" else a["moe_w_up_1"]), 512 * h, 512, 4
                    else:
                        src, rn, c = (a["moe_w_gate_1"] if kind == "g" else a["moe_w_up_1"]), D, 8
                    sp.dma_start(slot(k, c, n), src[i, r0:r0 + rn, c0:c0 + n].rearrange("(c p) n -> p c n", p=P))\
                      .then_inc(landed[k % RING], 16)

            if STOP > 5:
                with sp.Fori(0, NE) as i:
                    expert_loads(i, 0)
                sp.wait_ge(flag_ready, 1)
                again = sp.value_load(flag[0:1, 0:1], min_val=0, max_val=1)
                with sp.If(again > 0):
                    with sp.Fori(0, NE) as i:
                        expert_loads(i, NE)
            for t in range(TT):
                sp.wait_ge(fin_ready, t + 1)
                sp.dma_start(O_dram[:, t, :], XN[:, t, :]).then_inc(out_done, 16)
            sp.wait_ge(out_done, 32)

        @block.tensor
        def _(pe):
            mm, tr = nc.tensor.matmul, nc.tensor.transpose
            rows = Chain(pe, row_order)

            def open_out(name):
                o = IDX[name]
                if o >= 4:
                    pe.wait_ge(bank_free[o % 4], o // 4)
                return bank[o % 4]

            def full(ins, name):
                ins.then_inc(bank_full[IDX[name] % 4], 1)

            def wait_out(name):
                o = IDX[name]
                pe.wait_ge(bank_free[o % 4], o // 4 + 1)

            def norm_transposes(k):
                names = [f"memT{j}" if k == 0 else f"h{k - 1}_{j}" for j in range(4)]
                for t in range(TT):
                    pe.wait_ge(xn_ready, 2 * k + t + 1)
                    for j in range(4):
                        b = open_out(names[j]) if t == 0 else bank[IDX[names[j]] % 4]
                        for c in range(2):
                            r = tr(b[:, 256 * c + P * t:256 * c + P * t + P], XN[:, t, P * (2 * j + c):P * (2 * j + c) + P], ident[:, :])
                        if t == 1:
                            full(r, names[j])

            def project_T(name, n, c0, src, m=P):
                b = open_out(name)
                width_ = loads[n][2]
                w = slot(n, DC, width_)
                for c in range(DC):
                    r = mm(b[0:m, 0:256], w[:, c, c0:c0 + m], src[:, c, :], start=c == 0, stop=c == DC - 1)
                full(r, name)

            def project(name, n, c0, c1, t, src):
                b = open_out(name)
                w = slot(n, DC, loads[n][2])
                for c in range(DC):
                    r = mm(b[:, 0:c1 - c0], src[:, c, P * t:P * t + P], w[:, c, c0:c1], start=c == 0, stop=c == DC - 1)
                full(r, name)

            def project_wide(names, n):
                bs = [open_out(x) for x in names]
                for h in range(2):
                    wait_landed(pe, n + h)
                    w = slot(n + h, 4, 512)
                    for t in range(TT):
                        for c in range(4):
                            r = mm(bs[t][:, :], HT[:, 4 * h + c, P * t:P * t + P], w[:, c, :], start=h + c == 0, stop=h + c == 4)
                        if h == 1:
                            full(r, names[t])

            def project_out(names, n, chunks):
                bs = [open_out(x) for x in names]
                for j in range(chunks // 2):
                    wait_landed(pe, n + j)
                    w = slot(n + j, 2, D)
                    for t in range(TT):
                        for nh in range(2):
                            for c in range(2):
                                r = mm(bs[2 * t + nh][:, :], OT[:, 2 * j + c, P * t:P * t + P], w[:, c, 512 * nh:512 * nh + 512],
                                       start=j + c == 0, stop=2 * j + c == chunks - 1)
                            if j == chunks // 2 - 1:
                                full(r, names[2 * t + nh])

            def scores(u, pairs, between=None):
                if u >= 2 and from_psum(u - 2):
                    pe.wait_ge(exp_done, u - 1)
                elif u >= 2:
                    pe.wait_ge(s_used, S_USED[u - 2])
                b = bank[4 + u % 2]
                w = width(u)
                for k, (q, kk) in enumerate(pairs):
                    r = mm(b[:, w * k:w * k + w], q, kk, start=True, stop=True)
                    if k == 0 and u not in range(U_D, U_X1):
                        r.then_inc(row_order, 1)
                        rows.n += 1
                        if between is not None:
                            between()
                        pe.wait_ge(row_order, rows.n)
                r.then_inc(s_full, 1)

            def prob_transposes(u, halves):
                pe.wait_ge(p_ready, u + 1)
                if u >= 2:
                    pe.wait_ge(pt_ready, u - 1)
                b = bank[6 + u % 2]
                for hh in range(halves):
                    for kb in range(width(u) // P):
                        r = tr(b[:, 256 * hh + P * kb:256 * hh + P * kb + P], TP[u % 4][:, hh, P * kb:P * kb + P], ident[:, :])
                r.then_inc(pt_full, 1)

            def values_T(u, name, V, cols, first, last, extra=None):
                pe.wait_ge(pt_ready, u + 1)
                b = open_out(name) if first else bank[IDX[name] % 4]
                kbs = width(u) // P
                for hh in range(2):
                    for kb in range(kbs):
                        r = mm(b[64 * hh:64 * hh + 64, 0:P], V[:, kb, cols[hh]:cols[hh] + 64], PT[u % 4][:, hh, kb, :],
                               start=first and kb == 0, stop=last and extra is None and kb == kbs - 1)
                    if extra is not None:
                        r = mm(b[64 * hh:64 * hh + 64, 0:P], *extra[hh], start=False, stop=True)
                if last:
                    full(r, name)
                else:
                    r.then_inc(pv_done, 1)

            def cross_attention(l, n0, base_u):
                wait_out(f"h{(1, 4)[l]}_2")
                wait_out(f"h{(1, 4)[l]}_3")
                wait_landed(pe, n0)
                for j in range(2):
                    project_T(f"xq{l}_{j}", n0, P * j, HT)
                for s in range(7):
                    after = None if s < 2 else (lambda: prob_transposes(base_u + s - 2, 2))
                    if s < 4:
                        u = base_u + s
                        t, hp = s // 2, s % 2
                        if s < 2:
                            wait_out(f"xq{l}_{hp}")
                        scores(u, [(QX[64 * hh:64 * hh + 64, hp, P * t:P * t + P], KM[l][64 * hh:64 * hh + 64, hp, :]) for hh in range(2)], after)
                    elif s < 6:
                        after()
                    if s >= 3:
                        k = s - 3
                        hp = k % 2
                        values_T(base_u + k, f"xo{l}_{k}", VM[l], [P * hp, P * hp + 64], True, True)
                wait_out(f"xo{l}_3")
                wait_out(f"xo{l}_2")
                project_out([f"xy{l}_{j}" for j in range(4)], n0 + 1, 2)

            pe.wait_ge(ident_ready, 2)
            pe.wait_ge(sv_in, 16 * 13)
            b = open_out("ct")
            full(tr(b[:, 0:CV["rows"]], sv, ident[0:CV["rows"], 0:CV["rows"]]), "ct")
            norm_transposes(0)
            wait_out("memT2")
            wait_out("memT3")
            for l, src in enumerate((HT, OT)):
                wait_landed(pe, 2 * l)
                for j in range(2):
                    project_T(f"km{l}{j}", 2 * l, P * j, src)
                wait_landed(pe, 2 * l + 1)
                for t in range(TT):
                    project(f"vm{l}{t}", 2 * l + 1, 0, 256, t, src)
            norm_transposes(1)
            wait_out("h0_2")
            wait_out("h0_3")
            wait_landed(pe, 4)
            project_T("a", 4, 0, HT, m=16)
            project_T("nq0", 4, 16, HT)
            wait_landed(pe, 5)
            project_T("nq1", 5, 0, HT)
            project_T("nq2", 5, P, HT)
            wait_landed(pe, 6)
            project_T("nq3", 6, 0, HT)
            project_T("kc", 6, P, HT)
            wait_landed(pe, 7)
            project_T("vc", 7, 0, HT)
            project_T("ks", 7, P, HT)
            wait_landed(pe, 8)
            for t in range(TT):
                project(f"vs{t}", 8, 0, P, t, HT)
            project_T("kw", 8, P, HT)
            wait_landed(pe, 9)
            for t in range(TT):
                project(f"vw{t}", 9, 0, P, t, HT)
            for t in range(TT):
                project(f"g{t}", 9, P, P + 24, t, HT)
            for k, w in enumerate(("gq", "gk")):
                wait_landed(pe, 10 + k)
                for j in range(2):
                    project_T(f"{w}{j}", 10 + k, P * j, HT)
            project_wide(["gv0", "gv1"], 12)
            project_wide(["gr0", "gr1"], 14)
            pe.wait_ge(small_in, 16 * 8)
            for j in range(2):
                b = open_out(f"z{j}")
                full(mm(b[:, 0:256], WA[:, P * j:P * j + P], ATa[:, :], start=True, stop=True), f"z{j}")
            for k, name in enumerate(("ck", "cv")):
                b = open_out(name)
                pe.wait_ge(r_ready, k + 1)
                for h in range(2):
                    wait_landed(pe, 16 + 2 * k + h)
                for m in range(16):
                    w = slot(16 + 2 * k + m // 8, 8, 256)
                    r = mm(b[0:30, 0:256], RR[k][:, m, :, :].rearrange("p g c -> p (g c)"), w[:, m % 8, :], start=m == 0, stop=m == 15)
                full(r, name)
            for k, name in enumerate(("ck", "cv")):
                b = open_out(name + "T")
                wait_out(name)
                for jh in range(2):
                    r = tr(b[:, 32 * jh:32 * jh + 30], XN[0:30, k, P * jh:P * jh + P], ident[0:30, 0:30])
                full(r, name + "T")
            b = open_out("c2k")
            wait_out("ckT")
            for half in range(2):
                for jh in range(2):
                    r = mm(b[64 * half:64 * half + 64, 0:30], W2[0][:, jh, :], GH[0][:, jh, :], start=jh == 0, stop=jh == 1)
            full(r, "c2k")
            b = open_out("c2v")
            wait_out("cvT")
            for g in range(2):
                for jh in range(2):
                    r = mm(b[0:CMP, 64 * g:64 * g + 64], GH[1][:, jh, CMP * g:CMP * g + CMP], W2[1][:, jh, :], start=jh == 0, stop=jh == 1)
            full(r, "c2v")
            b = open_out("sc")
            wait_out("c2k")
            for par in range(2):
                if par == 1:
                    rows.link(r)
                for t, h in [(t, h) for t in range(TT) for h in range(par, 8, 2)]:
                    p0 = 64 * (h % 2)
                    c0 = 16 * (8 * t + h)
                    r = mm(b[:, c0:c0 + CMP], NQ[p0:p0 + 64, h // 2, P * t:P * t + P], KC[p0:p0 + 64, CMP * (h // 4):CMP * (h // 4) + CMP],
                           start=True, stop=True)
            full(r, "sc")
            pe.wait_ge(pc_ready, 1)
            for j in range(4):
                b = open_out(f"pct{j}")
                for k in range(4):
                    r = tr(b[0:CMP, P * k:P * k + P], PCC[:, 4 * j + k, 0:CMP], ident[:, :])
                full(r, f"pct{j}")

            def nsa_unit(u):
                return u // 8, u // 2 % 4, u % 2

            for s in range(19):
                after = None if s < 2 else (lambda: prob_transposes(s - 2, 2))
                if s < 16:
                    t, hp, br = nsa_unit(s)
                    K = (KS, KW)[br]
                    scores(s, [(NQ[64 * hh:64 * hh + 64, hp, P * t:P * t + P], K[64 * hh:64 * hh + 64, hp // 2, 0:width(s)]) for hh in range(2)], after)
                elif s < 18:
                    after()
                if s >= 3:
                    t, hp, br = nsa_unit(s - 3)
                    g = hp // 2
                    if s == 3:
                        wait_out("pct3")
                    extra = [(VC[:, g, :], PCT[:, 8 * t + 2 * hp + hh, :]) for hh in range(2)] if br else None
                    values_T(s - 3, f"n{t}{hp}", (VS, VW)[br], [64 * g, 64 * g], br == 0, br == 1, extra)

            def gla_scores(k, lev, kt, qt, q, kk):
                if k >= 4:
                    pe.wait_ge(gl_used, k - 3)
                b = bank[4 + k % 4]
                for h in (0, 2, 1, 3):
                    p0 = 64 * (h % 2)
                    if h == 1:
                        rows.link(r)
                    r = mm(b[:, P * h:P * h + P], kk[p0:p0 + 64, h // 2, P * kt:P * kt + P], q[p0:p0 + 64, h // 2, P * qt:P * qt + P],
                           start=True, stop=True)
                r.then_inc(gl_full, 1)

            pe.wait_ge(pt_ready, 16)
            k = 0
            for t in range(TT):
                gla_scores(k, 0, t, t, QG, KG)
                k += 1
            for m in range(8):
                pe.wait_ge(ql_ready, m + 1)
                pe.wait_ge(kl_ready, m + 1)
                for t in range(TT if m < 7 else 1):
                    gla_scores(k, m, t, t if m < 7 else 1, QL[m % 2], KL[m % 2])
                    k += 1
            for t in range(TT):
                b = open_out(f"og{t}")
                if t == 0:
                    pe.wait_ge(pg_done, 3)
                for h in range(4):
                    r = mm(b[:, P * h:P * h + P], PG[t][:, h, :], VG[:, t, P * h:P * h + P], start=True, stop=t == 0)
                    if t == 1:
                        r = mm(b[:, P * h:P * h + P], PG[2][:, h, :], VG[:, 0, P * h:P * h + P], start=False, stop=True)
                full(r, f"og{t}")
            for t in range(TT):
                b = open_out(f"ogT{t}")
                pe.wait_ge(ogs, t + 1)
                for h in range(4):
                    r = tr(b[:, P * h:P * h + P], SR[:, t, P * h:P * h + P], ident[:, :])
                full(r, f"ogT{t}")
            wait_out("ogT0")
            wait_out("ogT1")
            project_out([f"y{j}" for j in range(4)], 20, 8)
            if STOP == 0:
                return
            norm_transposes(2)
            cross_attention(0, 24, U_X0)
            if STOP == 1:
                return
            norm_transposes(3)
            for j in range(4):
                wait_out(f"h2_{j}")

            def split_products(c, pairs, last):
                pe.wait_ge(lo_ready, c + 1)
                for b, ah, al, wsel, start, stop in pairs:
                    wh, wl = wsel(hi[c % CONV]), wsel(lo[c % CONV])
                    mm(b, ah, wh, start=start, stop=False)
                    mm(b, ah, wl, start=False, stop=False)
                    r = mm(b, al, wh, start=False, stop=stop)
                r.then_inc(conv_used, 1)

            def view(chunks, w, c, c0, c1):
                return lambda x: x[:, 0:chunks * w].rearrange("p (c n) -> p c n", c=chunks)[:, c, c0:c1]

            def transposes0(u):
                for t in range(TT):
                    pe.wait_ge(f_a, 2 * u + t + 1)
                    for j in range(FU[u] // P):
                        r = tr(bank[2 * t][:, P * j:P * j + P], AB[t][:, P * j:P * j + P], ident[:, :])
                    r.then_inc(f_t, 1)

            for u in range(7):
                if u < 6:
                    n = FU[u]
                    parts = 2 if n == 512 else 1
                    for kind, off in (("u", 1), ("g", 0)):
                        if u >= 1:
                            if kind == "u":
                                pe.wait_ge(f_a, 2 * u)
                            else:
                                pe.wait_ge(f_tl, 2 * u)
                        for h in range(parts):
                            ch = DC // parts
                            split_products(AT0[(kind, u, h)],
                                           [(bank[2 * t + off][:, 0:n], HTH[:, ch * h + c, P * t:P * t + P], HTL[:, ch * h + c, P * t:P * t + P],
                                             view(ch, n, c, 0, n), h + c == 0, h == parts - 1 and c == ch - 1)
                                            for t in range(TT) for c in range(ch)], False)
                if u >= 1:
                    v = u - 1
                    jn = FU[v] // P
                    pe.wait_ge(f_tl, 2 * v + 2)
                    for h in range(jn // 2):
                        if u == 5 and h == 1:
                            transposes0(u)
                        split_products(AT0[("d", v, h)],
                                       [(bank[4 + 2 * t + nh][:, :], ATH[t][:, 2 * h + c, :], ATL[t][:, 2 * h + c, :],
                                         view(2, D, c, 512 * nh, 512 * nh + 512), v + h + c == 0, v == 5 and c == 1)
                                        for t in range(TT) for nh in range(2) for c in range(2)], False)
                if u < 5:
                    transposes0(u)
            if STOP == 2:
                return

            norm_transposes(4)
            wait_out("h3_2")
            wait_out("h3_3")
            for hf in range(2):
                for w, name in enumerate(("q1", "q2", "k1", "k2")):
                    wait_landed(pe, DIFF_LOAD + 4 * hf + w)
                    for j in range(2):
                        project_T(f"d{name}{2 * hf + j}", DIFF_LOAD + 4 * hf + w, P * j, HT)
            for half in range(2):
                project_wide([f"dv{t}{half}" for t in range(TT)], DIFF_LOAD + 8 + 2 * half)
            b = open_out("lam")
            pe.wait_ge(lams, 1)
            full(mm(b[:, 0:1], ones[0:1, :], small[0:1, 50:51], start=True, stop=True), "lam")
            def head_transposes(k):
                pe.wait_ge(ods, k + 1)
                name = f"odT{k // 2}{k % 2}"
                b = open_out(name)
                for j in range(4):
                    h = 4 * (k % 2) + j
                    r = tr(b[:, P * j:P * j + P], OD[:, k // 2, P * h:P * h + P], ident[:, :])
                full(r, name)

            for s in range(19):
                if s < 16:
                    t, h = s // 8, s % 8
                    p0 = 64 * (h % 2)
                    scores(U_D + s, [(QD[p0:p0 + 64, i, h // 2, P * t:P * t + P], KD[p0:p0 + 64, i, h // 2, 0:width(U_D + s)]) for i in range(2)])
                if 2 <= s < 18:
                    prob_transposes(U_D + s - 2, 1)
                if s >= 10 and s % 4 == 2:
                    head_transposes((s - 10) // 4)
                if s >= 3:
                    u = U_D + s - 3
                    t, h = (s - 3) // 8, (s - 3) % 8
                    name, last = attn_pv_group(u)
                    pe.wait_ge(pt_ready, u + 1)
                    b = open_out(name) if h % 4 == 0 else bank[IDX[name] % 4]
                    for kb in range(t + 1):
                        r = mm(b[:, P * (h % 4):P * (h % 4) + P], PT[u % 4][:, 0, kb, :], VD[:, kb, P * h:P * h + P], start=kb == 0, stop=kb == t)
                    if last:
                        full(r, name)
                    else:
                        r.then_inc(pv_done, 1)
            head_transposes(3)
            wait_out("odT10")
            wait_out("odT11")
            project_out([f"dy{j}" for j in range(4)], DIFF_LOAD + 12, 8)
            if STOP == 3:
                return
            norm_transposes(5)
            cross_attention(1, DIFF_LOAD + 16, U_X1)
            if STOP == 4:
                return

            norm_transposes(6)
            wait_out("h5_2")
            wait_out("h5_3")
            b = open_out("lg")
            for t in range(TT):
                for c in range(DC):
                    r = mm(b[:, NE * t:NE * t + NE], HT[:, c, P * t:P * t + P], WR[:, c, :], start=c == 0, stop=c == DC - 1)
            full(r, "lg")
            b = open_out("rk")
            pe.wait_ge(ch_ready, 1)
            CH = RA
            for t in range(TT):
                if t == 1:
                    mm(b[:, NE:2 * NE], ones[:, :], CH[:, 0, :], start=True, stop=False)
                r = mm(b[:, NE * t:NE * t + NE], U_strict[:, :], CH[:, t, :], start=t == 0, stop=True)
            for t in range(TT):
                r = mm(b[:, 2 * NE:3 * NE], ones[:, :], CH[:, t, :], start=t == 0, stop=t == 1)
            full(r, "rk")
            pe.wait_ge(grow_in, 32)
            for nh in range(2):
                b = open_out(f"gb{nh}")
                full(mm(b[:, :], ones[0:1, :], grow[0:1, 0, 512 * nh:512 * nh + 512], start=True, stop=True), f"gb{nh}")
            for nh in range(2):
                r = mm(bank[4 + nh][:, :], ones[0:1, :], grow[0:1, 1, 512 * nh:512 * nh + 512], start=True, stop=True)
            r.then_inc(m_y, 1)
            if STOP == 5:
                return

            def gather():
                for half in range(2):
                    b = bank[6 + half]
                    for c in range(4):
                        for t in range(TT):
                            cs = slice(P * (4 * half + c), P * (4 * half + c) + P)
                            mm(b[:, P * c:P * c + P], XGH[:, t, cs], SELR[:, t, :], start=t == 0, stop=False)
                            r = mm(b[:, P * c:P * c + P], XGL[:, t, cs], SELR[:, t, :], start=False, stop=t == 1)
                r.then_inc(ga_full, 1)

            def expert(i, past):
                it = i + past if past else i

                def unit_up(u):
                    n = FU[u]
                    parts = 2 if n == 512 else 1
                    ch = DC // parts
                    pe.wait_ge(m_a, it * 6 + (u + 1))
                    if u == 0:
                        pe.wait_ge(hgl, it + 1)
                    for off, kind in ((1, "u"), (0, "g")):
                        if kind == "g":
                            pe.wait_ge(m_tl, it * 6 + (u + 1))
                        for h in range(parts):
                            products(ATM[(kind, u, h)],
                                     [(bank[2 * (u % 2) + off][:, 0:n], HGH[:, ch * h + c, :], HGL[:, ch * h + c, :],
                                       view(ch, n, c, 0, n), h + c == 0, h == parts - 1 and c == ch - 1) for c in range(ch)])

                def products(k, pairs):
                    pe.wait_ge(lo_ready, it * 33 + (34 + k))
                    for b, ah, al, wsel, start, stop in pairs:
                        wh, wl = wsel(hi[k % CONV]), wsel(lo[k % CONV])
                        mm(b, ah, wh, start=start, stop=False)
                        mm(b, ah, wl, start=False, stop=False)
                        r = mm(b, al, wh, start=False, stop=stop)
                    r.then_inc(conv_used, 1)

                def unit_transposes(u):
                    pe.wait_ge(m_a, it * 6 + (u + 3))
                    for j in range(FU[u] // P):
                        r = tr(bank[2 * (u % 2)][:, P * j:P * j + P], AB[u % 2][:, P * j:P * j + P], ident[:, :])
                    r.then_inc(m_t, 1)

                def unit_down(u):
                    pe.wait_ge(m_tl, it * 6 + (u + 3))
                    if u == 0:
                        pe.wait_ge(m_yl, it + 1)
                    jn = FU[u] // P
                    for h in range(jn // 2):
                        products(ATM[("d", u, h)],
                                 [(bank[4 + nh][:, :], ATH[u % 2][:, 2 * h + c, :], ATL[u % 2][:, 2 * h + c, :],
                                   view(2, D, c, 512 * nh, 512 * nh + 512), u + h + c == 0, u == 5 and c == 1)
                                  for nh in range(2) for c in range(2)])

                for u in range(8):
                    if u < 6:
                        unit_up(u)
                    if u == 0:
                        scatter(it)
                    if u == 1:
                        pe.wait_ge(sc_add, it * 4 + 4)
                        for t in range(TT):
                            tr(bank[6][:, P * t:P * t + P], SEL[:, t, :], ident[:, :])
                        for t in range(TT):
                            r = mm(bank[6][:, 256:257], SEL[:, t, :], CBI[:, t:t + 1], start=t == 0, stop=t == 1)
                        r.then_inc(st_full, 1)
                    if u == 6:
                        pe.wait_ge(sel_ready, it + 2)
                        pe.wait_ge(st_done, it + 1)
                        gather()
                    if 1 <= u < 7:
                        unit_transposes(u - 1)
                    if u >= 2:
                        unit_down(u - 2)

            def scatter(it):
                pe.wait_ge(m_yl, it + 1)
                pe.wait_ge(hgl, it + 1)
                for k in range(4):
                    if k >= 2:
                        pe.wait_ge(sc_add, it * 4 + (k - 1))
                    cs = slice(512 * (k % 2), 512 * (k % 2) + 512)
                    mm(bank[6 + k % 2][:, :], SELT[:, k // 2, :], YEH[:, cs], start=True, stop=False)
                    r = mm(bank[6 + k % 2][:, :], SELT[:, k // 2, :], YEL[:, cs], start=False, stop=True)
                    r.then_inc(sc_full, 1)

            pe.wait_ge(xg_ready, 1)
            pe.wait_ge(sel_ready, 1)
            gather()
            with pe.Fori(0, NE) as i:
                expert(i, 0)
            pe.wait_ge(flag_ready, 1)
            again = pe.value_load(flag[0:1, 0:1], min_val=0, max_val=1)
            with pe.If(again > 0):
                with pe.Fori(0, NE) as i:
                    expert(i, NE)
            scatter(again * NE + NE)

        def step_slots(order, lag, s):
            up = [k for k, x in enumerate(order) if x[0] != "d" and x[1] == s]
            down = [k for k, x in enumerate(order) if x[0] == "d" and x[1] == s - lag]
            return up, down

        G2 = [NQ[:, 2 * t:2 * t + 2, :].rearrange("p a b -> p (a b)") for t in range(TT)]
        GAINS = ("mix0", "xat0", "ffn0", "mix1", "xat1", "ffn1")

        def nm(u, n=2):
            return small[:, 32 + 2 * (u % 4):32 + 2 * (u % 4) + n]

        def ls(u, n=2):
            return small[:, 40 + 2 * (u % 4):40 + 2 * (u % 4) + n]

        @block.scalar
        def _(act):
            af = nc.scalar.activation
            chain = Chain(act, act_chain)

            gains = (("mix0", "mix_norm_0"), ("xat0", "xattn_norm_0"), ("xmem0", "xattn_mem_norm_0"), ("ffn0", "ffn_norm_0"),
                     ("mix1", "mix_norm_1"), ("xat1", "xattn_norm_1"), ("xmem1", "xattn_mem_norm_1"), ("ffn1", "ffn_norm_1"),
                     ("balpha", "gla_b_alpha_0"), ("glan", "gla_out_norm_0"), ("diffn", "diff_out_norm_1"))
            for key, name in gains:
                src = a[name].rearrange("(r n) -> r n", n=P)
                act.dma_start(TP[0][CV[key]:CV[key] + src.shape[0], 0, 0:P], src).then_inc(sv_in, 16)
            for k, w in enumerate("kv"):
                act.dma_start(TP[0][CV["pos" + w]:CV["pos" + w] + 16, 0, 0:P],
                              a[f"nsa_cmp_pos_{w}_0"].rearrange("(m l) d -> m (l d)", l=2)).then_inc(sv_in, 16)
            def squares(n, src, junk):
                for t in range(TT):
                    if n >= 2:
                        act.wait_ge(x_ready, 2 * n - 3 + t)
                    af(junk(t), src[:, t, :], ACT.Square, accum_out=small[:, 2 * n + t:2 * n + t + 1]).then_inc(ss_ready, 1)

            def xsquares(n):
                squares(n, X, lambda t: XN[:, t, :])

            def out_norm(k):
                g = CV[GAINS[k]]
                for j in (0, 2):
                    b = wait_full(act, f"h{k}_{j}")
                    for c in range(2):
                        r = af(HT[:, 2 * j + c, :], b[:, 256 * c:256 * c + 256], ACT.Copy, scale=CT[:, g + 2 * j + c:g + 2 * j + c + 1])
                    freed(r, f"h{k}_{j}")

            def take(name, dst, src, func=ACT.Copy, scale=1.0, bias=None):
                b = wait_full(act, name)
                kw = {} if bias is None else {"bias": bias}
                freed(af(dst, src(b), func, scale=scale, **kw), name)

            def exps(u, from_psum, widths=None):
                act.wait_ge(nm_ready, u + 1)
                w = width(u)
                for k in range(2):
                    src = bank[4 + u % 2][:, w * k:w * k + w] if from_psum else TP[u % 4][:, k, 0:w]
                    if k == 0 and from_psum and u >= 4:
                        act.wait_ge(pt_full, u - 3)
                    r = af(TP[u % 4][:, k, 0:w], src, ACT.Exp, bias=nm(u)[:, k:k + 1], accum_out=ls(u)[:, k:k + 1])
                r.then_inc(exp_done, 1)

            def copy_pt(u, halves):
                act.wait_ge(pt_full, u + 1)
                if u >= 4:
                    wait_pv(act, u - 4)
                b = bank[6 + u % 2]
                w = width(u)
                if halves == 1:
                    r = af(PT[u % 4][:, 0, :, :].rearrange("p a b -> p (a b)")[:, 0:w], b[:, 0:w], ACT.Copy)
                else:
                    v = b[:, :].rearrange("p (h n) -> p h n", h=2)[:, :, 0:w]
                    r = af(PT[u % 4][:, :, :, :].rearrange("p h a b -> p h (a b)")[:, :, 0:w], v, ACT.Copy)
                r.then_inc(pt_ready, 1)

            def cross_attention(l, base_u, k):
                out_norm(k)
                for j in range(2):
                    take(f"xq{l}_{j}", QX[:, j, :], lambda b: b[:, 0:256], scale=0.125)
                for s in range(7):
                    if s < 4:
                        exps(base_u + s, True)
                    if 2 <= s < 6:
                        copy_pt(base_u + s - 2, 2)
                    if s >= 3:
                        q = s - 3
                        take(f"xo{l}_{q}", OT[:, q % 2, P * (q // 2):P * (q // 2) + P], lambda b: b[:, 0:P])

            act.wait_ge(mem_in, 16)
            squares(0, XN, lambda t: OT[:, 4 * t:4 * t + 4, :].rearrange("p a b -> p (a b)"))
            take("ct", CT[:, :], lambda b: b[:, 0:CV["rows"]])
            act.dma_start(WA[:, :], a["gla_w_alpha_0"]).then_inc(small_in, 16)
            for k, w in enumerate("kv"):
                act.dma_start(W2[k][:, :, :], a[f"nsa_cmp_w2_{w}_0"].rearrange("(c p) n -> p c n", p=P)).then_inc(small_in, 16)
            act.dma_start(WR[:, :, :], a["moe_router_1"].rearrange("(c p) n -> p c n", p=P)).then_inc(small_in, 16)
            for k, w in enumerate(("lq1", "lk1", "lq2", "lk2")):
                act.dma_start(lrow[:, k, :], a[f"diff_{w}_1"].rearrange("(a n) -> a n", a=1)).then_inc(small_in, 16)
            act.wait_ge(x_in, 16)
            squares(1, X, lambda t: HT[:, 4 * t:4 * t + 4, :].rearrange("p a b -> p (a b)"))
            act.wait_ge(bank_free[0], 1)
            act.wait_ge(ss_ready, 4)
            for j in (0, 2):
                b = wait_full(act, f"memT{j}")
                for l, dst in enumerate((HT, OT)):
                    for c in range(2):
                        g = CV[f"xmem{l}"] + 2 * j + c
                        r = af(dst[:, 2 * j + c, :], b[:, 256 * c:256 * c + 256], ACT.Copy, scale=CT[:, g:g + 1])
                freed(r, f"memT{j}")
            for l in range(2):
                for j in range(2):
                    take(f"km{l}{j}", KM[l][:, j, :], lambda b: b[:, 0:256])
                for t in range(2):
                    take(f"vm{l}{t}", VM[l][:, t, :], lambda b: b[:, 0:256])
            out_norm(0)
            take("a", ATa[:, :], lambda b: b[0:16, 0:256])

            def both_halves(name, dst, shift):
                b = wait_full(act, name)
                for half in range(2):
                    for g in range(2):
                        s = shift * half
                        r = af(dst[64 * half:64 * half + 64, g, 0:256 - s], b[64 * g:64 * g + 64, s:256], ACT.Copy)
                freed(r, name)

            for j in range(4):
                take(f"nq{j}", NQ[:, j, :], lambda b: b[:, 0:256], scale=0.125)
            both_halves("kc", T2[0], 1)
            both_halves("vc", T2[1], 1)
            both_halves("ks", KS, 0)
            for t in range(TT):
                take(f"vs{t}", VS[:, t, :], lambda b: b[:, 0:P])
            both_halves("kw", KW, 0)
            for t in range(TT):
                take(f"vw{t}", VW[:, t, :], lambda b: b[:, 0:P])
            for t in range(TT):
                take(f"g{t}", GT[:, t, :], lambda b: b[:, 0:24], func=ACT.Sigmoid)
            for j in range(2):
                take(f"gq{j}", QG[:, j, :], lambda b: b[:, 0:256], scale=0.125)
            for j in range(2):
                take(f"gk{j}", KG[:, j, :], lambda b: b[:, 0:256])
            for t in range(TT):
                take(f"gv{t}", VG[:, t, :], lambda b: b[:, :])
            for t in range(TT):
                take(f"gr{t}", SR[:, t, :], lambda b: b[:, :], func=ACT.Silu)
            for j in range(2):
                take(f"z{j}", LA[:, j, :], lambda b: b[:, 0:256], func=ACT.Identity, bias=CT[:, CV["balpha"] + j:CV["balpha"] + j + 1])
            act.wait_ge(z_ready, 1)
            chain.link(af(EL1[:, :, :], EL1[:, :, :], ACT.Exp, scale=-1.0))
            af(EL1[:, :, :], EL1[:, :, :], ACT.Ln, bias=1.0).then_inc(l_ready, 1)

            def decay(m):
                act.wait_ge(d_ready, m + 1)
                af(EL[m % 2][:, :, :], EL[m % 2][:, :, :], ACT.Exp, scale=-1.0).then_inc(el_ready, 1)

            decay(0)
            decay(1)
            for k, name in enumerate(("ck", "cv")):
                take(name, XN[0:30, k, 0:256], lambda b: b[0:30, 0:256], func=ACT.Gelu_apprx_tanh)
            for k, name in enumerate(("ckT", "cvT")):
                take(name, GH[k][:, :, :], lambda b: b[:, 0:64].rearrange("p (j n) -> p j n", j=2)[:, :, 0:30])
            take("c2k", KC[:, :], lambda b: b[:, 0:30])
            take("c2v", VC[:, :, :], lambda b: b[0:CMP, 0:P].rearrange("p (g d) -> p g d", g=2))
            act.wait_ge(pc_t, 1)
            af(PCC[:, :, 0:CMP], PCC[:, :, 0:CMP], ACT.Exp).then_inc(pc_e, 1)
            for j in range(4):
                take(f"pct{j}", PCT[:, 4 * j:4 * j + 4, :], lambda b: b[0:CMP, :].rearrange("p (a b) -> p a b", a=4))
            for s in range(19):
                if s < 16:
                    exps(s, False)
                if 2 <= s < 18:
                    copy_pt(s - 2, 2)
                if s >= 4 and s % 2 == 0:
                    k = (s - 4) // 2
                    take(f"n{k // 4}{k % 4}", OT[:, 4 + k % 4, P * (k // 4):P * (k // 4) + P], lambda b: b[:, 0:P])
            for m in range(2, 8):
                decay(m)
            for t in range(TT):
                b = wait_full(act, f"og{t}")
                af(G2[t], b[:, :], ACT.Square).then_inc(osq, 1)
            for t in range(TT):
                take(f"ogT{t}", OT[:, 0:4, P * t:P * t + P], lambda b: b[:, :].rearrange("p (a b) -> p a b", a=4),
                     scale=CT[:, CV["glan"]:CV["glan"] + 1])
            if STOP == 0:
                return
            xsquares(2)
            cross_attention(0, U_X0, 1)
            if STOP == 1:
                return
            xsquares(3)
            for j in range(4):
                b = wait_full(act, f"h2_{j}")
                if j == 0:
                    wait_full(act, "h2_3")
                for c in range(2):
                    g = CV["ffn0"] + 2 * j + c
                    r = af(HTH[:, 2 * j + c, :], b[:, 256 * c:256 * c + 256], ACT.Copy, scale=CT[:, g:g + 1])
                r.then_inc(hth, 1)

            def split_hi(c):
                n = FFN0_LOAD + c
                wait_landed(act, n)
                if c >= CONV:
                    act.wait_ge(conv_used, c - CONV + 1)
                w = loads[n][1] * loads[n][2]
                af(hi[c % CONV][:, 0:w], ring[n % RING][:, 0:w], ACT.Copy).then_inc(hi_ready, 1)

            def act0(u):
                act.wait_ge(conv_used, step_slots(ORDER0, 1, u)[0][-1] + 1)
                for t in range(TT):
                    af(AB[t][:, 0:FU[u]], bank[2 * t][:, 0:FU[u]], ACT.Silu).then_inc(f_e, 1)

            def ath0(u):
                for t in range(TT):
                    act.wait_ge(f_t, 2 * u + t + 1)
                    j = FU[u] // P
                    af(ATH[t][:, 0:j, :].rearrange("p a b -> p (a b)"), bank[2 * t][:, 0:FU[u]], ACT.Copy).then_inc(f_th, 1)

            for u in range(7):
                up, down = step_slots(ORDER0, 1, u)
                if u == 6:
                    for c in down:
                        split_hi(c)
                    continue
                for c in (up if u == 0 else up[len(up) // 2:]) + down:
                    split_hi(c)
                act0(u)
                if u < 5:
                    nxt = step_slots(ORDER0, 1, u + 1)[0]
                    for c in nxt[:len(nxt) // 2]:
                        split_hi(c)
                ath0(u)
            if STOP == 2:
                return

            act.wait_ge(conv_used, 33)
            if STOP > 4:
                act.dma_start(grow[:, 0, :], a["ffn_norm_1"].rearrange("(a n) -> a n", a=1)).then_inc(grow_in, 16)
                act.dma_start(grow[:, 1, :], a["final_norm"].rearrange("(a n) -> a n", a=1)).then_inc(grow_in, 16)
            xsquares(4)
            out_norm(3)
            for hf in range(2):
                for w, (name, dst) in enumerate((("q1", QD), ("q2", QD), ("k1", KD), ("k2", KD))):
                    for j in range(2):
                        take(f"d{name}{2 * hf + j}", dst[:, w % 2, 2 * hf + j, :], lambda b: b[:, 0:256], scale=0.125 if w < 2 else 1.0)
            for half in range(2):
                for t in range(TT):
                    take(f"dv{t}{half}", VD[:, t, 512 * half:512 * half + 512], lambda b: b[:, :])
            act.wait_ge(er_ready, 1)
            af(small[0:1, 52:54], small[0:1, 48:50], ACT.Exp).then_inc(r_e, 1)
            take("lam", small[:, 51:52], lambda b: b[:, 0:1])

            def head_copy(k):
                t, hq = k // 2, k % 2
                take(f"odT{t}{hq}", OT[:, 4 * hq:4 * hq + 4, P * t:P * t + P], lambda b: b[:, :].rearrange("p (a b) -> p a b", a=4),
                     scale=CT[:, CV["diffn"]:CV["diffn"] + 1])

            for s in range(20):
                if s < 16:
                    exps(U_D + s, False)
                if 2 <= s < 18:
                    copy_pt(U_D + s - 2, 1)
                if s >= 7 and s % 4 == 3:
                    k = (s - 7) // 4
                    take(f"od{k // 2}{k % 2}", OD[:, k // 2, 512 * (k % 2):512 * (k % 2) + 512], lambda b: b[:, :])
                if s >= 11 and s % 4 == 3:
                    head_copy((s - 11) // 4)
            head_copy(3)
            if STOP == 3:
                return
            xsquares(5)
            cross_attention(1, U_X1, 4)
            if STOP == 4:
                return
            xsquares(6)
            out_norm(5)
            act.wait_ge(e_ready, 1)
            af(small[:, 56:58], small[:, 54:56], ACT.Exp).then_inc(r_e, 1)
            act.wait_ge(m_y, 1)
            act.wait_ge(m_init, 1)
            for nh in range(2):
                r = af(FG[:, 512 * nh:512 * nh + 512], bank[4 + nh][:, :], ACT.Copy)
            r.then_inc(m_ye, 1)
            if STOP == 5:
                return

            def result_hi(it):
                act.wait_ge(conv_used, it * 33 + 33)
                for nh in range(2):
                    r = af(YEH[:, 512 * nh:512 * nh + 512], bank[4 + nh][:, :], ACT.Copy, scale=WS[:, :])
                r.then_inc(m_ye, 1)

            def gather_hi(past):
                act.wait_ge(ga_full, past + 1)
                for half in range(2):
                    r = af(HGH[:, 4 * half:4 * half + 4, :].rearrange("p a b -> p (a b)"), bank[6 + half][:, :], ACT.Copy)
                r.then_inc(hgh, 1)

            def expert(i, past):
                it = i + past if past else i

                def split_hi_m(k):
                    act.wait_ge(landed[k % RING], it * 48 + 16 * (MOE_LOAD // RING + k // RING + 1))
                    act.wait_ge(conv_used, it * 33 + (33 + k - CONV + 1))
                    kind, u, h = ORDERM[k]
                    af(hi[k % CONV][:, :], ring[k % RING][:, :], ACT.Copy).then_inc(hi_ready, 1)

                for s in range(8):
                    up, down = step_slots(ORDERM, 2, s)
                    for k in up[:2]:
                        split_hi_m(k)
                    if s >= 2:
                        u = s - 2
                        act.wait_ge(m_t, it * 6 + (u + 1))
                        af(ATH[u % 2][:, 0:FU[u] // P, :].rearrange("p a b -> p (a b)"), bank[2 * (u % 2)][:, 0:FU[u]], ACT.Copy).then_inc(m_th, 1)
                    for k in up[2:3]:
                        split_hi_m(k)
                    if s == 0:
                        result_hi(it)
                    if 1 <= s < 7:
                        u = s - 1
                        last_up = step_slots(ORDERM, 2, u)[0][-1]
                        act.wait_ge(conv_used, it * 33 + (33 + last_up + 1))
                        af(AB[u % 2][:, 0:FU[u]], bank[2 * (u % 2)][:, 0:FU[u]], ACT.Silu).then_inc(m_e, 1)
                    for k in up[3:] + down:
                        split_hi_m(k)
                    if s == 2:
                        act.wait_ge(st_full, it + 1)
                        af(SELT[:, :, :].rearrange("p a b -> p (a b)"), bank[6][:, 0:256], ACT.Copy)
                        af(WS[:, :], bank[6][:, 256:257], ACT.Copy).then_inc(st_done, 1)
                    if s == 6:
                        gather_hi(it + 1)

            act.wait_ge(xg_ready, 1)
            gather_hi(0)
            with act.Fori(0, NE) as i:
                expert(i, 0)
            act.wait_ge(flag_ready, 1)
            again = act.value_load(flag[0:1, 0:1], min_val=0, max_val=1)
            with act.If(again > 0):
                with act.Fori(0, NE) as i:
                    expert(i, NE)
            result_hi(again * NE + NE)
            act.wait_ge(xn_ready, 14)
            squares(7, X, lambda t: XN[:, t, :])

        @block.vector
        def _(dve):
            v = nc.vector
            chain = Chain(dve, dve_chain)
            link = chain.link
            tt, ts = v.tensor_tensor, v.tensor_scalar

            def bc(ap, n):
                return ap.unsqueeze(2).broadcast_to([ap.shape[0], ap.shape[1], n])

            def normalise(n, src):
                for t in range(TT):
                    dve.wait_ge(ss_ready, 2 * n + t + 1)
                    ts(small[:, 16 + 2 * n + t:17 + 2 * n + t], small[:, 2 * n + t:2 * n + t + 1], 1.0 / D, EPS,
                       ALU.mult, ALU.add).then_inc(ms_ready, 1)
                    dve.wait_ge(rstd_ready, 2 * n + t + 1)
                    if n < 7:
                        ts(XN[:, t, :], src[:, t, :], rstd[:, t:t + 1], None, ALU.mult).then_inc(xn_ready, 1)
                    else:
                        v.scalar_tensor_tensor(XN[:, t, :], src[:, t, :], rstd[:, t:t + 1], FG[:, :], ALU.mult, ALU.mult).then_inc(fin_ready, 1)

            def out_norm(k):
                for j in (1, 3):
                    b = wait_full(dve, f"h{k}_{j}")
                    for c in range(2):
                        g = CV[GAINS[k]] + 2 * j + c
                        r = ts(HT[:, 2 * j + c, :], b[:, 256 * c:256 * c + 256], CT[:, g:g + 1], None, ALU.mult)
                    freed(r, f"h{k}_{j}")

            dve.wait_ge(pool_const, 1)
            link(v.tensor_copy(NB[:, 7, :], IOn[:, :]))
            for h in range(7):
                r = ts(NB[:, h, :], NB[:, 7, :], SLOPES[h], None, ALU.mult)
            link(r)
            link(ts(NB[:, 7, :], NB[:, 7, :], SLOPES[7], None, ALU.mult))
            link(v.tensor_copy(CB[:, 7, :], IOc[:, 0, :]))
            link(v.tensor_copy(CB[:, 15, :], IOc[:, 1, :]))
            for t in range(TT):
                for h in range(7):
                    r = ts(CB[:, 8 * t + h, :], CB[:, 8 * t + 7, :], SLOPES[h], None, ALU.mult)
            link(r)
            for t in range(TT):
                r = ts(CB[:, 8 * t + 7, :], CB[:, 8 * t + 7, :], SLOPES[7], None, ALU.mult)
            link(r)
            link(v.memset(CM[:, :, :], 1.0))
            link(tt(out=IOx[:, :], in0=IOs[:, :], in1=IOt[:, :], op=ALU.bitwise_xor))
            for m in range(8):
                if m == 0:
                    ts(MKf[:, 0, :], IOx[:, :], 0, None, ALU.is_equal)
                else:
                    link(ts(IOy[:, :], IOx[:, :], m - 1, None, ALU.logical_shift_right))
                    link(ts(MKf[:, m, :], IOy[:, :], 1, None, ALU.is_equal))
            r = v.memset(halfneg[:, :], -0.5)
            r.then_inc(dve_const, 1)
            dve.wait_ge(mk_ready, 1)
            link(v.tensor_copy(MK[:, :, :], MKf[:, :, :]))

            dve.wait_ge(mem_in, 16)
            normalise(0, XN)
            dve.wait_ge(bank_free[0], 1)
            dve.wait_ge(ss_ready, 4)
            for j in (1, 3):
                b = wait_full(dve, f"memT{j}")
                for l, dst in enumerate((HT, OT)):
                    for c in range(2):
                        g = CV[f"xmem{l}"] + 2 * j + c
                        r = ts(dst[:, 2 * j + c, :], b[:, 256 * c:256 * c + 256], CT[:, g:g + 1], None, ALU.mult)
                freed(r, f"memT{j}")
            normalise(1, X)
            out_norm(0)
            dve.wait_ge(small_in, 16 * 8)
            link(ts(CT[:, CV["diffn"]:CV["diffn"] + 1], CT[:, CV["diffn"]:CV["diffn"] + 1], 1.0 - LAMBDA_INIT, None, ALU.mult))
            link(tt(out=lrow[:, 0::2, :], in0=lrow[:, 0::2, :], in1=lrow[:, 1::2, :], op=ALU.mult))
            v.tensor_reduce(small[0:1, 48:50], lrow[:, 0::2, :], AX, ALU.add).then_inc(er_ready, 1)
            for k, name in enumerate(("kc", "vc")):
                o = IDX[name]
                dve.wait_ge(bank_free[o % 4], o // 4 + 1)
                for g in range(2):
                    for mh in range(2):
                        src = T2[k][:, g, 16 * mh:16 * mh + 240].rearrange("p (c m) -> p m c", m=16)[:, 0::2, :]
                        pos = CT[:, CV["pos" + "kv"[k]] + 8 * mh:CV["pos" + "kv"[k]] + 8 * mh + 8]
                        r = tt(out=RR[k][:, 8 * mh:8 * mh + 8, g, :], in0=src, in1=bc(pos, CMP), op=ALU.add)
                r.then_inc(r_ready, 1)
            dve.wait_ge(bank_free[IDX["z1"] % 4], IDX["z1"] // 4 + 1)
            v.scalar_tensor_tensor(EL1[:, :, :], LA[:, :, :], -1.0, LA[:, :, :], ALU.mult, ALU.max).then_inc(z_ready, 1)
            dve.wait_ge(l_ready, 1)
            link(v.scalar_tensor_tensor(LA[:, :, :], LA[:, :, :], 0.0, EL1[:, :, :], ALU.min, ALU.subtract))
            link(ts(LA[:, :, :], LA[:, :, :], 1.0 / 16.0, None, ALU.mult))
            link(v.memset(EL1[:, :, :], 1.0))
            for j in range(2):
                r = v.tensor_tensor_scan(BG[:, j, :], EL1[:, j, :], LA[:, j, :], 0.0, ALU.mult, ALU.add)
            link(r)

            def distances(m):
                L = 1 << m
                if m >= 2:
                    dve.wait_ge(kl_ready, m - 1)
                    dve.wait_ge(ql_ready, m - 1)
                bv = BG[:, :, :].rearrange("p a (n l) -> p (a n) l", l=2 * L)
                ev = EL[m % 2][:, :, :].rearrange("p a (n l) -> p (a n) l", l=2 * L)
                ref = bv[:, :, L - 1:L].broadcast_to([P, 256 // L, 2 * L])
                link(tt(out=ev, in0=bv, in1=ref, op=ALU.subtract))
                v.scalar_tensor_tensor(EL[m % 2][:, :, :], EL[m % 2][:, :, :], -1.0, EL[m % 2][:, :, :], ALU.mult, ALU.max).then_inc(d_ready, 1)

            def decayed_queries(m):
                if m >= 2:
                    dve.wait_ge(gl_full, 2 * m)
                dve.wait_ge(el_ready, m + 1)
                tt(out=QL[m % 2][:, :, :], in0=QG[:, :, :], in1=EL[m % 2][:, :, :], op=ALU.mult).then_inc(ql_ready, 1)

            for m in range(2):
                distances(m)
            for m in range(2):
                decayed_queries(m)
            b = wait_full(dve, "sc")
            dve.wait_ge(nb_ready, 1)
            bs = b[:, 0:256].rearrange("p (h c) -> p h c", c=16)[:, :, 0:CMP]
            PC = PCC[:, :, 0:CMP]
            r = tt(out=PC, in0=bs, in1=CB[:, :, 0:CMP], op=ALU.add)
            freed(r, "sc")
            dve.wait_ge(bank_free[IDX["sc"] % 4], IDX["sc"] // 4 + 1)
            PM, PS = CX[:, 0:16], CX[:, 16:32]
            link(v.tensor_reduce(PM, PC, AX, ALU.max))
            tt(out=PC, in0=PC, in1=bc(PM, CMP), op=ALU.subtract).then_inc(pc_t, 1)
            dve.wait_ge(pc_e, 1)
            for t in range(TT):
                link(tt(out=PCC[:, 8 * t:8 * t + 8, 0:CMP], in0=PCC[:, 8 * t:8 * t + 8, 0:CMP],
                        in1=CM[:, t:t + 1, 0:CMP].broadcast_to([P, 8, CMP]), op=ALU.mult))
            link(v.tensor_reduce(PS, PC, AX, ALU.add))
            link(ts(PS, PS, TINY, None, ALU.max))
            link(v.reciprocal(PS, PS))
            o = IDX["g1"]
            dve.wait_ge(bank_free[o % 4], o // 4 + 1)
            link(tt(out=PS, in0=PS, in1=GT[:, :, :].rearrange("p t (h b) -> p (t h) b", b=3)[:, :, 0], op=ALU.mult))
            tt(out=PC, in0=PC, in1=bc(PS, CMP), op=ALU.mult).then_inc(pc_ready, 1)

            def add_bias(u, h0, step):
                dve.wait_ge(s_full, u + 1)
                if u >= 4:
                    dve.wait_ge(pt_full, u - 3)
                w = width(u)
                T = TP[u % 4][:, :, 0:w]
                bias = NB[:, h0:h0 + 2, 256 - w:256] if step else NB[:, h0:h0 + 1, 256 - w:256].broadcast_to([P, 2, w])
                tt(out=T, in0=bank[4 + u % 2][:, 0:2 * w].rearrange("p (h w) -> p h w", h=2), in1=bias, op=ALU.add).then_inc(s_used, 1)
                dve.wait_ge(s_used, S_USED[u])
                v.tensor_reduce(nm(u), T, AX, ALU.max, negate=True).then_inc(nm_ready, 1)

            def scale_probs(u, gate):
                dve.wait_ge(exp_done, u + 1)
                w = width(u)
                link(v.reciprocal(ls(u), ls(u)))
                if gate is not None:
                    link(tt(out=ls(u), in0=ls(u), in1=gate, op=ALU.mult))
                for k in range(2):
                    r = ts(TP[u % 4][:, k, 0:w], TP[u % 4][:, k, 0:w], ls(u)[:, k:k + 1], None, ALU.mult)
                r.then_inc(p_ready, 1)

            for s in range(17):
                if s < 16:
                    add_bias(s, 2 * (s // 2 % 4), True)
                if s >= 1:
                    t, hp, br = (s - 1) // 8, (s - 1) // 2 % 4, (s - 1) % 2
                    gate = GT[:, t, :].rearrange("p (h b) -> p h b", b=3)[:, 2 * hp:2 * hp + 2, 1 + br]
                    scale_probs(s - 1, gate)
            wait_full(dve, "n13")
            for t in range(3):
                r = v.memset(PG[t][:, :, :], 0.0)
            link(r)

            def take_scores(k, lev, dst):
                dve.wait_ge(gl_full, k + 1)
                if k >= 2:
                    dve.wait_ge(gl_used, k - 1)
                src = bank[4 + k % 4][:, :].rearrange("p (h n) -> p h n", h=4)
                if lev is None:
                    v.tensor_copy(dst[:, :, :], src).then_inc(gl_used, 1)
                else:
                    v.copy_predicated(dst[:, :, :], MK[:, lev:lev + 1, :].broadcast_to([P, 4, P]), src).then_inc(gl_used, 1)

            k = 0
            for m in range(10):
                if 2 <= m < 8:
                    distances(m)
                if m == 0:
                    for t in range(TT):
                        take_scores(k, 0, PG[t])
                        k += 1
                if m >= 2:
                    for t in range(TT if m < 9 else 1):
                        take_scores(k, m - 1 if m < 9 else None, PG[t] if m < 9 else PG[2])
                        k += 1
                if 2 <= m < 8:
                    decayed_queries(m)
            v.memset(small[:, 58:59], 0.0).then_inc(pg_done, 3)
            for t in range(TT):
                b = wait_full(dve, f"og{t}")
                dve.wait_ge(osq, t + 1)
                freed(tt(out=SR[:, t, :], in0=b[:, :], in1=SR[:, t, :], op=ALU.mult), f"og{t}")
                link(v.tensor_reduce(CX[:, 8 * t:8 * t + 4], G2[t].rearrange("p (h n) -> p h n", h=4), AX, ALU.add))
                ts(CX[:, 8 * t:8 * t + 4], CX[:, 8 * t:8 * t + 4], 1.0 / P, EPS, ALU.mult, ALU.add).then_inc(ogm, 1)
            for t in range(TT):
                dve.wait_ge(ogr, t + 1)
                V3 = SR[:, t, :].rearrange("p (h n) -> p h n", h=4)
                tt(out=V3, in0=V3, in1=bc(CX[:, 8 * t + 4:8 * t + 8], P), op=ALU.mult).then_inc(ogs, 1)

            def add_residual(names):
                for j in range(4):
                    b = wait_full(dve, names[j])
                    r = tt(out=X[:, j // 2, 512 * (j % 2):512 * (j % 2) + 512], in0=X[:, j // 2, 512 * (j % 2):512 * (j % 2) + 512],
                           in1=b[:, :], op=ALU.add)
                    freed(r, names[j])
                    if j % 2 == 1:
                        v.memset(small[:, 59 + j:60 + j], 0.0).then_inc(x_ready, 1)

            def finish():
                dve.wait_ge(x_ready, 2 * min(STOP + 1, 5))
                v.tensor_copy(XN[:, :, :], X[:, :, :]).then_inc(fin_ready, 2)

            add_residual([f"y{j}" for j in range(4)])
            if STOP == 0:
                return finish()

            def cross_attention(l, base_u):
                for s in range(5):
                    if s < 4:
                        u = base_u + s
                        dve.wait_ge(s_full, u + 1)
                        v.tensor_reduce(nm(u), bank[4 + u % 2][:, :].rearrange("p (h w) -> p h w", h=2), AX, ALU.max,
                                        negate=True).then_inc(nm_ready, 1)
                    if s >= 1:
                        scale_probs(base_u + s - 1, None)
                add_residual([f"xy{l}_{j}" for j in range(4)])

            normalise(2, X)
            out_norm(1)
            cross_attention(0, U_X0)
            if STOP == 1:
                return finish()
            normalise(3, X)
            for j in range(4):
                dve.wait_ge(hth, j + 1)
                b = wait_full(dve, f"h2_{j}")
                for c in range(2):
                    g = CV["ffn0"] + 2 * j + c
                    r = v.scalar_tensor_tensor(HTL[:, 2 * j + c, :], b[:, 256 * c:256 * c + 256], CT[:, g:g + 1],
                                               HTH[:, 2 * j + c, :].bitcast(F32), ALU.mult, ALU.subtract)
                freed(r, f"h2_{j}")

            def split_lo(c):
                n = FFN0_LOAD + c
                dve.wait_ge(hi_ready, c + 1)
                w = loads[n][1] * loads[n][2]
                tt(out=lo[c % CONV][:, 0:w], in0=ring[n % RING][:, 0:w], in1=hi[c % CONV][:, 0:w].bitcast(F32), op=ALU.subtract).then_inc(lo_ready, 1)

            def act0(u):
                for t in range(TT):
                    dve.wait_ge(f_e, 2 * u + t + 1)
                    tt(out=AB[t][:, 0:FU[u]], in0=AB[t][:, 0:FU[u]], in1=bank[2 * t + 1][:, 0:FU[u]], op=ALU.mult).then_inc(f_a, 1)

            def atl0(u):
                for t in range(TT):
                    dve.wait_ge(f_th, 2 * u + t + 1)
                    j = FU[u] // P
                    tt(out=ATL[t][:, 0:j, :].rearrange("p a b -> p (a b)"), in0=bank[2 * t][:, 0:FU[u]],
                       in1=ATH[t][:, 0:j, :].rearrange("p a b -> p (a b)").bitcast(F32), op=ALU.subtract).then_inc(f_tl, 1)

            for u in range(7):
                up, down = step_slots(ORDER0, 1, u)
                if u == 6:
                    for c in down:
                        split_lo(c)
                    continue
                for c in (up if u == 0 else up[len(up) // 2:]) + down:
                    split_lo(c)
                act0(u)
                if u < 5:
                    nxt = step_slots(ORDER0, 1, u + 1)[0]
                    for c in nxt[:len(nxt) // 2]:
                        split_lo(c)
                atl0(u)
            dve.wait_ge(conv_used, 33)
            for j in range(4):
                tt(out=X[:, j // 2, 512 * (j % 2):512 * (j % 2) + 512], in0=X[:, j // 2, 512 * (j % 2):512 * (j % 2) + 512],
                   in1=bank[4 + j][:, :], op=ALU.add)
                if j % 2 == 1:
                    v.memset(small[:, 59 + j:60 + j], 0.0).then_inc(x_ready, 1)
            if STOP == 2:
                return finish()

            normalise(4, X)
            out_norm(3)
            dve.wait_ge(r_e, 1)
            link(ts(small[0:1, 50:51], small[0:1, 53:54], -LAMBDA_INIT, None, ALU.add))
            tt(out=small[0:1, 50:51], in0=small[0:1, 50:51], in1=small[0:1, 52:53], op=ALU.subtract).then_inc(lams, 1)
            dve.wait_ge(bank_free[IDX["lam"] % 4], IDX["lam"] // 4 + 1)
            def head_squares(k):
                o = IDX[f"od{k // 2}{k % 2}"]
                dve.wait_ge(bank_free[o % 4], o // 4 + 1)
                V = OD[:, k // 2, 512 * (k % 2):512 * (k % 2) + 512]
                if k >= 1:
                    dve.wait_ge(odm, k)
                link(tt(out=SQ[:, 0:512], in0=V, in1=V, op=ALU.mult))
                link(v.tensor_reduce(CX[:, 0:4], SQ[:, 0:512].rearrange("p (h n) -> p h n", h=4), AX, ALU.add))
                ts(CX[:, 0:4], CX[:, 0:4], 1.0 / P, EPS, ALU.mult, ALU.add).then_inc(odm, 1)

            def head_norm(k):
                dve.wait_ge(odr, k + 1)
                V3 = OD[:, k // 2, 512 * (k % 2):512 * (k % 2) + 512].rearrange("p (h n) -> p h n", h=4)
                tt(out=V3, in0=V3, in1=bc(CX[:, 4:8], P), op=ALU.mult).then_inc(ods, 1)

            for s in range(22):
                if s < 16:
                    add_bias(U_D + s, s % 8, False)
                if s >= 8 and s % 4 == 0:
                    head_squares((s - 8) // 4)
                if s >= 9 and s % 4 == 1:
                    head_norm((s - 9) // 4)
                if 1 <= s < 17:
                    u = U_D + s - 1
                    dve.wait_ge(exp_done, u + 1)
                    w = width(u)
                    link(v.reciprocal(ls(u), ls(u)))
                    link(tt(out=ls(u)[:, 1:2], in0=ls(u)[:, 1:2], in1=small[:, 51:52], op=ALU.mult))
                    A0, A1 = TP[u % 4][:, 0, 0:w], TP[u % 4][:, 1, 0:w]
                    link(ts(A0, A0, ls(u)[:, 0:1], None, ALU.mult))
                    v.scalar_tensor_tensor(A0, A1, ls(u)[:, 1:2], A0, ALU.mult, ALU.add).then_inc(p_ready, 1)
            add_residual([f"dy{j}" for j in range(4)])
            if STOP == 3:
                return finish()
            normalise(5, X)
            out_norm(4)
            cross_attention(1, U_X1)
            if STOP == 4:
                return finish()

            normalise(6, X)
            out_norm(5)
            b = wait_full(dve, "lg")
            dve.wait_ge(pt_ready, 40)
            link(v.memset(SELT[:, :, :].bitcast(F32), 0.0))
            v.memset(WS[:, :], 0.0).then_inc(m_init, 1)
            dve.wait_ge(pool_const, 2)
            link(v.tensor_copy(iota_e[:, :, :], IOe[:, :, :]))
            link(v.tensor_copy(iota_s[:, :], IOf[:, :]))
            freed(v.tensor_copy(LG[:, :, :], b[:, 0:2 * NE].rearrange("p (t e) -> p t e", t=TT)), "lg")
            dve.wait_ge(bank_free[IDX["lg"] % 4], IDX["lg"] // 4 + 1)
            M1, M2, MI = CX[:, 0:2], CX[:, 2:4], CX[:, 4:6]
            for mx, oh in ((M1, O1), (M2, O2)):
                link(v.tensor_reduce(mx, LG[:, :, :], AX, ALU.max))
                link(tt(out=RA[:, :, :], in0=LG[:, :, :], in1=bc(mx, NE), op=ALU.is_equal))
                link(v.scalar_tensor_tensor(RB[:, :, :], RA[:, :, :], -64.0, iota_e[:, :, :], ALU.mult, ALU.add))
                link(v.tensor_reduce(MI, RB[:, :, :], AX, ALU.min))
                link(tt(out=oh[:, :, :], in0=RB[:, :, :], in1=bc(MI, NE), op=ALU.is_equal))
                if mx is M1:
                    link(v.scalar_tensor_tensor(LG[:, :, :], O1[:, :, :], -3e38, LG[:, :, :], ALU.mult, ALU.add))
            link(tt(out=RA[:, :, :], in0=O1[:, :, :], in1=O2[:, :, :], op=ALU.add))
            tt(out=small[:, 54:56], in0=M2, in1=M1, op=ALU.subtract).then_inc(e_ready, 1)
            v.memset(small[:, 58:59], 0.0).then_inc(ch_ready, 1)
            dve.wait_ge(r_e, 2)
            W1, W2_ = CX[:, 6:8], CX[:, 8:10]
            link(ts(W1, small[:, 56:58], 1.0, None, ALU.add))
            link(v.reciprocal(W1, W1))
            link(tt(out=W2_, in0=W1, in1=small[:, 56:58], op=ALU.mult))
            link(tt(out=O1[:, :, :], in0=O1[:, :, :], in1=bc(W1, NE), op=ALU.mult))
            link(tt(out=O2[:, :, :], in0=O2[:, :, :], in1=bc(W2_, NE), op=ALU.mult))
            for p in range(2):
                tt(out=COMB[:, NE * p:NE * p + NE, :].rearrange("p e t -> p t e"), in0=O1[:, :, :], in1=O2[:, :, :], op=ALU.add)
            link(v.memset(COMB[:, 16, :], 0.0))
            b = wait_full(dve, "rk")
            rank = b[:, 0:2 * NE].rearrange("p (t e) -> p t e", t=TT)
            for p in range(2):
                link(v.scalar_tensor_tensor(RB[:, :, :], rank, 1.0 - P * p, RA[:, :, :], ALU.add, ALU.mult))
                link(ts(POS[:, NE * p:NE * p + NE, :].rearrange("p e t -> p t e"), RB[:, :, :], -1.0, None, ALU.add))
            link(v.memset(POS[:, 16, :], -1.0))
            freed(v.tensor_reduce(CX[:, 10:11], b[:, 2 * NE:3 * NE], AX, ALU.max), "rk")
            dve.wait_ge(bank_free[IDX["rk"] % 4], IDX["rk"] // 4 + 1)
            ts(flag[:, :], CX[:, 10:11], float(P), None, ALU.is_gt).then_inc(flag_ready, 1)
            wait_full(dve, "rk")
            for nh in range(2):
                b = wait_full(dve, f"gb{nh}")
                cs = slice(512 * nh, 512 * nh + 512)
                for t in range(TT):
                    link(tt(out=XGH[:, t, cs], in0=XN[:, t, cs], in1=b[:, :], op=ALU.mult))
                    link(tt(out=XN[:, t, cs], in0=XN[:, t, cs], in1=b[:, :], op=ALU.mult))
                    r = tt(out=XGL[:, t, cs], in0=XN[:, t, cs], in1=XGH[:, t, cs].bitcast(F32), op=ALU.subtract)
                freed(r, f"gb{nh}")
            v.memset(small[:, 58:59], 0.0).then_inc(xg_ready, 1)
            if STOP == 5:
                dve.wait_ge(m_ye, 1)
                return finish()
            link(v.memset(small[:, 59:60], 0.0))
            v.memset(small[:, 59:60], 0.0).then_inc(m_tl, 2)
            v.memset(small[:, 60:61], 0.0).then_inc(m_a, 2)

            def select(i):
                v.tensor_copy(PSI[:, :], POS[:, i, :])
                link(v.tensor_copy(CBI[:, :], COMB[:, i, :]))
                for t in range(TT):
                    ts(SEL[:, t, :], iota_s[:, :], PSI[:, t:t + 1], None, ALU.is_equal)
                    r = ts(SELR[:, t, :], iota_s[:, :], PSI[:, t:t + 1], None, ALU.is_equal)
                r.then_inc(sel_ready, 1)

            def gather_lo(past):
                dve.wait_ge(hgh, past + 1)
                for half in range(2):
                    r = tt(out=HGL[:, 4 * half:4 * half + 4, :].rearrange("p a b -> p (a b)"), in0=bank[6 + half][:, :],
                           in1=HGH[:, 4 * half:4 * half + 4, :].rearrange("p a b -> p (a b)").bitcast(F32), op=ALU.subtract)
                r.then_inc(hgl, 1)

            def result_lo(it):
                dve.wait_ge(m_ye, it + 2)
                for nh in range(2):
                    r = v.scalar_tensor_tensor(YEL[:, 512 * nh:512 * nh + 512], bank[4 + nh][:, :], WS[:, :],
                                               YEH[:, 512 * nh:512 * nh + 512].bitcast(F32), ALU.mult, ALU.subtract)
                r.then_inc(m_yl, 1)

            def scatter_add(it, last=False):
                for k in range(4):
                    dve.wait_ge(sc_full, it * 4 + (k + 1))
                    xs = X[:, k // 2, 512 * (k % 2):512 * (k % 2) + 512]
                    tt(out=xs, in0=xs, in1=bank[6 + k % 2][:, :], op=ALU.add).then_inc(sc_add, 1)
                    if last and k % 2 == 1:
                        v.memset(small[:, 59 + k:60 + k], 0.0).then_inc(x_ready, 1)

            def expert(i, past):
                it = i + past if past else i

                def split_lo_m(k):
                    dve.wait_ge(hi_ready, it * 33 + (33 + k + 1))
                    tt(out=lo[k % CONV][:, :], in0=ring[k % RING][:, :], in1=hi[k % CONV][:, :].bitcast(F32),
                       op=ALU.subtract).then_inc(lo_ready, 1)

                for s in range(8):
                    up, down = step_slots(ORDERM, 2, s)
                    for k in up[:2]:
                        split_lo_m(k)
                    if s == 1:
                        scatter_add(it)
                    if s >= 2:
                        u = s - 2
                        dve.wait_ge(m_th, it * 6 + (u + 1))
                        j = FU[u] // P
                        tt(out=ATL[u % 2][:, 0:j, :].rearrange("p a b -> p (a b)"), in0=bank[2 * (u % 2)][:, 0:FU[u]],
                           in1=ATH[u % 2][:, 0:j, :].rearrange("p a b -> p (a b)").bitcast(F32), op=ALU.subtract).then_inc(m_tl, 1)
                    for k in up[2:3]:
                        split_lo_m(k)
                    if s == 0:
                        result_lo(it)
                    if 1 <= s < 7:
                        u = s - 1
                        dve.wait_ge(m_e, it * 6 + (u + 1))
                        tt(out=AB[u % 2][:, 0:FU[u]], in0=AB[u % 2][:, 0:FU[u]], in1=bank[2 * (u % 2) + 1][:, 0:FU[u]], op=ALU.mult).then_inc(m_a, 1)
                    for k in up[3:] + down:
                        split_lo_m(k)
                    if s == 4:
                        dve.wait_ge(st_full, it + 1)
                        select(it + 1)
                    if s == 6:
                        gather_lo(it + 1)

            select(0)
            gather_lo(0)
            start = chain.n
            with dve.Fori(0, NE) as i:
                chain.loop(i, 1)
                expert(i, 0)
                chain.loop_end()
            dve.wait_ge(flag_ready, 1)
            again = dve.value_load(flag[0:1, 0:1], min_val=0, max_val=1)
            with dve.If(again > 0):
                chain.n = start
                with dve.Fori(0, NE) as i:
                    chain.loop(i + NE, 1)
                    expert(i, NE)
                    chain.loop_end()
            result_lo(again * NE + NE)
            scatter_add(again * NE + NE, True)
            normalise(7, X)

        @block.gpsimd
        def _(pool):
            g = nc.gpsimd
            g.memset(ident[:, :], 0.0).then_inc(ident_ready, 1)
            g.memset(ones[:, :], 1.0).then_inc(pool_chain, 1)
            pool.wait_ge(ident_ready, 1)
            g.affine_select(out=ident[:, :], in_=ident[:, :], compare_op=ALU.not_equal, fill=1.0, base=0, pattern=[[-1, P]],
                            channel_multiplier=1).then_inc(ident_ready, 1)
            g.iota(IOn[:, :], [[1, 256]], base=-P, channel_multiplier=-1)
            g.iota(IOc[:, :, :], [[-P, 2], [16, 16]], base=31, channel_multiplier=-1)
            g.iota(IOs[:, :], [[0, P]], base=0, channel_multiplier=1)
            g.iota(IOt[:, :], [[1, P]], base=0, channel_multiplier=0).then_inc(pool_const, 1)
            pool.wait_ge(pool_chain, 1)
            g.affine_select(out=U_strict[:, :], in_=ones[:, :], compare_op=ALU.is_gt, fill=0.0, base=0, pattern=[[1, P]],
                            channel_multiplier=-1)
            pool.wait_ge(dve_const, 1)
            g.affine_select(out=MKf[:, :, :], in_=MKf[:, :, :], compare_op=ALU.is_ge, fill=0.0, base=0, pattern=[[0, 8], [1, P]],
                            channel_multiplier=-1).then_inc(mk_ready, 1)
            g.affine_select(out=NB[:, :, :], in_=NB[:, :, :], compare_op=ALU.is_ge, fill=NEG, base=P, pattern=[[0, 8], [-1, 256]],
                            channel_multiplier=1)
            g.affine_select(out=CB[:, :, :], in_=CB[:, :, :], compare_op=ALU.is_ge, fill=NEG, base=-31,
                            pattern=[[P, 2], [0, 8], [-16, 16]], channel_multiplier=1)
            g.affine_select(out=CM[:, :, :], in_=CM[:, :, :], compare_op=ALU.is_ge, fill=0.0, base=-31,
                            pattern=[[P, 2], [-16, 16]], channel_multiplier=1).then_inc(nb_ready, 1)

            def root(n):
                for t in range(TT):
                    pool.wait_ge(ms_ready, 2 * n + t + 1)
                    g.tensor_tensor(out=rstd[:, t:t + 1], in0=small[:, 16 + 2 * n + t:17 + 2 * n + t], in1=halfneg[:, 0:1],
                                    op=ALU.pow).then_inc(rstd_ready, 1)

            root(0)
            root(1)
            for m in range(8):
                pool.wait_ge(el_ready, m + 1)
                if m == 0:
                    wait_full(pool, "cv")
                if m >= 2:
                    pool.wait_ge(gl_full, 2 * m)
                g.tensor_tensor(out=KL[m % 2][:, :, :], in0=KG[:, :, :], in1=EL[m % 2][:, :, :], op=ALU.mult).then_inc(kl_ready, 1)
            for t in range(TT):
                pool.wait_ge(ogm, t + 1)
                g.tensor_tensor(out=CX[:, 8 * t + 4:8 * t + 8], in0=CX[:, 8 * t:8 * t + 4], in1=halfneg[:, 0:4], op=ALU.pow).then_inc(ogr, 1)
            if STOP >= 1:
                root(2)
            if STOP >= 2:
                root(3)
            if STOP >= 3:
                root(4)
                for k in range(4):
                    pool.wait_ge(odm, k + 1)
                    g.tensor_tensor(out=CX[:, 4:8], in0=CX[:, 0:4], in1=halfneg[:, 0:4], op=ALU.pow).then_inc(odr, 1)
            if STOP >= 4:
                root(5)
            if STOP >= 5:
                root(6)
                g.iota(IOe[:, :, :], [[0, TT], [1, NE]], base=0, channel_multiplier=0)
                g.iota(IOf[:, :], [[1, P]], base=0, channel_multiplier=0).then_inc(pool_const, 1)
            if STOP >= 6:
                root(7)


_INS = ["x", "mem", "mix_norm_0", "w_in_0", "gla_w_alpha_0", "gla_b_alpha_0", "gla_out_norm_0", "nsa_cmp_pos_k_0",
        "nsa_cmp_w1_k_0", "nsa_cmp_w2_k_0", "nsa_cmp_pos_v_0", "nsa_cmp_w1_v_0", "nsa_cmp_w2_v_0", "w_out_0",
        "xattn_norm_0", "xattn_mem_norm_0", "xattn_wq_0", "xattn_wk_0", "xattn_wv_0", "xattn_wo_0", "ffn_norm_0",
        "ffn_w_gate_0", "ffn_w_up_0", "ffn_w_down_0", "mix_norm_1", "w_in_1", "diff_lq1_1", "diff_lk1_1", "diff_lq2_1",
        "diff_lk2_1", "diff_out_norm_1", "w_out_1", "xattn_norm_1", "xattn_mem_norm_1", "xattn_wq_1", "xattn_wk_1",
        "xattn_wv_1", "xattn_wo_1", "ffn_norm_1", "moe_router_1", "moe_w_gate_1", "moe_w_up_1", "moe_w_down_1",
        "final_norm"]


def kernel(**inputs):
    import numpy as np
    import concourse.bacc as bacc
    from concourse.bass_utils import run_bass_kernel_spmd as run

    nc = bacc.Bacc("TRN2", target_bir_lowering=False, num_devices=1)
    arrays, aps = {}, {}
    for name in _INS:
        arr = np.ascontiguousarray(inputs[name])
        arrays[f"in_{name}"] = arr
        aps[name] = nc.dram_tensor(f"in_{name}", arr.shape, mybir.dt.from_np(arr.dtype), kind="ExternalInput").ap()
    out = nc.dram_tensor("out", (1, 256, D), F32, kind="ExternalOutput").ap()
    build(nc, aps, out, UPTO)
    return run(nc, [arrays], core_ids=[0]).results[0]["out"]
```

```python
import math
from contextlib import ExitStack

import concourse.bass as bass
from concourse import mybir

F32 = mybir.dt.float32
F32R = mybir.dt.float32r
I32 = mybir.dt.int32
U8 = mybir.dt.uint8
ALU = mybir.AluOpType
ACT = mybir.ActivationFunctionType
AX = mybir.AxisListType.X

P = 128
D = 1024
DC = D // P
TT = 2
EPS = 1e-6
NEG = -1e30
TINY = 1e-30
SLOPES = [2.0 ** -(h + 1) for h in range(8)]
LAMBDA_INIT = 0.8 - 0.6 * math.exp(-0.3 * 1)
FF = 2816
FU = [512] * 5 + [256]
NE = 8
CMP = 15
RING = 11
CONV = 3
W0 = dict(q=0, k=256, v=512, r=1024, a=1536, nq=1552, kc=2064, vc=2192, ks=2320, vs=2448, kw=2576, vw=2704,
          g=2832, end=2856)
CV = dict(mix0=0, xat0=8, xmem0=16, ffn0=24, mix1=32, xat1=40, xmem1=48, ffn1=56, posk=64, posv=80,
          balpha=96, glan=98, diffn=99, rows=100)

OUTS = (["ct"] + [f"memT{j}" for j in range(4)]
        + [f"{w}{l}{j}" for l in range(2) for w in ("km", "vm") for j in range(2)]
        + [f"h0_{j}" for j in range(4)]
        + ["a", "nq0", "nq1", "nq2", "nq3", "kc", "vc", "ks", "vs0", "vs1", "kw", "vw0", "vw1", "g0", "g1"]
        + ["gq0", "gq1", "gk0", "gk1", "gv0", "gv1", "gr0", "gr1", "z0", "z1"]
        + ["ck", "cv", "ckT", "cvT", "c2k", "c2v", "sc", "pct0", "pct1", "pct2", "pct3"]
        + [f"n{t}{hp}" for t in range(2) for hp in range(4)]
        + ["og0", "og1", "ogT0", "y0", "y1", "ogT1", "y2", "y3"]
        + [f"h1_{j}" for j in range(4)] + ["xq0_0", "xq0_1"] + [f"x{w}0_{2 * t + j}" for t in range(2) for w in "oy" for j in range(2)]
        + [f"h2_{j}" for j in range(4)]
        + [f"h3_{j}" for j in range(4)]
        + [f"d{w}{2 * hf + j}" for hf in range(2) for w in ("q1", "q2", "k1", "k2") for j in range(2)]
        + ["dv00", "dv10", "dv01", "dv11", "lam"]
        + ["od00", "od01", "odT00", "od10", "odT01", "od11", "odT10", "dy0", "dy1", "odT11", "dy2", "dy3"]
        + [f"h4_{j}" for j in range(4)] + ["xq1_0", "xq1_1"] + [f"x{w}1_{2 * t + j}" for t in range(2) for w in "oy" for j in range(2)]
        + [f"h5_{j}" for j in range(4)] + ["lg", "rk"])
IDX = {n: i for i, n in enumerate(OUTS)}
assert len(IDX) == len(OUTS)

U_NSA, U_X0, U_D, U_X1 = 0, 16, 20, 36
FFN0_LOAD = 26
MOE_LOAD = 77


def ffn_order(first):
    lag = 1 if first else 2
    order = []
    for u in range(6 + lag):
        if u < 6:
            for kind in "ug":
                order += [(kind, u, h) for h in range(2 if u < 5 else 1)]
        if u >= lag:
            order += [("d", u - lag, h) for h in range(2 if u - lag < 5 else 1)]
    return order


ORDER0 = ffn_order(True)
ORDERM = ffn_order(False)
AT0 = {k: n for n, k in enumerate(ORDER0)}
ATM = {k: n for n, k in enumerate(ORDERM)}
assert len(ORDER0) == len(ORDERM) == 33 and (MOE_LOAD % RING, 33 % RING, 33 % CONV) == (0, 0, 0)


def build(nc, a, out):
    ctx = ExitStack()
    with ctx:
        TOTAL = 207 * 1024 + 512
        arena_start = (nc.sbuf_base + 31) // 32 * 32
        arena = ctx.enter_context(nc.sbuf_tensor("arena", [P, TOTAL // 4], F32))
        base = arena_start

        def size(shape, dt=F32):
            n = 1 if dt == U8 else 4
            for s in shape[1:]:
                n *= s
            return (n + 31) // 32 * 32

        def region(start):
            def put(name, shape, dt=F32):
                off = put.pos
                put.pos += size(shape, dt)
                return nc.alloc_sbuf_tensor_at(name, shape, dt, offset=off)
            put.pos = start
            return put

        def sem(name):
            return ctx.enter_context(nc.semaphore(name))

        sb = region(base)
        ring = [sb(f"ring{i}", [P, 2048]) for i in range(RING)]
        conv_base = sb.pos
        hi = [sb(f"whi{i}", [P, 2048], F32R) for i in range(CONV)]
        lo = [sb(f"wlo{i}", [P, 2048], F32R) for i in range(CONV)]
        conv_end = sb.pos
        X = sb("X", [P, TT, D])
        xn_base = sb.pos
        XN = sb("XN", [P, TT, D])
        ht_base = sb.pos
        HT = sb("HT", [P, DC, 256])
        ident = sb("ident", [P, P])
        CT = sb("CT", [P, CV["rows"]])
        small = sb("small", [P, 64])
        U_strict = sb("U_strict", [P, P])
        ones = sb("ones", [P, P])
        halfneg = sb("halfneg", [P, 8])
        WR = sb("WR", [P, DC, NE])
        WA = sb("WA", [16, 256])
        ATa = sb("ATa", [16, 256])
        W2 = [sb(f"W2{w}", [P, 2, 64]) for w in "kv"]
        CM = sb("CM", [P, TT, 16])
        CX = sb("CX", [P, 32])
        rstd = sb("rstd", [P, 8])
        ot_base = sb.pos
        OT = sb("OT", [P, DC, 256])
        MK = sb("MK", [P, 8, P], U8)
        tp_base = sb.pos
        TP = [sb(f"TP{i}", [P, 2, 256]) for i in range(4)]
        pt_base = sb.pos
        PT = [sb(f"PT{i}", [P, 2, 2, P]) for i in range(4)]
        nb_base = sb.pos
        NB = sb("NB", [P, 8, 256])
        KM = [sb(f"KM{l}", [P, 2, 256]) for l in range(2)]
        VM = [sb(f"VM{l}", [P, 2, 256]) for l in range(2)]
        end = sb.pos
        assert end - base <= TOTAL, (end - base, TOTAL)
        lrow = PT[0][0:1, :, :, :].rearrange("p h a b -> p (h a b)")[:, 0:256].rearrange("p (w d) -> p w d", w=4)
        l0 = region(conv_base)
        QG, KG, LA, BG, EL1 = (l0(n, [P, 2, 256]) for n in ("QG", "KG", "LA", "BG", "EL1"))
        EL = [LA, EL1]
        VG, SR = (l0(n, [P, TT, 512]) for n in ("VG", "SR"))
        NQ = l0("NQ", [P, 4, 256])
        KS, KW = (l0(n, [P, 2, 256]) for n in ("KS", "KW"))
        VS, VW = (l0(n, [P, TT, P]) for n in ("VS", "VW"))
        r1 = region(l0.pos)
        T2 = [l0(f"T2{w}", [P, 2, 256]) for w in "kv"]
        QL = [r1(f"QL{i}", [P, 2, 256]) for i in range(2)]
        l0.pos = r1.pos
        RR = [l0(f"RR{w}", [P, 16, 2, CMP]) for w in "kv"]
        KL = [r1(f"KL{i}", [P, 2, 256]) for i in range(2)]
        l0.pos = r1.pos
        r2 = region(l0.pos)
        PCT = l0("PCT", [CMP, 16, P])
        PG, PGX = r2("PG", [P, TT, 4, P]), r2("PGX", [P, 4, P])
        GH = [l0(f"GH{w}", [P, 2, 2 * CMP]) for w in "kv"]
        KC = l0("KC", [P, 2 * CMP])
        VC = l0("VC", [CMP, 2, 64])
        GT = l0("GT", [P, TT, 24])
        PCC = l0("PCC", [P, 16, 16])
        CB = l0("CB", [P, 16, 16])
        assert l0.pos <= conv_end, (l0.pos - conv_end)
        li = region(conv_base)
        IOn = li("IOn", [P, 256], I32)
        IOc = li("IOc", [P, TT, 16], I32)
        IOs, IOt, IOx, IOy = (li(n, [P, P], I32) for n in ("IOs", "IOt", "IOx", "IOy"))
        MKf = li("MKf", [P, 8, P])
        QX = region(conv_base)("QX", [P, 2, 256])
        HTL1 = region(ot_base)("HTL1", [P, DC, 256], F32R)
        l1 = region(conv_base)
        QD = l1("QD", [P, 2, 4, 256])
        KD = l1("KD", [P, 2, 4, 256])
        VD = l1("VD", [P, TT, D])
        OD = l1("OD", [P, TT, D])
        SQ = l1("SQ", [P, D])
        grow = l1("grow", [1, D])
        assert l1.pos <= conv_end
        hi_d, lo_d = zip(*[(region(p)(f"dhi{i}", [P, 2048], F32R), region(q)(f"dlo{i}", [P, 2048], F32R))
                           for i, (p, q) in enumerate(((conv_base + 24576, conv_base + 32768), (conv_base + 40960, tp_base), (ht_base, pt_base)))])
        f0 = region(ot_base)
        AB = [f0(f"AB{i}", [P, 512]) for i in range(2)]
        ATH = [f0(f"ATH{i}", [P, 4, P], F32R) for i in range(2)]
        ATL = [f0(f"ATL{i}", [P, 4, P], F32R) for i in range(2)]
        f1 = region(f0.pos)
        HTL = f1("HTL", [P, DC, 256], F32R)
        assert f1.pos <= nb_base
        XGH = region(ht_base)("XGH", [P, TT, D], F32R)
        XGL = region(xn_base)("XGL", [P, TT, D], F32R)
        HTH = region(xn_base)("HTH", [P, DC, 256], F32R)
        HTR = region(conv_base)("HTR", [P, DC, 256])
        HGH = f0("HGH", [P, DC, P], F32R)
        HGL = f0("HGL", [P, DC, P], F32R)
        YEH = f0("YEH", [P, D], F32R)
        YEL = f0("YEL", [P, D], F32R)
        SEL = f0("SEL", [P, TT, P])
        SELR = f0("SELR", [P, TT, P], F32R)
        SELT = f0("SELT", [P, TT, P], F32R)
        FG = f0("FG", [P, D])
        POS = f0("POS", [P, 17, TT])
        COMB = f0("COMB", [P, 17, TT])
        CBI = f0("CBI", [P, TT])
        PSI = f0("PSI", [P, TT])
        LG, O1, O2, RA, RB = (f0(n, [P, TT, NE]) for n in ("LG", "O1", "O2", "RA", "RB"))
        iota_e = f0("iota_e", [P, TT, NE])
        iota_s = f0("iota_s", [P, P])
        WS = f0("WS", [P, 1])
        flag = f0("flag", [P, 1], I32)
        IOe = f0("IOe", [P, TT, NE], I32)
        IOf = f0("IOf", [P, P], I32)
        assert f0.pos <= end

        bank = [ctx.enter_context(nc.psum_tensor(f"bank{i}", [P, 512], F32)) for i in range(8)]

        landed = [sem(f"landed{i}") for i in range(RING)]
        slot_free = [sem(f"slot_free{i}") for i in range(RING)]
        bank_full = [sem(f"bank_full{i}") for i in range(4)]
        bank_free = [sem(f"bank_free{i}") for i in range(4)]
        x_in, mem_in, sv_in, small_in, grow_in, out_done = (
            sem(n) for n in ("x_in", "mem_in", "sv_in", "small_in", "grow_in", "out_done"))
        ident_ready, pool_const, nb_ready, mk_ready = (sem(n) for n in ("ident_ready", "pool_const", "nb_ready", "mk_ready"))
        dve_const = sem("dve_const")
        pool_chain, dve_chain, act_chain, row_order = (sem(n) for n in ("pool_chain", "dve_chain", "act_chain", "row_order"))
        ss_ready, ms_ready, rstd_ready, xn_ready = (sem(n) for n in ("ss_ready", "ms_ready", "rstd_ready", "xn_ready"))
        s_full, s_used, nm_ready, exp_done, p_ready, pt_full, pt_ready, pv_done = (
            sem(n) for n in ("s_full", "s_used", "nm_ready", "exp_done", "p_ready", "pt_full", "pt_ready", "pv_done"))
        r_ready, pc_ready = sem("r_ready"), sem("pc_ready")
        z_ready, e_ready, l_ready, b_ready, d_ready, el_ready, ql_ready, kl_ready, gl_full, gl_used = (
            sem(n) for n in ("z_ready", "e_ready", "l_ready", "b_ready", "d_ready", "el_ready", "ql_ready", "kl_ready", "gl_full", "gl_used"))
        pc_t, pc_e = sem("pc_t"), sem("pc_e")
        pg_done, ogm, ogr, ogs, lams = sem("pg_done"), sem("ogm"), sem("ogr"), sem("ogs"), sem("lams")
        er_ready, osq = sem("er_ready"), sem("osq")
        odm, odr, ods = sem("odm"), sem("odr"), sem("ods")
        hi_ready, lo_ready, conv_used = sem("hi_ready"), sem("lo_ready"), sem("conv_used")
        f_e, f_a, f_t, f_th, f_tl = (sem(n) for n in ("f_e", "f_a", "f_t", "f_th", "f_tl"))
        hth, xgh_ready = sem("hth"), sem("xgh_ready")
        m_e, m_a, m_t, m_th, m_tl = (sem(n) for n in ("m_e", "m_a", "m_t", "m_th", "m_tl"))
        m_y, m_ye, m_yl, sc_full, sc_add, st_full, st_done, ga_full, hgh, hgl, sel_ready = (
            sem(n) for n in ("m_y", "m_ye", "m_yl", "sc_full", "sc_add", "st_full", "st_done", "ga_full", "hgh", "hgl", "sel_ready"))
        r_e, ch_ready, flag_ready, m_init, xg_ready, fin_ready, x_ready = (
            sem(n) for n in ("r_e", "ch_ready", "flag_ready", "m_init", "xg_ready", "fin_ready", "x_ready"))

        class Chain:

            def __init__(self, eng, s):
                self.eng, self.s, self.n, self.it, self.per = eng, s, 0, None, 0

            def link(self, ins):
                self.n += 1
                ins.then_inc(self.s, 1)
                self.eng.wait_ge(self.s, self.n if self.it is None else self.it * self.per + self.n)

            def loop(self, it, per):
                self.it, self.per, self.start = it, per, self.n

            def loop_end(self):
                assert self.n - self.start == self.per, (self.n - self.start, self.per)
                self.it = None

        def wcols(w, c0, c1, r0=0, r1=D):
            return w[r0:r1, c0:c1].rearrange("(c p) n -> p c n", p=P)

        def slot(n, c, w):
            return ring[n % RING][:, 0:c * w].rearrange("p (c n) -> p c n", c=c)

        loads = []
        for l in range(2):
            loads += [(wcols(a[f"xattn_wk_{l}"], 0, 256), 8, 256), (wcols(a[f"xattn_wv_{l}"], 0, 256), 8, 256)]
        w_in0 = a["w_in_0"]
        NSA_CUT = [W0["a"], W0["nq"] + 128, W0["nq"] + 384, W0["vc"], W0["vs"], W0["vw"], W0["end"]]
        for c0, c1 in zip(NSA_CUT, NSA_CUT[1:]):
            loads.append((wcols(w_in0, c0, c1), 8, c1 - c0))
        loads += [(wcols(w_in0, 0, 256), 8, 256), (wcols(w_in0, 256, 512), 8, 256)]
        for c in ("v", "r"):
            loads += [(wcols(w_in0, W0[c], W0[c] + 512, 512 * h, 512 * h + 512), 4, 512) for h in range(2)]
        for w in "kv":
            loads += [(wcols(a[f"nsa_cmp_w1_{w}_0"], 0, 256, 1024 * h, 1024 * h + 1024), 8, 256) for h in range(2)]
        loads += [(wcols(a["w_out_0"], 0, D, 256 * j, 256 * j + 256), 2, D) for j in range(4)]
        loads += [(wcols(a["xattn_wq_0"], 0, 256), 8, 256), (wcols(a["xattn_wo_0"], 0, D, 0, 256), 2, D)]
        assert len(loads) == FFN0_LOAD

        def ffn_load(kind, u, h, wg, wu, wd):
            c0, n = 512 * u, FU[u]
            if kind == "d":
                return wd[c0 + 256 * h:c0 + 256 * h + 256, :], 2, D
            w = wg if kind == "g" else wu
            if n == 512:
                return w[512 * h:512 * h + 512, c0:c0 + n], 4, 512
            return w[:, c0:c0 + n], 8, 256

        for k in ORDER0:
            src, c, w = ffn_load(*k, a["ffn_w_gate_0"], a["ffn_w_up_0"], a["ffn_w_down_0"])
            loads.append((src.rearrange("(c p) n -> p c n", p=P), c, w))
        DIFF_LOAD = len(loads)
        for hf in range(2):
            for w in range(4):
                loads.append((wcols(a["w_in_1"], 512 * w + 256 * hf, 512 * w + 256 * hf + 256), 8, 256))
        for half in range(2):
            for h in range(2):
                loads.append((wcols(a["w_in_1"], 2048 + 512 * half, 2560 + 512 * half, 512 * h, 512 * h + 512), 4, 512))
        loads += [(wcols(a["w_out_1"], 0, D, 256 * j, 256 * j + 256), 2, D) for j in range(4)]
        loads += [(wcols(a["xattn_wq_1"], 0, 256), 8, 256), (wcols(a["xattn_wo_1"], 0, D, 0, 256), 2, D)]
        assert len(loads) == MOE_LOAD

        def wait_landed(eng, n):
            eng.wait_ge(landed[n % RING], 16 * (n // RING + 1))

        def wait_full(eng, name):
            o = IDX[name]
            eng.wait_ge(bank_full[o % 4], o // 4 + 1)
            return bank[o % 4]

        def freed(ins, name):
            ins.then_inc(bank_free[IDX[name] % 4], 1)

        X_dram = a["x"].rearrange("b (t p) d -> p (b t) d", p=P)
        M_dram = a["mem"].rearrange("b (t p) d -> p (b t) d", p=P)
        O_dram = out.rearrange("b (t p) d -> p (b t) d", p=P)
        sv = TP[0][0:CV["rows"], 0, 0:P]
        block = ctx.enter_context(nc.Block())

        LAST = {0: "km01", 1: "vm01", 2: "km11", 3: "vm11", 4: "nq0", 5: "nq2", 6: "kc", 7: "ks", 8: "kw", 9: "g1",
                10: "gq1", 11: "gk1", 12: "gv1", 13: "gv1", 14: "gr1", 15: "gr1", 16: "ck", 17: "ck", 18: "cv", 19: "cv",
                20: "y3", 21: "y3", 22: "y3", 23: "y3", 24: "xq0_1", 25: "xy0_3"}
        for hf in range(2):
            for w, name in enumerate(("q1", "q2", "k1", "k2")):
                LAST[DIFF_LOAD + 4 * hf + w] = f"d{name}{2 * hf + 1}"
        for j in range(4):
            LAST[DIFF_LOAD + 8 + j] = ("dv10", "dv11")[j // 2]
            LAST[DIFF_LOAD + 12 + j] = "dy3"
        LAST[DIFF_LOAD + 16], LAST[DIFF_LOAD + 17] = "xq1_1", "xy1_3"

        def attn_pv_group(u):
            if u < U_X0:
                return f"n{u // 8}{u // 2 % 4}", u % 2 == 1
            if u < U_D:
                return f"xo0_{u - U_X0}", True
            if u < U_X1:
                return f"od{(u - U_D) // 8}{(u - U_D) // 4 % 2}", (u - U_D) % 4 == 3
            return f"xo1_{u - U_X1}", True

        PV_COUNT = [sum(not attn_pv_group(k)[1] for k in range(u + 1)) for u in range(40)]

        def wait_pv(eng, u):
            name, last = attn_pv_group(u)
            if last:
                wait_full(eng, name)
            else:
                eng.wait_ge(pv_done, PV_COUNT[u])

        def from_psum(u):
            return U_X0 <= u < U_D or u >= U_X1

        S_USED = [sum(not from_psum(k) for k in range(u + 1)) for u in range(40)]

        def width(u):
            if u < U_X0:
                return (P, 256)[u // 8]
            if U_D <= u < U_X1:
                return (P, 256)[(u - U_D) // 8]
            return 256

        @block.sync
        def _(sp):
            sp.dma_start(XN[:, :, :], M_dram).then_inc(mem_in, 16)
            for n, (src, c, w) in enumerate(loads):
                if n == 1:
                    sp.wait_ge(sv_in, 16 * 13)
                if n == 2:
                    sp.dma_start(X[:, :, :], X_dram).then_inc(x_in, 16)
                if n == 6:
                    sp.dma_start(WA[:, :], a["gla_w_alpha_0"]).then_inc(small_in, 16)
                    for j, kv in enumerate("kv"):
                        sp.dma_start(W2[j][:, :, :], a[f"nsa_cmp_w2_{kv}_0"].rearrange("(c p) n -> p c n", p=P)).then_inc(small_in, 16)
                    sp.dma_start(WR[:, :, :], a["moe_router_1"].rearrange("(c p) n -> p c n", p=P)).then_inc(small_in, 16)
                    for j, vec in enumerate(("lq1", "lk1", "lq2", "lk2")):
                        sp.dma_start(lrow[:, j, :], a[f"diff_{vec}_1"].rearrange("(a n) -> a n", a=1)).then_inc(small_in, 16)
                if n >= RING:
                    m = n - RING
                    if m < FFN0_LOAD or m >= DIFF_LOAD + 12:
                        wait_full(sp, LAST[m])
                    else:
                        sp.wait_ge(lo_ready, m - FFN0_LOAD + 1)
                sp.dma_start(slot(n, c, w), src).then_inc(landed[n % RING], 16)

            def expert_loads(i, past):
                for k, key in enumerate(ORDERM):
                    if k < RING:
                        wait_full(sp, LAST[MOE_LOAD - RING + k])
                    sp.wait_ge(lo_ready, 33 * i + (33 * past + 35 + k))
                    kind, u, h = key
                    c0, n = 512 * u, FU[u]
                    r0 = 0
                    if kind == "d":
                        src, r0, rn, c0, n, c = a["moe_w_down_1"], c0 + 256 * h, 256, 0, D, 2
                    elif n == 512:
                        src, r0, rn, c = (a["moe_w_gate_1"] if kind == "g" else a["moe_w_up_1"]), 512 * h, 512, 4
                    else:
                        src, rn, c = (a["moe_w_gate_1"] if kind == "g" else a["moe_w_up_1"]), D, 8
                    sp.dma_start(slot(k, c, n), src[i, r0:r0 + rn, c0:c0 + n].rearrange("(c p) n -> p c n", p=P))\
                      .then_inc(landed[k % RING], 16)

            with sp.Fori(0, NE) as i:
                expert_loads(i, 0)
            sp.wait_ge(flag_ready, 1)
            again = sp.value_load(flag[0:1, 0:1], min_val=0, max_val=1)
            with sp.If(again > 0):
                with sp.Fori(0, NE) as i:
                    expert_loads(i, NE)
            for t in range(TT):
                sp.wait_ge(fin_ready, t + 1)
                sp.dma_start(O_dram[:, t, :], XN[:, t, :]).then_inc(out_done, 16)
            sp.wait_ge(out_done, 32)

        @block.tensor
        def _(pe):
            mm, tr = nc.tensor.matmul, nc.tensor.transpose
            rows = Chain(pe, row_order)

            def open_out(name):
                o = IDX[name]
                if o >= 4:
                    pe.wait_ge(bank_free[o % 4], o // 4)
                return bank[o % 4]

            def full(ins, name):
                ins.then_inc(bank_full[IDX[name] % 4], 1)

            def wait_out(name):
                o = IDX[name]
                pe.wait_ge(bank_free[o % 4], o // 4 + 1)

            def norm_transposes(k):
                names = [f"memT{j}" if k == 0 else f"h{k - 1}_{j}" for j in range(4)]
                for t in range(TT):
                    pe.wait_ge(xn_ready, 2 * k + t + 1)
                    for j in range(4):
                        b = open_out(names[j]) if t == 0 else bank[IDX[names[j]] % 4]
                        for c in range(2):
                            r = tr(b[:, 256 * c + P * t:256 * c + P * t + P], XN[:, t, P * (2 * j + c):P * (2 * j + c) + P], ident[:, :])
                        if t == 1:
                            full(r, names[j])

            def project_T(name, n, c0, src, m=P):
                b = open_out(name)
                width_ = loads[n][2]
                w = slot(n, DC, width_)
                for c in range(DC):
                    r = mm(b[0:m, 0:256], w[:, c, c0:c0 + m], src[:, c, :], start=c == 0, stop=c == DC - 1)
                full(r, name)

            def project(name, n, c0, c1, t, src):
                b = open_out(name)
                w = slot(n, DC, loads[n][2])
                for c in range(DC):
                    r = mm(b[:, 0:c1 - c0], src[:, c, P * t:P * t + P], w[:, c, c0:c1], start=c == 0, stop=c == DC - 1)
                full(r, name)

            def project_wide(names, n):
                bs = [open_out(x) for x in names]
                for h in range(2):
                    wait_landed(pe, n + h)
                    w = slot(n + h, 4, 512)
                    for t in range(TT):
                        for c in range(4):
                            r = mm(bs[t][:, :], HT[:, 4 * h + c, P * t:P * t + P], w[:, c, :], start=h + c == 0, stop=h + c == 4)
                        if h == 1:
                            full(r, names[t])

            def project_out(name, t, n, chunks):
                for nh in range(2):
                    b = open_out(f"{name}{2 * t + nh}")
                    for c in range(chunks):
                        wait_landed(pe, n + c // 2)
                        w = slot(n + c // 2, 2, D)
                        r = mm(b[:, :], OT[:, c, P * t:P * t + P], w[:, c % 2, 512 * nh:512 * nh + 512], start=c == 0, stop=c == chunks - 1)
                    full(r, f"{name}{2 * t + nh}")

            def scores(u, pairs, between=None):
                if u >= 2 and from_psum(u - 2):
                    pe.wait_ge(exp_done, u - 1)
                elif u >= 2:
                    pe.wait_ge(s_used, S_USED[u - 2])
                b = bank[4 + u % 2]
                w = width(u)
                for k, (q, kk) in enumerate(pairs):
                    r = mm(b[:, w * k:w * k + w], q, kk, start=True, stop=True)
                    if k == 0 and u not in range(U_D, U_X1):
                        r.then_inc(row_order, 1)
                        rows.n += 1
                        if between is not None:
                            between()
                        pe.wait_ge(row_order, rows.n)
                r.then_inc(s_full, 1)

            def prob_transposes(u, halves):
                pe.wait_ge(p_ready, u + 1)
                if u >= 2:
                    pe.wait_ge(pt_ready, u - 1)
                b = bank[6 + u % 2]
                for hh in range(halves):
                    for kb in range(width(u) // P):
                        r = tr(b[:, 256 * hh + P * kb:256 * hh + P * kb + P], TP[u % 4][:, hh, P * kb:P * kb + P], ident[:, :])
                r.then_inc(pt_full, 1)

            def values_T(u, name, V, cols, first, last, extra=None):
                pe.wait_ge(pt_ready, u + 1)
                b = open_out(name) if first else bank[IDX[name] % 4]
                kbs = width(u) // P
                for hh in range(2):
                    for kb in range(kbs):
                        r = mm(b[64 * hh:64 * hh + 64, 0:P], V[:, kb, cols[hh]:cols[hh] + 64], PT[u % 4][:, hh, kb, :],
                               start=first and kb == 0, stop=last and extra is None and kb == kbs - 1)
                    if extra is not None:
                        r = mm(b[64 * hh:64 * hh + 64, 0:P], *extra[hh], start=False, stop=True)
                if last:
                    full(r, name)
                else:
                    r.then_inc(pv_done, 1)

            def cross_attention(l, n0, base_u):
                wait_out(f"h{(1, 4)[l]}_2")
                wait_out(f"h{(1, 4)[l]}_3")
                wait_landed(pe, n0)
                for j in range(2):
                    project_T(f"xq{l}_{j}", n0, P * j, HT)
                for s in range(7):
                    after = None if s < 2 else (lambda: prob_transposes(base_u + s - 2, 2))
                    if s < 4:
                        u = base_u + s
                        t, hp = s // 2, s % 2
                        if s < 2:
                            wait_out(f"xq{l}_{hp}")
                        scores(u, [(QX[64 * hh:64 * hh + 64, hp, P * t:P * t + P], KM[l][64 * hh:64 * hh + 64, hp, :]) for hh in range(2)], after)
                    elif s < 6:
                        after()
                    if s == 5:
                        for j in range(2):
                            wait_out(f"xo{l}_{j}")
                        project_out(f"xy{l}_", 0, n0 + 1, 2)
                    if s >= 3:
                        k = s - 3
                        hp = k % 2
                        values_T(base_u + k, f"xo{l}_{k}", VM[l], [P * hp, P * hp + 64], True, True)
                for j in range(2, 4):
                    wait_out(f"xo{l}_{j}")
                project_out(f"xy{l}_", 1, n0 + 1, 2)

            pe.wait_ge(ident_ready, 2)
            pe.wait_ge(sv_in, 16 * 13)
            b = open_out("ct")
            full(tr(b[:, 0:CV["rows"]], sv, ident[0:CV["rows"], 0:CV["rows"]]), "ct")
            norm_transposes(0)
            wait_out("memT2")
            wait_out("memT3")
            for l, src in enumerate((HT, OT)):
                wait_landed(pe, 2 * l)
                for j in range(2):
                    project_T(f"km{l}{j}", 2 * l, P * j, src)
                wait_landed(pe, 2 * l + 1)
                for t in range(TT):
                    project(f"vm{l}{t}", 2 * l + 1, 0, 256, t, src)
            norm_transposes(1)
            wait_out("h0_2")
            wait_out("h0_3")
            wait_landed(pe, 4)
            project_T("a", 4, 0, HT, m=16)
            project_T("nq0", 4, 16, HT)
            wait_landed(pe, 5)
            project_T("nq1", 5, 0, HT)
            project_T("nq2", 5, P, HT)
            wait_landed(pe, 6)
            project_T("nq3", 6, 0, HT)
            project_T("kc", 6, P, HT)
            wait_landed(pe, 7)
            project_T("vc", 7, 0, HT)
            project_T("ks", 7, P, HT)
            wait_landed(pe, 8)
            for t in range(TT):
                project(f"vs{t}", 8, 0, P, t, HT)
            project_T("kw", 8, P, HT)
            wait_landed(pe, 9)
            for t in range(TT):
                project(f"vw{t}", 9, 0, P, t, HT)
            for t in range(TT):
                project(f"g{t}", 9, P, P + 24, t, HT)
            for k, w in enumerate(("gq", "gk")):
                wait_landed(pe, 10 + k)
                for j in range(2):
                    project_T(f"{w}{j}", 10 + k, P * j, HT)
            project_wide(["gv0", "gv1"], 12)
            project_wide(["gr0", "gr1"], 14)
            pe.wait_ge(small_in, 16 * 8)
            for j in range(2):
                b = open_out(f"z{j}")
                full(mm(b[:, 0:256], WA[:, P * j:P * j + P], ATa[:, :], start=True, stop=True), f"z{j}")
            for k, name in enumerate(("ck", "cv")):
                b = open_out(name)
                pe.wait_ge(r_ready, k + 1)
                for h in range(2):
                    wait_landed(pe, 16 + 2 * k + h)
                for m in range(16):
                    w = slot(16 + 2 * k + m // 8, 8, 256)
                    r = mm(b[0:30, 0:256], RR[k][:, m, :, :].rearrange("p g c -> p (g c)"), w[:, m % 8, :], start=m == 0, stop=m == 15)
                full(r, name)
            for k, name in enumerate(("ck", "cv")):
                b = open_out(name + "T")
                wait_out(name)
                for jh in range(2):
                    r = tr(b[:, 32 * jh:32 * jh + 30], XN[0:30, k, P * jh:P * jh + P], ident[0:30, 0:30])
                full(r, name + "T")
            b = open_out("c2k")
            wait_out("ckT")
            for half in range(2):
                for jh in range(2):
                    r = mm(b[64 * half:64 * half + 64, 0:30], W2[0][:, jh, :], GH[0][:, jh, :], start=jh == 0, stop=jh == 1)
            full(r, "c2k")
            b = open_out("c2v")
            wait_out("cvT")
            for g in range(2):
                for jh in range(2):
                    r = mm(b[0:CMP, 64 * g:64 * g + 64], GH[1][:, jh, CMP * g:CMP * g + CMP], W2[1][:, jh, :], start=jh == 0, stop=jh == 1)
            full(r, "c2v")
            b = open_out("sc")
            wait_out("c2k")
            for par in range(2):
                if par == 1:
                    rows.link(r)
                for t, h in [(t, h) for t in range(TT) for h in range(par, 8, 2)]:
                    p0 = 64 * (h % 2)
                    c0 = 16 * (8 * t + h)
                    r = mm(b[:, c0:c0 + CMP], NQ[p0:p0 + 64, h // 2, P * t:P * t + P], KC[p0:p0 + 64, CMP * (h // 4):CMP * (h // 4) + CMP],
                           start=True, stop=True)
            full(r, "sc")
            pe.wait_ge(pc_ready, 1)
            for j in range(4):
                b = open_out(f"pct{j}")
                for k in range(4):
                    r = tr(b[0:CMP, P * k:P * k + P], PCC[:, 4 * j + k, 0:CMP], ident[:, :])
                full(r, f"pct{j}")

            def nsa_unit(u):
                return u // 8, u // 2 % 4, u % 2

            for s in range(19):
                after = None if s < 2 else (lambda: prob_transposes(s - 2, 2))
                if s < 16:
                    t, hp, br = nsa_unit(s)
                    K = (KS, KW)[br]
                    scores(s, [(NQ[64 * hh:64 * hh + 64, hp, P * t:P * t + P], K[64 * hh:64 * hh + 64, hp // 2, 0:width(s)]) for hh in range(2)], after)
                elif s < 18:
                    after()
                if s >= 3:
                    t, hp, br = nsa_unit(s - 3)
                    g = hp // 2
                    if s == 3:
                        wait_out("pct3")
                    extra = [(VC[:, g, :], PCT[:, 8 * t + 2 * hp + hh, :]) for hh in range(2)] if br else None
                    values_T(s - 3, f"n{t}{hp}", (VS, VW)[br], [64 * g, 64 * g], br == 0, br == 1, extra)

            def gla_scores(level, tiles, q, kk):
                if level >= 2:
                    pe.wait_ge(gl_used, 2 * level - 2)
                for j, (kt, qt) in enumerate(tiles):
                    for h in range(4):
                        p0 = 64 * (h % 2)
                        col = P * (2 * j + h // 2)
                        r = mm(bank[4 + 2 * (level % 2) + h % 2][:, col:col + P], kk[p0:p0 + 64, h // 2, P * kt:P * kt + P],
                               q[p0:p0 + 64, h // 2, P * qt:P * qt + P], start=True, stop=True)
                        if j == len(tiles) - 1 and h >= 2:
                            r.then_inc(gl_full, 1)

            pe.wait_ge(pt_ready, 16)
            gla_scores(0, [(0, 0), (1, 1)], QG, KG)
            for m in range(8):
                pe.wait_ge(ql_ready, m + 1)
                pe.wait_ge(kl_ready, m + 1)
                gla_scores(m + 1, [(0, 0), (1, 1)] if m < 7 else [(0, 1)], QL[m % 2], KL[m % 2])
            for t in range(TT):
                b = open_out(f"og{t}")
                if t == 0:
                    pe.wait_ge(pg_done, 3)
                for h in range(4):
                    r = mm(b[:, P * h:P * h + P], PG[:, t, h, :], VG[:, t, P * h:P * h + P], start=True, stop=t == 0)
                    if t == 1:
                        r = mm(b[:, P * h:P * h + P], PGX[:, h, :], VG[:, 0, P * h:P * h + P], start=False, stop=True)
                full(r, f"og{t}")
            for t in range(TT):
                b = open_out(f"ogT{t}")
                pe.wait_ge(ogs, t + 1)
                for h in range(4):
                    r = tr(b[:, P * h:P * h + P], SR[:, t, P * h:P * h + P], ident[:, :])
                full(r, f"ogT{t}")
                wait_out(f"ogT{t}")
                project_out("y", t, 20, 8)
            norm_transposes(2)
            cross_attention(0, 24, U_X0)
            norm_transposes(3)
            for j in range(4):
                wait_out(f"h2_{j}")

            def split_products(c, pairs, last):
                pe.wait_ge(lo_ready, c + 1)
                for b, ah, al, wsel, start, stop in pairs:
                    wh, wl = wsel(hi[c % CONV]), wsel(lo[c % CONV])
                    mm(b, ah, wh, start=start, stop=False)
                    mm(b, ah, wl, start=False, stop=False)
                    r = mm(b, al, wh, start=False, stop=stop)
                r.then_inc(conv_used, 1)

            def view(chunks, w, c, c0, c1):
                return lambda x: x[:, 0:chunks * w].rearrange("p (c n) -> p c n", c=chunks)[:, c, c0:c1]

            def transposes0(u):
                for t in range(TT):
                    pe.wait_ge(f_a, 2 * u + t + 1)
                    for j in range(FU[u] // P):
                        r = tr(bank[2 * t][:, P * j:P * j + P], AB[t][:, P * j:P * j + P], ident[:, :])
                    r.then_inc(f_t, 1)

            for u in range(7):
                if u < 6:
                    n = FU[u]
                    parts = 2 if n == 512 else 1
                    for kind, off in (("u", 1), ("g", 0)):
                        if u >= 1:
                            if kind == "u":
                                pe.wait_ge(f_a, 2 * u)
                            else:
                                pe.wait_ge(f_tl, 2 * u)
                        for h in range(parts):
                            ch = DC // parts
                            split_products(AT0[(kind, u, h)],
                                           [(bank[2 * t + off][:, 0:n], HTH[:, ch * h + c, P * t:P * t + P], HTL[:, ch * h + c, P * t:P * t + P],
                                             view(ch, n, c, 0, n), h + c == 0, h == parts - 1 and c == ch - 1)
                                            for t in range(TT) for c in range(ch)], False)
                if u >= 1:
                    v = u - 1
                    jn = FU[v] // P
                    pe.wait_ge(f_tl, 2 * v + 2)
                    for h in range(jn // 2):
                        if u == 5 and h == 1:
                            transposes0(u)
                        split_products(AT0[("d", v, h)],
                                       [(bank[4 + 2 * t + nh][:, :], ATH[t][:, 2 * h + c, :], ATL[t][:, 2 * h + c, :],
                                         view(2, D, c, 512 * nh, 512 * nh + 512), v + h + c == 0, v == 5 and c == 1)
                                        for t in range(TT) for nh in range(2) for c in range(2)], False)
                if u < 5:
                    transposes0(u)

            norm_transposes(4)
            for j in range(4):
                wait_out(f"h3_{j}")

            def three(b, c, wh, wl, cs, ts_, first, last):
                mm(b, wh[:, c, cs], HTH[:, ts_, :], start=first, stop=False)
                mm(b, wl[:, c, cs], HTH[:, ts_, :], start=False, stop=False)
                return mm(b, wh[:, c, cs], HTL1[:, ts_, :], start=False, stop=last)

            def split_view(k, c):
                pe.wait_ge(lo_ready, 33 + k + 1)
                return [x[k % CONV][:, :].rearrange("p (c n) -> p c n", c=c) for x in (hi_d, lo_d)]

            for k in range(8):
                hf, name = k // 4, ("q1", "q2", "k1", "k2")[k % 4]
                wh, wl = split_view(k, DC)
                for j in range(2):
                    b = open_out(f"d{name}{2 * hf + j}")
                    for c in range(DC):
                        r = three(b[:, 0:256], c, wh, wl, slice(P * j, P * j + P), c, c == 0, c == DC - 1)
                    full(r, f"d{name}{2 * hf + j}")
            for half in range(2):
                names = [f"dv{t}{half}" for t in range(TT)]
                bs = [open_out(x) for x in names]
                for h in range(2):
                    wh, wl = split_view(8 + 2 * half + h, 4)
                    for t in range(TT):
                        for c in range(4):
                            tok = slice(P * t, P * t + P)
                            mm(bs[t][:, :], HTH[:, 4 * h + c, tok], wh[:, c, :], start=h + c == 0, stop=False)
                            mm(bs[t][:, :], HTH[:, 4 * h + c, tok], wl[:, c, :], start=False, stop=False)
                            r = mm(bs[t][:, :], HTL1[:, 4 * h + c, tok], wh[:, c, :], start=False, stop=h + c == 4)
                        if h == 1:
                            full(r, names[t])
            b = open_out("lam")
            pe.wait_ge(lams, 1)
            full(mm(b[:, 0:1], ones[0:1, :], small[0:1, 50:51], start=True, stop=True), "lam")
            def head_transposes(k):
                pe.wait_ge(ods, k + 1)
                name = f"odT{k // 2}{k % 2}"
                b = open_out(name)
                for j in range(4):
                    h = 4 * (k % 2) + j
                    r = tr(b[:, P * j:P * j + P], OD[:, k // 2, P * h:P * h + P], ident[:, :])
                full(r, name)

            for s in range(19):
                if s < 16:
                    t, h = s // 8, s % 8
                    p0 = 64 * (h % 2)
                    scores(U_D + s, [(QD[p0:p0 + 64, i, h // 2, P * t:P * t + P], KD[p0:p0 + 64, i, h // 2, 0:width(U_D + s)]) for i in range(2)])
                if 2 <= s < 18:
                    prob_transposes(U_D + s - 2, 1)
                if s >= 10 and s % 4 == 2:
                    head_transposes((s - 10) // 4)
                if s >= 3:
                    u = U_D + s - 3
                    t, h = (s - 3) // 8, (s - 3) % 8
                    name, last = attn_pv_group(u)
                    pe.wait_ge(pt_ready, u + 1)
                    b = open_out(name) if h % 4 == 0 else bank[IDX[name] % 4]
                    for kb in range(t + 1):
                        r = mm(b[:, P * (h % 4):P * (h % 4) + P], PT[u % 4][:, 0, kb, :], VD[:, kb, P * h:P * h + P], start=kb == 0, stop=kb == t)
                    if last:
                        full(r, name)
                    else:
                        r.then_inc(pv_done, 1)
            wait_out("odT01")
            wait_out("odT00")
            project_out("dy", 0, DIFF_LOAD + 12, 8)
            head_transposes(3)
            wait_out("odT10")
            wait_out("odT11")
            project_out("dy", 1, DIFF_LOAD + 12, 8)
            norm_transposes(5)
            cross_attention(1, DIFF_LOAD + 16, U_X1)

            pe.wait_ge(grow_in, 16)
            for nh in range(2):
                r = mm(bank[4 + nh][:, :], ones[0:1, :], grow[0:1, 512 * nh:512 * nh + 512], start=True, stop=True)
            r.then_inc(m_y, 1)
            norm_transposes(6)
            wait_out("h5_2")
            wait_out("h5_3")
            b = open_out("lg")
            for t in range(TT):
                for c in range(DC):
                    r = mm(b[:, NE * t:NE * t + NE], HTR[:, c, P * t:P * t + P], WR[:, c, :], start=c == 0, stop=c == DC - 1)
            full(r, "lg")
            b = open_out("rk")
            pe.wait_ge(ch_ready, 1)
            CH = RA
            for t in range(TT):
                if t == 1:
                    mm(b[:, NE:2 * NE], ones[:, :], CH[:, 0, :], start=True, stop=False)
                r = mm(b[:, NE * t:NE * t + NE], U_strict[:, :], CH[:, t, :], start=t == 0, stop=True)
            for t in range(TT):
                r = mm(b[:, 2 * NE:3 * NE], ones[:, :], CH[:, t, :], start=t == 0, stop=t == 1)
            full(r, "rk")

            def gather():
                for half in range(2):
                    b = bank[6 + half]
                    for c in range(4):
                        for t in range(TT):
                            cs = slice(P * (4 * half + c), P * (4 * half + c) + P)
                            mm(b[:, P * c:P * c + P], XGH[:, t, cs], SELR[:, t, :], start=t == 0, stop=False)
                            r = mm(b[:, P * c:P * c + P], XGL[:, t, cs], SELR[:, t, :], start=False, stop=t == 1)
                r.then_inc(ga_full, 1)

            def expert(i, past):
                it = i + past if past else i

                def unit_up(u):
                    n = FU[u]
                    parts = 2 if n == 512 else 1
                    ch = DC // parts
                    pe.wait_ge(m_a, it * 6 + (u + 1))
                    if u == 0:
                        pe.wait_ge(hgl, it + 1)
                    for off, kind in ((1, "u"), (0, "g")):
                        if kind == "g":
                            pe.wait_ge(m_tl, it * 6 + (u + 1))
                        for h in range(parts):
                            products(ATM[(kind, u, h)],
                                     [(bank[2 * (u % 2) + off][:, 0:n], HGH[:, ch * h + c, :], HGL[:, ch * h + c, :],
                                       view(ch, n, c, 0, n), h + c == 0, h == parts - 1 and c == ch - 1) for c in range(ch)])

                def products(k, pairs):
                    pe.wait_ge(lo_ready, it * 33 + (46 + k))
                    for b, ah, al, wsel, start, stop in pairs:
                        wh, wl = wsel(hi[k % CONV]), wsel(lo[k % CONV])
                        mm(b, ah, wh, start=start, stop=False)
                        mm(b, ah, wl, start=False, stop=False)
                        r = mm(b, al, wh, start=False, stop=stop)
                    r.then_inc(conv_used, 1)

                def unit_transposes(u):
                    pe.wait_ge(m_a, it * 6 + (u + 3))
                    for j in range(FU[u] // P):
                        r = tr(bank[2 * (u % 2)][:, P * j:P * j + P], AB[u % 2][:, P * j:P * j + P], ident[:, :])
                    r.then_inc(m_t, 1)

                def unit_down(u):
                    pe.wait_ge(m_tl, it * 6 + (u + 3))
                    if u == 0:
                        pe.wait_ge(m_yl, it + 1)
                    jn = FU[u] // P
                    for h in range(jn // 2):
                        products(ATM[("d", u, h)],
                                 [(bank[4 + nh][:, :], ATH[u % 2][:, 2 * h + c, :], ATL[u % 2][:, 2 * h + c, :],
                                   view(2, D, c, 512 * nh, 512 * nh + 512), u + h + c == 0, u == 5 and c == 1)
                                  for nh in range(2) for c in range(2)])

                for u in range(8):
                    if u < 6:
                        unit_up(u)
                    if u == 0:
                        scatter(it, 0)
                    if u == 1:
                        scatter(it, 1)
                    if u == 2:
                        pe.wait_ge(sc_add, it * 4 + 4)
                        for t in range(TT):
                            tr(bank[6][:, P * t:P * t + P], SEL[:, t, :], ident[:, :])
                        for t in range(TT):
                            r = mm(bank[6][:, 256:257], SEL[:, t, :], CBI[:, t:t + 1], start=t == 0, stop=t == 1)
                        r.then_inc(st_full, 1)
                    if u == 6:
                        pe.wait_ge(sel_ready, it + 2)
                        pe.wait_ge(st_done, it + 1)
                        gather()
                    if 1 <= u < 7:
                        unit_transposes(u - 1)
                    if u >= 2:
                        unit_down(u - 2)

            def scatter(it, t):
                if t == 0:
                    pe.wait_ge(m_yl, it + 1)
                    pe.wait_ge(hgl, it + 1)
                for nh in range(2):
                    if t == 1:
                        pe.wait_ge(sc_add, it * 4 + (nh + 1))
                    cs = slice(512 * nh, 512 * nh + 512)
                    mm(bank[6 + nh][:, :], SELT[:, t, :], YEH[:, cs], start=True, stop=False)
                    r = mm(bank[6 + nh][:, :], SELT[:, t, :], YEL[:, cs], start=False, stop=True)
                    r.then_inc(sc_full, 1)

            pe.wait_ge(xg_ready, 1)
            pe.wait_ge(sel_ready, 1)
            gather()
            with pe.Fori(0, NE) as i:
                expert(i, 0)
            pe.wait_ge(flag_ready, 1)
            again = pe.value_load(flag[0:1, 0:1], min_val=0, max_val=1)
            with pe.If(again > 0):
                with pe.Fori(0, NE) as i:
                    expert(i, NE)
            for t in range(TT):
                scatter(again * NE + NE, t)

        def step_slots(order, lag, s):
            up = [k for k, x in enumerate(order) if x[0] != "d" and x[1] == s]
            down = [k for k, x in enumerate(order) if x[0] == "d" and x[1] == s - lag]
            return up, down

        G2 = [NQ[:, 2 * t:2 * t + 2, :].rearrange("p a b -> p (a b)") for t in range(TT)]
        def expert_slots(s):
            up, down = step_slots(ORDERM, 2, s)
            return up, {6: down + [32], 7: []}.get(s, down)

        GAINS = ("mix0", "xat0", "ffn0", "mix1", "xat1", "ffn1")

        def nm(u, n=2):
            return small[:, 32 + 2 * (u % 4):32 + 2 * (u % 4) + n]

        def ls(u, n=2):
            return small[:, 40 + 2 * (u % 4):40 + 2 * (u % 4) + n]

        @block.scalar
        def _(act):
            af = nc.scalar.activation
            chain = Chain(act, act_chain)

            gains = (("mix0", "mix_norm_0"), ("xat0", "xattn_norm_0"), ("xmem0", "xattn_mem_norm_0"), ("ffn0", "ffn_norm_0"),
                     ("mix1", "mix_norm_1"), ("xat1", "xattn_norm_1"), ("xmem1", "xattn_mem_norm_1"), ("ffn1", "ffn_norm_1"),
                     ("balpha", "gla_b_alpha_0"), ("glan", "gla_out_norm_0"), ("diffn", "diff_out_norm_1"))
            for key, name in gains:
                src = a[name].rearrange("(r n) -> r n", n=P)
                act.dma_start(TP[0][CV[key]:CV[key] + src.shape[0], 0, 0:P], src).then_inc(sv_in, 16)
            for k, w in enumerate("kv"):
                act.dma_start(TP[0][CV["pos" + w]:CV["pos" + w] + 16, 0, 0:P],
                              a[f"nsa_cmp_pos_{w}_0"].rearrange("(m l) d -> m (l d)", l=2)).then_inc(sv_in, 16)
            def squares(n, src, junk):
                for t in range(TT):
                    if n >= 2:
                        act.wait_ge(x_ready, 2 * n - 3 + t)
                    af(junk(t), src[:, t, :], ACT.Square, accum_out=small[:, 2 * n + t:2 * n + t + 1]).then_inc(ss_ready, 1)

            def xsquares(n):
                squares(n, X, lambda t: XN[:, t, :])

            def out_norm(k, HT=HT):
                g = CV[GAINS[k]]
                for j in (0, 2):
                    b = wait_full(act, f"h{k}_{j}")
                    for c in range(2):
                        r = af(HT[:, 2 * j + c, :], b[:, 256 * c:256 * c + 256], ACT.Copy, scale=CT[:, g + 2 * j + c:g + 2 * j + c + 1])
                    freed(r, f"h{k}_{j}")

            def split_tokens_hi(k):
                wait_full(act, f"h{k}_3")
                for j in range(4):
                    b = wait_full(act, f"h{k}_{j}")
                    for c in range(2):
                        g = CV[GAINS[k]] + 2 * j + c
                        r = af(HTH[:, 2 * j + c, :], b[:, 256 * c:256 * c + 256], ACT.Copy, scale=CT[:, g:g + 1])
                    r.then_inc(hth, 1)

            def take(name, dst, src, func=ACT.Copy, scale=1.0, bias=None):
                b = wait_full(act, name)
                kw = {} if bias is None else {"bias": bias}
                freed(af(dst, src(b), func, scale=scale, **kw), name)

            def exps(u, from_psum, widths=None):
                act.wait_ge(nm_ready, u + 1)
                w = width(u)
                for k in range(2):
                    src = bank[4 + u % 2][:, w * k:w * k + w] if from_psum else TP[u % 4][:, k, 0:w]
                    if k == 0 and from_psum and u >= 4:
                        act.wait_ge(pt_full, u - 3)
                    r = af(TP[u % 4][:, k, 0:w], src, ACT.Exp, bias=nm(u)[:, k:k + 1], accum_out=ls(u)[:, k:k + 1])
                r.then_inc(exp_done, 1)

            def copy_pt(u, halves):
                act.wait_ge(pt_full, u + 1)
                if u >= 4:
                    wait_pv(act, u - 4)
                b = bank[6 + u % 2]
                w = width(u)
                if halves == 1:
                    r = af(PT[u % 4][:, 0, :, :].rearrange("p a b -> p (a b)")[:, 0:w], b[:, 0:w], ACT.Copy)
                else:
                    v = b[:, :].rearrange("p (h n) -> p h n", h=2)[:, :, 0:w]
                    r = af(PT[u % 4][:, :, :, :].rearrange("p h a b -> p h (a b)")[:, :, 0:w], v, ACT.Copy)
                r.then_inc(pt_ready, 1)

            def cross_attention(l, base_u, k):
                out_norm(k)
                for j in range(2):
                    take(f"xq{l}_{j}", QX[:, j, :], lambda b: b[:, 0:256], scale=0.125)
                for s in range(7):
                    if s < 4:
                        exps(base_u + s, True)
                    if 2 <= s < 6:
                        copy_pt(base_u + s - 2, 2)
                    if s >= 3:
                        q = s - 3
                        take(f"xo{l}_{q}", OT[:, q % 2, P * (q // 2):P * (q // 2) + P], lambda b: b[:, 0:P])

            act.wait_ge(mem_in, 16)
            squares(0, XN, lambda t: OT[:, 4 * t:4 * t + 4, :].rearrange("p a b -> p (a b)"))
            take("ct", CT[:, :], lambda b: b[:, 0:CV["rows"]])
            act.wait_ge(bank_free[0], 1)
            for j in (0, 2):
                b = wait_full(act, f"memT{j}")
                for l, dst in enumerate((HT, OT)):
                    for c in range(2):
                        g = CV[f"xmem{l}"] + 2 * j + c
                        r = af(dst[:, 2 * j + c, :], b[:, 256 * c:256 * c + 256], ACT.Copy, scale=CT[:, g:g + 1])
                freed(r, f"memT{j}")
            act.wait_ge(x_in, 16)
            squares(1, X, lambda t: (VG, SR)[t][:, :, :].rearrange("p a b -> p (a b)"))
            for l in range(2):
                for j in range(2):
                    take(f"km{l}{j}", KM[l][:, j, :], lambda b: b[:, 0:256])
                for t in range(2):
                    take(f"vm{l}{t}", VM[l][:, t, :], lambda b: b[:, 0:256])
            out_norm(0)
            take("a", ATa[:, :], lambda b: b[0:16, 0:256])

            def both_halves(name, dst, shift):
                b = wait_full(act, name)
                for half in range(2):
                    for g in range(2):
                        s = shift * half
                        r = af(dst[64 * half:64 * half + 64, g, 0:256 - s], b[64 * g:64 * g + 64, s:256], ACT.Copy)
                freed(r, name)

            for j in range(4):
                take(f"nq{j}", NQ[:, j, :], lambda b: b[:, 0:256], scale=0.125)
            both_halves("kc", T2[0], 1)
            both_halves("vc", T2[1], 1)
            both_halves("ks", KS, 0)
            for t in range(TT):
                take(f"vs{t}", VS[:, t, :], lambda b: b[:, 0:P])
            both_halves("kw", KW, 0)
            for t in range(TT):
                take(f"vw{t}", VW[:, t, :], lambda b: b[:, 0:P])
            for t in range(TT):
                take(f"g{t}", GT[:, t, :], lambda b: b[:, 0:24], func=ACT.Sigmoid)
            for j in range(2):
                take(f"gq{j}", QG[:, j, :], lambda b: b[:, 0:256], scale=0.125)
            for j in range(2):
                take(f"gk{j}", KG[:, j, :], lambda b: b[:, 0:256])
            for t in range(TT):
                take(f"gv{t}", VG[:, t, :], lambda b: b[:, :])
            for t in range(TT):
                take(f"gr{t}", SR[:, t, :], lambda b: b[:, :], func=ACT.Silu)
            for j in range(2):
                take(f"z{j}", LA[:, j, :], lambda b: b[:, 0:256], func=ACT.Identity, bias=CT[:, CV["balpha"] + j:CV["balpha"] + j + 1])
            act.wait_ge(z_ready, 1)
            chain.link(af(EL1[:, :, :], EL1[:, :, :], ACT.Exp, scale=-1.0))
            af(EL1[:, :, :], EL1[:, :, :], ACT.Ln, bias=1.0).then_inc(l_ready, 1)

            def decay(m):
                act.wait_ge(d_ready, m + 1)
                af(EL[m % 2][:, :, :], EL[m % 2][:, :, :], ACT.Exp, scale=-1.0).then_inc(el_ready, 1)

            decay(0)
            decay(1)
            for k, name in enumerate(("ck", "cv")):
                take(name, XN[0:30, k, 0:256], lambda b: b[0:30, 0:256], func=ACT.Gelu_apprx_tanh)
            for k, name in enumerate(("ckT", "cvT")):
                take(name, GH[k][:, :, :], lambda b: b[:, 0:64].rearrange("p (j n) -> p j n", j=2)[:, :, 0:30])
            take("c2k", KC[:, :], lambda b: b[:, 0:30])
            take("c2v", VC[:, :, :], lambda b: b[0:CMP, 0:P].rearrange("p (g d) -> p g d", g=2))
            act.wait_ge(pc_t, 1)
            af(PCC[:, :, 0:CMP], PCC[:, :, 0:CMP], ACT.Exp).then_inc(pc_e, 1)
            for j in range(4):
                take(f"pct{j}", PCT[:, 4 * j:4 * j + 4, :], lambda b: b[0:CMP, :].rearrange("p (a b) -> p a b", a=4))
            for s in range(19):
                if s < 16:
                    exps(s, False)
                if 2 <= s < 18:
                    copy_pt(s - 2, 2)
                if s >= 4 and s % 2 == 0:
                    k = (s - 4) // 2
                    take(f"n{k // 4}{k % 4}", OT[:, 4 + k % 4, P * (k // 4):P * (k // 4) + P], lambda b: b[:, 0:P])
            for m in range(2, 8):
                decay(m)
            for t in range(TT):
                b = wait_full(act, f"og{t}")
                af(G2[t], b[:, :], ACT.Square).then_inc(osq, 1)
            for t in range(TT):
                take(f"ogT{t}", OT[:, 0:4, P * t:P * t + P], lambda b: b[:, :].rearrange("p (a b) -> p a b", a=4),
                     scale=CT[:, CV["glan"]:CV["glan"] + 1])
            xsquares(2)
            cross_attention(0, U_X0, 1)
            xsquares(3)
            def split_hi(c):
                n = FFN0_LOAD + c
                wait_landed(act, n)
                if c >= CONV:
                    act.wait_ge(conv_used, c - CONV + 1)
                w = loads[n][1] * loads[n][2]
                af(hi[c % CONV][:, 0:w], ring[n % RING][:, 0:w], ACT.Copy).then_inc(hi_ready, 1)

            split_hi(0)
            split_tokens_hi(2)

            def act0(u):
                act.wait_ge(conv_used, step_slots(ORDER0, 1, u)[0][-1] + 1)
                for t in range(TT):
                    af(AB[t][:, 0:FU[u]], bank[2 * t][:, 0:FU[u]], ACT.Silu).then_inc(f_e, 1)

            def ath0(u):
                for t in range(TT):
                    act.wait_ge(f_t, 2 * u + t + 1)
                    j = FU[u] // P
                    af(ATH[t][:, 0:j, :].rearrange("p a b -> p (a b)"), bank[2 * t][:, 0:FU[u]], ACT.Copy).then_inc(f_th, 1)

            for u in range(7):
                up, down = step_slots(ORDER0, 1, u)
                if u == 6:
                    for c in down:
                        split_hi(c)
                    continue
                for c in (up[1:] if u == 0 else up[len(up) // 2:]) + down:
                    split_hi(c)
                act0(u)
                if u < 5:
                    nxt = step_slots(ORDER0, 1, u + 1)[0]
                    for c in nxt[:len(nxt) // 2]:
                        split_hi(c)
                ath0(u)

            act.wait_ge(conv_used, 33)
            xsquares(4)

            def split_hi_d(k):
                n = DIFF_LOAD + k
                wait_landed(act, n)
                if k >= CONV:
                    wait_full(act, LAST[n - CONV])
                af(hi_d[k % CONV][:, :], ring[n % RING][:, :], ACT.Copy).then_inc(hi_ready, 1)

            split_hi_d(0)
            split_tokens_hi(3)
            split_hi_d(1)
            act.wait_ge(bank_free[IDX["h3_3"] % 4], IDX["h3_3"] // 4 + 1)
            split_hi_d(2)
            for k in range(8):
                hf, name, dst = k // 4, ("q1", "q2", "k1", "k2")[k % 4], (QD, QD, KD, KD)[k % 4]
                for j in range(2):
                    take(f"d{name}{2 * hf + j}", dst[:, k % 2, 2 * hf + j, :], lambda b: b[:, 0:256], scale=0.125 if k % 4 < 2 else 1.0)
                if k + CONV < 12:
                    split_hi_d(k + CONV)
            for half in range(2):
                if half == 0:
                    wait_full(act, "dv10")
                    split_hi_d(11)
                for t in range(TT):
                    take(f"dv{t}{half}", VD[:, t, 512 * half:512 * half + 512], lambda b: b[:, :])
            act.wait_ge(er_ready, 1)
            af(small[0:1, 52:54], small[0:1, 48:50], ACT.Exp).then_inc(r_e, 1)
            take("lam", small[:, 51:52], lambda b: b[:, 0:1])

            act.dma_start(grow[:, :], a["final_norm"].rearrange("(a n) -> a n", a=1)).then_inc(grow_in, 16)

            def head_copy(k):
                t, hq = k // 2, k % 2
                take(f"odT{t}{hq}", OT[:, 4 * hq:4 * hq + 4, P * t:P * t + P], lambda b: b[:, :].rearrange("p (a b) -> p a b", a=4),
                     scale=CT[:, CV["diffn"]:CV["diffn"] + 1])

            for s in range(20):
                if s < 16:
                    exps(U_D + s, False)
                if 2 <= s < 18:
                    copy_pt(U_D + s - 2, 1)
                if s >= 7 and s % 4 == 3:
                    k = (s - 7) // 4
                    take(f"od{k // 2}{k % 2}", OD[:, k // 2, 512 * (k % 2):512 * (k % 2) + 512], lambda b: b[:, :])
                if s >= 11 and s % 4 == 3:
                    head_copy((s - 11) // 4)
            head_copy(3)
            xsquares(5)
            cross_attention(1, U_X1, 4)
            xsquares(6)
            out_norm(5, HTR)
            for t in range(TT):
                r = af(XGH[:, t, :], XN[:, t, :], ACT.Copy)
            r.then_inc(xgh_ready, 1)
            act.wait_ge(e_ready, 1)
            af(small[:, 56:58], small[:, 54:56], ACT.Exp).then_inc(r_e, 1)
            act.wait_ge(m_y, 1)
            act.wait_ge(m_init, 1)
            for nh in range(2):
                r = af(FG[:, 512 * nh:512 * nh + 512], bank[4 + nh][:, :], ACT.Copy)
            r.then_inc(m_ye, 1)

            def result_hi(it):
                act.wait_ge(conv_used, it * 33 + 33)
                for nh in range(2):
                    r = af(YEH[:, 512 * nh:512 * nh + 512], bank[4 + nh][:, :], ACT.Copy, scale=WS[:, :])
                r.then_inc(m_ye, 1)

            def gather_hi(past):
                act.wait_ge(ga_full, past + 1)
                for c in range(DC):
                    g = CV["ffn1"] + c
                    r = af(HGH[:, c, :], bank[6 + c // 4][:, P * (c % 4):P * (c % 4) + P], ACT.Copy, scale=CT[:, g:g + 1])
                r.then_inc(hgh, 1)

            def expert(i, past):
                it = i + past if past else i

                def split_hi_m(k):
                    act.wait_ge(landed[k % RING], it * 48 + 16 * (MOE_LOAD // RING + k // RING + 1))
                    act.wait_ge(conv_used, it * 33 + (33 + k - CONV + 1))
                    kind, u, h = ORDERM[k]
                    af(hi[k % CONV][:, :], ring[k % RING][:, :], ACT.Copy).then_inc(hi_ready, 1)

                for s in range(8):
                    up, down = expert_slots(s)
                    for k in up[:2]:
                        split_hi_m(k)
                    if s >= 2:
                        u = s - 2
                        act.wait_ge(m_t, it * 6 + (u + 1))
                        af(ATH[u % 2][:, 0:FU[u] // P, :].rearrange("p a b -> p (a b)"), bank[2 * (u % 2)][:, 0:FU[u]], ACT.Copy).then_inc(m_th, 1)
                    for k in up[2:3]:
                        split_hi_m(k)
                    if s == 0:
                        result_hi(it)
                    if 1 <= s < 7:
                        u = s - 1
                        last_up = step_slots(ORDERM, 2, u)[0][-1]
                        act.wait_ge(conv_used, it * 33 + (33 + last_up + 1))
                        af(AB[u % 2][:, 0:FU[u]], bank[2 * (u % 2)][:, 0:FU[u]], ACT.Silu).then_inc(m_e, 1)
                    for k in up[3:] + down:
                        split_hi_m(k)
                    if s == 3:
                        act.wait_ge(st_full, it + 1)
                        af(SELT[:, :, :].rearrange("p a b -> p (a b)"), bank[6][:, 0:256], ACT.Copy)
                        af(WS[:, :], bank[6][:, 256:257], ACT.Copy).then_inc(st_done, 1)
                    if s == 6:
                        gather_hi(it + 1)

            af(small[:, 62:63], CT[:, 0:1], ACT.Silu)
            gather_hi(0)
            with act.Fori(0, NE) as i:
                expert(i, 0)
            act.wait_ge(flag_ready, 1)
            again = act.value_load(flag[0:1, 0:1], min_val=0, max_val=1)
            with act.If(again > 0):
                with act.Fori(0, NE) as i:
                    expert(i, NE)
            result_hi(again * NE + NE)
            act.wait_ge(xn_ready, 14)
            squares(7, X, lambda t: XN[:, t, :])

        @block.vector
        def _(dve):
            v = nc.vector
            chain = Chain(dve, dve_chain)
            link = chain.link
            tt, ts = v.tensor_tensor, v.tensor_scalar

            def bc(ap, n):
                return ap.unsqueeze(2).broadcast_to([ap.shape[0], ap.shape[1], n])

            def normalise(n, src):
                for t in range(TT):
                    dve.wait_ge(ss_ready, 2 * n + t + 1)
                    ts(small[:, 16 + 2 * n + t:17 + 2 * n + t], small[:, 2 * n + t:2 * n + t + 1], 1.0 / D, EPS,
                       ALU.mult, ALU.add).then_inc(ms_ready, 1)
                    dve.wait_ge(rstd_ready, 2 * n + t + 1)
                    if n < 7:
                        ts(XN[:, t, :], src[:, t, :], rstd[:, t:t + 1], None, ALU.mult).then_inc(xn_ready, 1)
                    else:
                        v.scalar_tensor_tensor(XN[:, t, :], src[:, t, :], rstd[:, t:t + 1], FG[:, :], ALU.mult, ALU.mult).then_inc(fin_ready, 1)

            def out_norm(k, HT=HT):
                for j in (1, 3):
                    b = wait_full(dve, f"h{k}_{j}")
                    for c in range(2):
                        g = CV[GAINS[k]] + 2 * j + c
                        r = ts(HT[:, 2 * j + c, :], b[:, 256 * c:256 * c + 256], CT[:, g:g + 1], None, ALU.mult)
                    freed(r, f"h{k}_{j}")

            def split_tokens_lo(k, dst, before):
                for j in range(4):
                    dve.wait_ge(hth, before + j + 1)
                    b = wait_full(dve, f"h{k}_{j}")
                    for c in range(2):
                        g = CV[GAINS[k]] + 2 * j + c
                        r = v.scalar_tensor_tensor(dst[:, 2 * j + c, :], b[:, 256 * c:256 * c + 256], CT[:, g:g + 1],
                                                   HTH[:, 2 * j + c, :].bitcast(F32), ALU.mult, ALU.subtract)
                    freed(r, f"h{k}_{j}")

            dve.wait_ge(pool_const, 1)
            link(v.tensor_copy(NB[:, 7, :], IOn[:, :]))
            for h in range(7):
                r = ts(NB[:, h, :], NB[:, 7, :], SLOPES[h], None, ALU.mult)
            link(r)
            link(ts(NB[:, 7, :], NB[:, 7, :], SLOPES[7], None, ALU.mult))
            link(v.tensor_copy(CB[:, 7, :], IOc[:, 0, :]))
            link(v.tensor_copy(CB[:, 15, :], IOc[:, 1, :]))
            for t in range(TT):
                for h in range(7):
                    r = ts(CB[:, 8 * t + h, :], CB[:, 8 * t + 7, :], SLOPES[h], None, ALU.mult)
            link(r)
            for t in range(TT):
                r = ts(CB[:, 8 * t + 7, :], CB[:, 8 * t + 7, :], SLOPES[7], None, ALU.mult)
            link(r)
            link(v.memset(CM[:, :, :], 1.0))
            v.memset(halfneg[:, :], -0.5).then_inc(dve_const, 1)

            dve.wait_ge(mem_in, 16)
            normalise(0, XN)
            dve.wait_ge(bank_free[0], 1)
            dve.wait_ge(ss_ready, 2)
            for j in (1, 3):
                b = wait_full(dve, f"memT{j}")
                for l, dst in enumerate((HT, OT)):
                    for c in range(2):
                        g = CV[f"xmem{l}"] + 2 * j + c
                        r = ts(dst[:, 2 * j + c, :], b[:, 256 * c:256 * c + 256], CT[:, g:g + 1], None, ALU.mult)
                freed(r, f"memT{j}")
            normalise(1, X)
            link(tt(out=IOx[:, :], in0=IOs[:, :], in1=IOt[:, :], op=ALU.bitwise_xor))
            for m in range(8):
                if m == 0:
                    ts(MKf[:, 0, :], IOx[:, :], 0, None, ALU.is_equal)
                else:
                    link(ts(IOy[:, :], IOx[:, :], m - 1, None, ALU.logical_shift_right))
                    link(ts(MKf[:, m, :], IOy[:, :], 1, None, ALU.is_equal))
            v.memset(small[:, 61:62], 0.0).then_inc(dve_const, 1)
            dve.wait_ge(mk_ready, 1)
            link(v.tensor_copy(MK[:, :, :], MKf[:, :, :]))
            out_norm(0)
            dve.wait_ge(small_in, 16 * 8)
            link(ts(CT[:, CV["diffn"]:CV["diffn"] + 1], CT[:, CV["diffn"]:CV["diffn"] + 1], 1.0 - LAMBDA_INIT, None, ALU.mult))
            link(tt(out=lrow[:, 0::2, :], in0=lrow[:, 0::2, :], in1=lrow[:, 1::2, :], op=ALU.mult))
            v.tensor_reduce(small[0:1, 48:50], lrow[:, 0::2, :], AX, ALU.add).then_inc(er_ready, 1)
            for k, name in enumerate(("kc", "vc")):
                o = IDX[name]
                dve.wait_ge(bank_free[o % 4], o // 4 + 1)
                for g in range(2):
                    for mh in range(2):
                        src = T2[k][:, g, 16 * mh:16 * mh + 240].rearrange("p (c m) -> p m c", m=16)[:, 0::2, :]
                        pos = CT[:, CV["pos" + "kv"[k]] + 8 * mh:CV["pos" + "kv"[k]] + 8 * mh + 8]
                        r = tt(out=RR[k][:, 8 * mh:8 * mh + 8, g, :], in0=src, in1=bc(pos, CMP), op=ALU.add)
                r.then_inc(r_ready, 1)
            dve.wait_ge(bank_free[IDX["z1"] % 4], IDX["z1"] // 4 + 1)
            v.scalar_tensor_tensor(EL1[:, :, :], LA[:, :, :], -1.0, LA[:, :, :], ALU.mult, ALU.max).then_inc(z_ready, 1)
            dve.wait_ge(l_ready, 1)
            link(v.scalar_tensor_tensor(LA[:, :, :], LA[:, :, :], 0.0, EL1[:, :, :], ALU.min, ALU.subtract))
            link(ts(LA[:, :, :], LA[:, :, :], 1.0 / 16.0, None, ALU.mult))
            link(v.memset(EL1[:, :, :], 1.0))
            for j in range(2):
                r = v.tensor_tensor_scan(BG[:, j, :], EL1[:, j, :], LA[:, j, :], 0.0, ALU.mult, ALU.add)
            link(r)

            def distances(m):
                L = 1 << m
                if m >= 2:
                    dve.wait_ge(kl_ready, m - 1)
                    dve.wait_ge(ql_ready, m - 1)
                bv = BG[:, :, :].rearrange("p a (n l) -> p (a n) l", l=2 * L)
                ev = EL[m % 2][:, :, :].rearrange("p a (n l) -> p (a n) l", l=2 * L)
                ref = bv[:, :, L - 1:L].broadcast_to([P, 256 // L, 2 * L])
                link(tt(out=ev, in0=bv, in1=ref, op=ALU.subtract))
                v.scalar_tensor_tensor(EL[m % 2][:, :, :], EL[m % 2][:, :, :], -1.0, EL[m % 2][:, :, :], ALU.mult, ALU.max).then_inc(d_ready, 1)

            def decayed_queries(m):
                if m >= 2:
                    dve.wait_ge(gl_full, 2 * m)
                dve.wait_ge(el_ready, m + 1)
                tt(out=QL[m % 2][:, :, :], in0=QG[:, :, :], in1=EL[m % 2][:, :, :], op=ALU.mult).then_inc(ql_ready, 1)

            for m in range(2):
                distances(m)
            for m in range(2):
                decayed_queries(m)
            b = wait_full(dve, "sc")
            dve.wait_ge(nb_ready, 1)
            bs = b[:, 0:256].rearrange("p (h c) -> p h c", c=16)[:, :, 0:CMP]
            PC = PCC[:, :, 0:CMP]
            r = tt(out=PC, in0=bs, in1=CB[:, :, 0:CMP], op=ALU.add)
            freed(r, "sc")
            dve.wait_ge(bank_free[IDX["sc"] % 4], IDX["sc"] // 4 + 1)
            PM, PS = CX[:, 0:16], CX[:, 16:32]
            link(v.tensor_reduce(PM, PC, AX, ALU.max))
            tt(out=PC, in0=PC, in1=bc(PM, CMP), op=ALU.subtract).then_inc(pc_t, 1)
            dve.wait_ge(pc_e, 1)
            for t in range(TT):
                link(tt(out=PCC[:, 8 * t:8 * t + 8, 0:CMP], in0=PCC[:, 8 * t:8 * t + 8, 0:CMP],
                        in1=CM[:, t:t + 1, 0:CMP].broadcast_to([P, 8, CMP]), op=ALU.mult))
            link(v.tensor_reduce(PS, PC, AX, ALU.add))
            link(ts(PS, PS, TINY, None, ALU.max))
            link(v.reciprocal(PS, PS))
            o = IDX["g1"]
            dve.wait_ge(bank_free[o % 4], o // 4 + 1)
            link(tt(out=PS, in0=PS, in1=GT[:, :, :].rearrange("p t (h b) -> p (t h) b", b=3)[:, :, 0], op=ALU.mult))
            tt(out=PC, in0=PC, in1=bc(PS, CMP), op=ALU.mult).then_inc(pc_ready, 1)

            def add_bias(u, h0, step):
                dve.wait_ge(s_full, u + 1)
                if u >= 4:
                    dve.wait_ge(pt_full, u - 3)
                w = width(u)
                T = TP[u % 4][:, :, 0:w]
                bias = NB[:, h0:h0 + 2, 256 - w:256] if step else NB[:, h0:h0 + 1, 256 - w:256].broadcast_to([P, 2, w])
                tt(out=T, in0=bank[4 + u % 2][:, 0:2 * w].rearrange("p (h w) -> p h w", h=2), in1=bias, op=ALU.add).then_inc(s_used, 1)
                dve.wait_ge(s_used, S_USED[u])
                v.tensor_reduce(nm(u), T, AX, ALU.max, negate=True).then_inc(nm_ready, 1)

            def scale_probs(u, gate):
                dve.wait_ge(exp_done, u + 1)
                w = width(u)
                link(v.reciprocal(ls(u), ls(u)))
                if gate is not None:
                    link(tt(out=ls(u), in0=ls(u), in1=gate, op=ALU.mult))
                for k in range(2):
                    r = ts(TP[u % 4][:, k, 0:w], TP[u % 4][:, k, 0:w], ls(u)[:, k:k + 1], None, ALU.mult)
                r.then_inc(p_ready, 1)

            for s in range(17):
                if s < 16:
                    add_bias(s, 2 * (s // 2 % 4), True)
                if s >= 1:
                    t, hp, br = (s - 1) // 8, (s - 1) // 2 % 4, (s - 1) % 2
                    gate = GT[:, t, :].rearrange("p (h b) -> p h b", b=3)[:, 2 * hp:2 * hp + 2, 1 + br]
                    scale_probs(s - 1, gate)
            wait_full(dve, "n13")
            link(v.memset(PG[:, :, :, :], 0.0))

            def take_scores(level, par):
                k = 2 * level + par
                dve.wait_ge(gl_full, 2 * level + 2)
                if level >= 1:
                    dve.wait_ge(gl_used, k - 1)
                b = bank[4 + k % 4]
                if level == 8:
                    v.tensor_copy(PGX[:, par::2, :], b[:, 0:256].rearrange("p (h n) -> p h n", h=2)).then_inc(gl_used, 1)
                else:
                    mask = MK[:, level:level + 1, :].unsqueeze(1).broadcast_to([P, TT, 2, P])
                    v.copy_predicated(PG[:, :, par::2, :], mask, b[:, :].rearrange("p (t h n) -> p t h n", t=TT, h=2)).then_inc(gl_used, 1)

            for m in range(10):
                if 2 <= m < 8:
                    distances(m)
                if m != 1:
                    for par in range(2):
                        take_scores(max(m - 1, 0), par)
                if 2 <= m < 8:
                    decayed_queries(m)
            v.memset(small[:, 58:59], 0.0).then_inc(pg_done, 3)
            for t in range(TT):
                b = wait_full(dve, f"og{t}")
                dve.wait_ge(osq, t + 1)
                freed(tt(out=SR[:, t, :], in0=b[:, :], in1=SR[:, t, :], op=ALU.mult), f"og{t}")
                link(v.tensor_reduce(CX[:, 8 * t:8 * t + 4], G2[t].rearrange("p (h n) -> p h n", h=4), AX, ALU.add))
                ts(CX[:, 8 * t:8 * t + 4], CX[:, 8 * t:8 * t + 4], 1.0 / P, EPS, ALU.mult, ALU.add).then_inc(ogm, 1)
            for t in range(TT):
                dve.wait_ge(ogr, t + 1)
                V3 = SR[:, t, :].rearrange("p (h n) -> p h n", h=4)
                tt(out=V3, in0=V3, in1=bc(CX[:, 8 * t + 4:8 * t + 8], P), op=ALU.mult).then_inc(ogs, 1)

            def add_residual(names):
                for j in range(4):
                    b = wait_full(dve, names[j])
                    r = tt(out=X[:, j // 2, 512 * (j % 2):512 * (j % 2) + 512], in0=X[:, j // 2, 512 * (j % 2):512 * (j % 2) + 512],
                           in1=b[:, :], op=ALU.add)
                    freed(r, names[j])
                    if j % 2 == 1:
                        v.memset(small[:, 59 + j:60 + j], 0.0).then_inc(x_ready, 1)

            add_residual([f"y{j}" for j in range(4)])

            def cross_attention(l, base_u):
                for s in range(5):
                    if s < 4:
                        u = base_u + s
                        dve.wait_ge(s_full, u + 1)
                        v.tensor_reduce(nm(u), bank[4 + u % 2][:, :].rearrange("p (h w) -> p h w", h=2), AX, ALU.max,
                                        negate=True).then_inc(nm_ready, 1)
                    if s >= 1:
                        scale_probs(base_u + s - 1, None)
                add_residual([f"xy{l}_{j}" for j in range(4)])

            normalise(2, X)
            out_norm(1)
            cross_attention(0, U_X0)
            normalise(3, X)
            def split_lo(c):
                n = FFN0_LOAD + c
                dve.wait_ge(hi_ready, c + 1)
                w = loads[n][1] * loads[n][2]
                tt(out=lo[c % CONV][:, 0:w], in0=ring[n % RING][:, 0:w], in1=hi[c % CONV][:, 0:w].bitcast(F32), op=ALU.subtract).then_inc(lo_ready, 1)

            split_lo(0)
            split_tokens_lo(2, HTL, 0)

            def act0(u):
                for t in range(TT):
                    dve.wait_ge(f_e, 2 * u + t + 1)
                    tt(out=AB[t][:, 0:FU[u]], in0=AB[t][:, 0:FU[u]], in1=bank[2 * t + 1][:, 0:FU[u]], op=ALU.mult).then_inc(f_a, 1)

            def atl0(u):
                for t in range(TT):
                    dve.wait_ge(f_th, 2 * u + t + 1)
                    j = FU[u] // P
                    tt(out=ATL[t][:, 0:j, :].rearrange("p a b -> p (a b)"), in0=bank[2 * t][:, 0:FU[u]],
                       in1=ATH[t][:, 0:j, :].rearrange("p a b -> p (a b)").bitcast(F32), op=ALU.subtract).then_inc(f_tl, 1)

            for u in range(7):
                up, down = step_slots(ORDER0, 1, u)
                if u == 6:
                    for c in down:
                        split_lo(c)
                    continue
                for c in (up[1:] if u == 0 else up[len(up) // 2:]) + down:
                    split_lo(c)
                act0(u)
                if u < 5:
                    nxt = step_slots(ORDER0, 1, u + 1)[0]
                    for c in nxt[:len(nxt) // 2]:
                        split_lo(c)
                atl0(u)
            dve.wait_ge(conv_used, 33)
            for j in range(4):
                tt(out=X[:, j // 2, 512 * (j % 2):512 * (j % 2) + 512], in0=X[:, j // 2, 512 * (j % 2):512 * (j % 2) + 512],
                   in1=bank[4 + j][:, :], op=ALU.add)
                if j % 2 == 1:
                    v.memset(small[:, 59 + j:60 + j], 0.0).then_inc(x_ready, 1)

            normalise(4, X)

            def split_lo_d(k):
                dve.wait_ge(hi_ready, 33 + k + 1)
                tt(out=lo_d[k % CONV][:, :], in0=ring[(DIFF_LOAD + k) % RING][:, :], in1=hi_d[k % CONV][:, :].bitcast(F32),
                   op=ALU.subtract).then_inc(lo_ready, 1)

            split_lo_d(0)
            split_tokens_lo(3, HTL1, 4)
            for k in range(1, 12):
                split_lo_d(k)
            dve.wait_ge(r_e, 1)
            link(ts(small[0:1, 50:51], small[0:1, 53:54], -LAMBDA_INIT, None, ALU.add))
            tt(out=small[0:1, 50:51], in0=small[0:1, 50:51], in1=small[0:1, 52:53], op=ALU.subtract).then_inc(lams, 1)
            dve.wait_ge(bank_free[IDX["lam"] % 4], IDX["lam"] // 4 + 1)
            def head_squares(k):
                o = IDX[f"od{k // 2}{k % 2}"]
                dve.wait_ge(bank_free[o % 4], o // 4 + 1)
                V = OD[:, k // 2, 512 * (k % 2):512 * (k % 2) + 512]
                if k >= 1:
                    dve.wait_ge(odm, k)
                link(tt(out=SQ[:, 0:512], in0=V, in1=V, op=ALU.mult))
                link(v.tensor_reduce(CX[:, 0:4], SQ[:, 0:512].rearrange("p (h n) -> p h n", h=4), AX, ALU.add))
                ts(CX[:, 0:4], CX[:, 0:4], 1.0 / P, EPS, ALU.mult, ALU.add).then_inc(odm, 1)

            def head_norm(k):
                dve.wait_ge(odr, k + 1)
                V3 = OD[:, k // 2, 512 * (k % 2):512 * (k % 2) + 512].rearrange("p (h n) -> p h n", h=4)
                tt(out=V3, in0=V3, in1=bc(CX[:, 4:8], P), op=ALU.mult).then_inc(ods, 1)

            for s in range(22):
                if s < 16:
                    add_bias(U_D + s, s % 8, False)
                if s >= 8 and s % 4 == 0:
                    head_squares((s - 8) // 4)
                if s >= 9 and s % 4 == 1:
                    head_norm((s - 9) // 4)
                if 1 <= s < 17:
                    u = U_D + s - 1
                    dve.wait_ge(exp_done, u + 1)
                    w = width(u)
                    link(v.reciprocal(ls(u), ls(u)))
                    link(tt(out=ls(u)[:, 1:2], in0=ls(u)[:, 1:2], in1=small[:, 51:52], op=ALU.mult))
                    A0, A1 = TP[u % 4][:, 0, 0:w], TP[u % 4][:, 1, 0:w]
                    link(ts(A0, A0, ls(u)[:, 0:1], None, ALU.mult))
                    v.scalar_tensor_tensor(A0, A1, ls(u)[:, 1:2], A0, ALU.mult, ALU.add).then_inc(p_ready, 1)
            add_residual([f"dy{j}" for j in range(4)])
            normalise(5, X)
            out_norm(4)
            cross_attention(1, U_X1)

            normalise(6, X)
            out_norm(5, HTR)
            dve.wait_ge(pt_ready, 40)
            link(v.memset(SELT[:, :, :].bitcast(F32), 0.0))
            v.memset(WS[:, :], 0.0).then_inc(m_init, 1)
            dve.wait_ge(pool_const, 2)
            link(v.tensor_copy(iota_e[:, :, :], IOe[:, :, :]))
            link(v.tensor_copy(iota_s[:, :], IOf[:, :]))
            dve.wait_ge(xgh_ready, 1)
            for t in range(TT):
                r = tt(out=XGL[:, t, :], in0=XN[:, t, :], in1=XGH[:, t, :].bitcast(F32), op=ALU.subtract)
            r.then_inc(xg_ready, 1)
            b = wait_full(dve, "lg")
            freed(v.tensor_copy(LG[:, :, :], b[:, 0:2 * NE].rearrange("p (t e) -> p t e", t=TT)), "lg")
            dve.wait_ge(bank_free[IDX["lg"] % 4], IDX["lg"] // 4 + 1)
            M1, M2, MI = CX[:, 0:2], CX[:, 2:4], CX[:, 4:6]
            for mx, oh in ((M1, O1), (M2, O2)):
                link(v.tensor_reduce(mx, LG[:, :, :], AX, ALU.max))
                link(tt(out=RA[:, :, :], in0=LG[:, :, :], in1=bc(mx, NE), op=ALU.is_equal))
                link(v.scalar_tensor_tensor(RB[:, :, :], RA[:, :, :], -64.0, iota_e[:, :, :], ALU.mult, ALU.add))
                link(v.tensor_reduce(MI, RB[:, :, :], AX, ALU.min))
                link(tt(out=oh[:, :, :], in0=RB[:, :, :], in1=bc(MI, NE), op=ALU.is_equal))
                if mx is M1:
                    link(v.scalar_tensor_tensor(LG[:, :, :], O1[:, :, :], -3e38, LG[:, :, :], ALU.mult, ALU.add))
            link(tt(out=RA[:, :, :], in0=O1[:, :, :], in1=O2[:, :, :], op=ALU.add))
            tt(out=small[:, 54:56], in0=M2, in1=M1, op=ALU.subtract).then_inc(e_ready, 1)
            v.memset(small[:, 58:59], 0.0).then_inc(ch_ready, 1)
            dve.wait_ge(r_e, 2)
            W1, W2_ = CX[:, 6:8], CX[:, 8:10]
            link(ts(W1, small[:, 56:58], 1.0, None, ALU.add))
            link(v.reciprocal(W1, W1))
            link(tt(out=W2_, in0=W1, in1=small[:, 56:58], op=ALU.mult))
            link(tt(out=O1[:, :, :], in0=O1[:, :, :], in1=bc(W1, NE), op=ALU.mult))
            link(tt(out=O2[:, :, :], in0=O2[:, :, :], in1=bc(W2_, NE), op=ALU.mult))
            for p in range(2):
                tt(out=COMB[:, NE * p:NE * p + NE, :].rearrange("p e t -> p t e"), in0=O1[:, :, :], in1=O2[:, :, :], op=ALU.add)
            link(v.memset(COMB[:, 16, :], 0.0))
            b = wait_full(dve, "rk")
            rank = b[:, 0:2 * NE].rearrange("p (t e) -> p t e", t=TT)
            for p in range(2):
                link(v.scalar_tensor_tensor(RB[:, :, :], rank, 1.0 - P * p, RA[:, :, :], ALU.add, ALU.mult))
                link(ts(POS[:, NE * p:NE * p + NE, :].rearrange("p e t -> p t e"), RB[:, :, :], -1.0, None, ALU.add))
            link(v.memset(POS[:, 16, :], -1.0))
            freed(v.tensor_reduce(CX[:, 10:11], b[:, 2 * NE:3 * NE], AX, ALU.max), "rk")
            dve.wait_ge(bank_free[IDX["rk"] % 4], IDX["rk"] // 4 + 1)
            ts(flag[:, :], CX[:, 10:11], float(P), None, ALU.is_gt).then_inc(flag_ready, 1)
            link(v.memset(small[:, 59:60], 0.0))
            v.memset(small[:, 59:60], 0.0).then_inc(m_tl, 2)
            v.memset(small[:, 60:61], 0.0).then_inc(m_a, 2)

            def select(i):
                v.tensor_copy(PSI[:, :], POS[:, i, :])
                link(v.tensor_copy(CBI[:, :], COMB[:, i, :]))
                for t in range(TT):
                    ts(SEL[:, t, :], iota_s[:, :], PSI[:, t:t + 1], None, ALU.is_equal)
                    r = ts(SELR[:, t, :], iota_s[:, :], PSI[:, t:t + 1], None, ALU.is_equal)
                r.then_inc(sel_ready, 1)

            def gather_lo(past):
                dve.wait_ge(hgh, past + 1)
                for c in range(DC):
                    g = CV["ffn1"] + c
                    r = v.scalar_tensor_tensor(HGL[:, c, :], bank[6 + c // 4][:, P * (c % 4):P * (c % 4) + P], CT[:, g:g + 1],
                                               HGH[:, c, :].bitcast(F32), ALU.mult, ALU.subtract)
                r.then_inc(hgl, 1)

            def result_lo(it):
                dve.wait_ge(m_ye, it + 2)
                for nh in range(2):
                    r = v.scalar_tensor_tensor(YEL[:, 512 * nh:512 * nh + 512], bank[4 + nh][:, :], WS[:, :],
                                               YEH[:, 512 * nh:512 * nh + 512].bitcast(F32), ALU.mult, ALU.subtract)
                r.then_inc(m_yl, 1)

            def scatter_add(it, t):
                for nh in range(2):
                    dve.wait_ge(sc_full, it * 4 + (2 * t + nh + 1))
                    xs = X[:, t, 512 * nh:512 * nh + 512]
                    tt(out=xs, in0=xs, in1=bank[6 + nh][:, :], op=ALU.add).then_inc(sc_add, 1)

            def expert(i, past):
                it = i + past if past else i

                def split_lo_m(k):
                    dve.wait_ge(hi_ready, it * 33 + (45 + k + 1))
                    tt(out=lo[k % CONV][:, :], in0=ring[k % RING][:, :], in1=hi[k % CONV][:, :].bitcast(F32),
                       op=ALU.subtract).then_inc(lo_ready, 1)

                for s in range(8):
                    up, down = expert_slots(s)
                    for k in up[:2]:
                        split_lo_m(k)
                    if s in (1, 2):
                        scatter_add(it, s - 1)
                    if s >= 2:
                        u = s - 2
                        dve.wait_ge(m_th, it * 6 + (u + 1))
                        j = FU[u] // P
                        tt(out=ATL[u % 2][:, 0:j, :].rearrange("p a b -> p (a b)"), in0=bank[2 * (u % 2)][:, 0:FU[u]],
                           in1=ATH[u % 2][:, 0:j, :].rearrange("p a b -> p (a b)").bitcast(F32), op=ALU.subtract).then_inc(m_tl, 1)
                    for k in up[2:3]:
                        split_lo_m(k)
                    if s == 0:
                        result_lo(it)
                    if 1 <= s < 7:
                        u = s - 1
                        dve.wait_ge(m_e, it * 6 + (u + 1))
                        tt(out=AB[u % 2][:, 0:FU[u]], in0=AB[u % 2][:, 0:FU[u]], in1=bank[2 * (u % 2) + 1][:, 0:FU[u]], op=ALU.mult).then_inc(m_a, 1)
                    for k in up[3:] + down:
                        split_lo_m(k)
                    if s == 4:
                        dve.wait_ge(st_full, it + 1)
                        select(it + 1)
                    if s == 6:
                        gather_lo(it + 1)

            select(0)
            gather_lo(0)
            start = chain.n
            with dve.Fori(0, NE) as i:
                chain.loop(i, 1)
                expert(i, 0)
                chain.loop_end()
            dve.wait_ge(flag_ready, 1)
            again = dve.value_load(flag[0:1, 0:1], min_val=0, max_val=1)
            with dve.If(again > 0):
                chain.n = start
                with dve.Fori(0, NE) as i:
                    chain.loop(i + NE, 1)
                    expert(i, NE)
                    chain.loop_end()
            result_lo(again * NE + NE)
            for t in range(TT):
                scatter_add(again * NE + NE, t)
                v.memset(small[:, 60 + 2 * t:61 + 2 * t], 0.0).then_inc(x_ready, 1)
            normalise(7, X)

        @block.gpsimd
        def _(pool):
            g = nc.gpsimd
            g.memset(ident[:, :], 0.0).then_inc(ident_ready, 1)
            g.memset(ones[:, :], 1.0).then_inc(pool_chain, 1)
            pool.wait_ge(ident_ready, 1)
            g.affine_select(out=ident[:, :], in_=ident[:, :], compare_op=ALU.not_equal, fill=1.0, base=0, pattern=[[-1, P]],
                            channel_multiplier=1).then_inc(ident_ready, 1)
            g.iota(IOn[:, :], [[1, 256]], base=-P, channel_multiplier=-1)
            g.iota(IOc[:, :, :], [[-P, 2], [16, 16]], base=31, channel_multiplier=-1)
            g.iota(IOs[:, :], [[0, P]], base=0, channel_multiplier=1)
            g.iota(IOt[:, :], [[1, P]], base=0, channel_multiplier=0).then_inc(pool_const, 1)
            pool.wait_ge(pool_chain, 1)
            g.affine_select(out=U_strict[:, :], in_=ones[:, :], compare_op=ALU.is_gt, fill=0.0, base=0, pattern=[[1, P]],
                            channel_multiplier=-1)
            def root(n):
                for t in range(TT):
                    pool.wait_ge(ms_ready, 2 * n + t + 1)
                    g.tensor_tensor(out=rstd[:, t:t + 1], in0=small[:, 16 + 2 * n + t:17 + 2 * n + t], in1=halfneg[:, 0:1],
                                    op=ALU.pow).then_inc(rstd_ready, 1)

            pool.wait_ge(dve_const, 1)
            root(0)
            root(1)
            g.affine_select(out=NB[:, :, :], in_=NB[:, :, :], compare_op=ALU.is_ge, fill=NEG, base=P, pattern=[[0, 8], [-1, 256]],
                            channel_multiplier=1)
            g.affine_select(out=CB[:, :, :], in_=CB[:, :, :], compare_op=ALU.is_ge, fill=NEG, base=-31,
                            pattern=[[P, 2], [0, 8], [-16, 16]], channel_multiplier=1)
            g.affine_select(out=CM[:, :, :], in_=CM[:, :, :], compare_op=ALU.is_ge, fill=0.0, base=-31,
                            pattern=[[P, 2], [-16, 16]], channel_multiplier=1).then_inc(nb_ready, 1)

            pool.wait_ge(dve_const, 2)
            g.affine_select(out=MKf[:, :, :], in_=MKf[:, :, :], compare_op=ALU.is_ge, fill=0.0, base=0, pattern=[[0, 8], [1, P]],
                            channel_multiplier=-1).then_inc(mk_ready, 1)
            for m in range(8):
                pool.wait_ge(el_ready, m + 1)
                if m == 0:
                    wait_full(pool, "cv")
                if m >= 2:
                    pool.wait_ge(gl_full, 2 * m)
                g.tensor_tensor(out=KL[m % 2][:, :, :], in0=KG[:, :, :], in1=EL[m % 2][:, :, :], op=ALU.mult).then_inc(kl_ready, 1)
            for t in range(TT):
                pool.wait_ge(ogm, t + 1)
                g.tensor_tensor(out=CX[:, 8 * t + 4:8 * t + 8], in0=CX[:, 8 * t:8 * t + 4], in1=halfneg[:, 0:4], op=ALU.pow).then_inc(ogr, 1)
            root(2)
            root(3)
            root(4)
            for k in range(4):
                pool.wait_ge(odm, k + 1)
                g.tensor_tensor(out=CX[:, 4:8], in0=CX[:, 0:4], in1=halfneg[:, 0:4], op=ALU.pow).then_inc(odr, 1)
            root(5)
            root(6)
            g.iota(IOe[:, :, :], [[0, TT], [1, NE]], base=0, channel_multiplier=0)
            g.iota(IOf[:, :], [[1, P]], base=0, channel_multiplier=0).then_inc(pool_const, 1)
            root(7)


_INS = ["x", "mem", "mix_norm_0", "w_in_0", "gla_w_alpha_0", "gla_b_alpha_0", "gla_out_norm_0", "nsa_cmp_pos_k_0",
        "nsa_cmp_w1_k_0", "nsa_cmp_w2_k_0", "nsa_cmp_pos_v_0", "nsa_cmp_w1_v_0", "nsa_cmp_w2_v_0", "w_out_0",
        "xattn_norm_0", "xattn_mem_norm_0", "xattn_wq_0", "xattn_wk_0", "xattn_wv_0", "xattn_wo_0", "ffn_norm_0",
        "ffn_w_gate_0", "ffn_w_up_0", "ffn_w_down_0", "mix_norm_1", "w_in_1", "diff_lq1_1", "diff_lk1_1", "diff_lq2_1",
        "diff_lk2_1", "diff_out_norm_1", "w_out_1", "xattn_norm_1", "xattn_mem_norm_1", "xattn_wq_1", "xattn_wk_1",
        "xattn_wv_1", "xattn_wo_1", "ffn_norm_1", "moe_router_1", "moe_w_gate_1", "moe_w_up_1", "moe_w_down_1",
        "final_norm"]


def kernel(**inputs):
    import numpy as np
    import concourse.bacc as bacc
    from concourse.bass_utils import run_bass_kernel_spmd as run

    nc = bacc.Bacc("TRN2", target_bir_lowering=False, num_devices=1)
    arrays, aps = {}, {}
    for name in _INS:
        arr = np.ascontiguousarray(inputs[name])
        arrays[f"in_{name}"] = arr
        aps[name] = nc.dram_tensor(f"in_{name}", arr.shape, mybir.dt.from_np(arr.dtype), kind="ExternalInput").ap()
    out = nc.dram_tensor("out", (1, 256, D), F32, kind="ExternalOutput").ap()
    build(nc, aps, out)
    return run(nc, [arrays], core_ids=[0]).results[0]["out"]
```
